# Optimizing a Trainium2 kernel written in Bass

```python
import jax
import jax.numpy as jnp
from jax import lax
import jax, jax.numpy as jnp
import numpy as np

D_MODEL = 1024
BATCH = 1
SEQ = 512
DEPTH = 2

HEAD_DIM = 64
Q_BLOCK = 128
ROPE_THETA = 10000.0
NORM_EPS = 1e-6

A_HEADS = 8
A_KV_HEADS = 2
IDX_HEADS = 4
IDX_DIM = 64
DSA_TOPK = 256
B_HEADS = 8
B_KV_HEADS = 2
SWA_WINDOW = 128
C_HEADS = 8
C_KV_HEADS = 2
CMP_STRIDE = 16
CMP_LEN = 2 * CMP_STRIDE
CMP_HIDDEN = 128
SLC_BLOCK = 64
SLC_TOPN = 16
NSA_WINDOW = 512
D_HEADS = 8
Q_LORA = 256
KV_LORA = 128
NOPE_DIM = 64
ROPE_DIM = 32
V_DIM = 64

N_EVEN = (DEPTH + 1) // 2
N_ODD = DEPTH // 2

AB_SPLITS = (A_HEADS * HEAD_DIM, A_KV_HEADS * HEAD_DIM, A_KV_HEADS * HEAD_DIM, IDX_HEADS * IDX_DIM, IDX_DIM, IDX_HEADS, A_HEADS * HEAD_DIM, B_HEADS * HEAD_DIM, B_KV_HEADS * HEAD_DIM, B_KV_HEADS * HEAD_DIM, B_HEADS * HEAD_DIM)
AB_COLS = sum(AB_SPLITS)
AB_WIDTH = (A_HEADS + B_HEADS) * HEAD_DIM
CD_SPLITS = (C_HEADS * HEAD_DIM,) + (C_KV_HEADS * HEAD_DIM,) * 6 + (C_HEADS * 3, C_HEADS * HEAD_DIM, Q_LORA, KV_LORA, ROPE_DIM, D_HEADS * V_DIM)
CD_COLS = sum(CD_SPLITS)
CD_WIDTH = C_HEADS * HEAD_DIM + D_HEADS * V_DIM


def rms_norm(z, g):
    zf = z.astype(jnp.float32)
    y = zf * lax.rsqrt(jnp.mean(zf * zf, axis=-1, keepdims=True) + NORM_EPS)
    return (y * g.astype(jnp.float32)).astype(z.dtype)

def rope_tables(pos, dim):
    inv = jnp.power(jnp.float32(ROPE_THETA), -jnp.arange(0, dim, 2, dtype=jnp.float32) / dim)
    ang = pos.astype(jnp.float32)[:, None] * inv[None, :]
    return jnp.cos(ang), jnp.sin(ang)

def apply_rope(z, cos, sin):
    half = z.shape[-1] // 2
    z1 = z[..., :half].astype(jnp.float32)
    z2 = z[..., half:].astype(jnp.float32)
    c, s = cos[:, None, :], sin[:, None, :]
    return jnp.concatenate([z1 * c - z2 * s, z2 * c + z1 * s], axis=-1).astype(z.dtype)

def masked_softmax(s, mask):
    s = jnp.where(mask, s.astype(jnp.float32), -jnp.inf)
    m = jnp.max(s, axis=-1, keepdims=True)
    m = jnp.where(jnp.isfinite(m), m, 0.0)
    p = jnp.exp(s - m)
    return p / jnp.maximum(jnp.sum(p, axis=-1, keepdims=True), 1e-30)

def split_cols(y, sizes):
    offs, acc = [], 0
    for s in sizes[:-1]:
        acc += s
        offs.append(acc)
    return jnp.split(y, offs, axis=-1)

def dsa_attention(q, k, v, qi, ki, wi, k_sel):
    bsz, seq = q.shape[:2]
    grp = A_HEADS // A_KV_HEADS
    scale = HEAD_DIM ** -0.5
    idx_scale = (IDX_DIM * IDX_HEADS) ** -0.5
    key_pos = jnp.arange(seq)
    gather = jax.vmap(lambda zb, ib: zb[ib])

    def block(i):
        t0 = i * Q_BLOCK
        t = t0 + jnp.arange(Q_BLOCK)
        qb = lax.dynamic_slice_in_dim(q, t0, Q_BLOCK, 1).reshape(bsz, Q_BLOCK, A_KV_HEADS, grp, HEAD_DIM)
        qib = lax.dynamic_slice_in_dim(qi, t0, Q_BLOCK, 1)
        wib = lax.dynamic_slice_in_dim(wi, t0, Q_BLOCK, 1).astype(jnp.float32)
        logits = jnp.einsum('bqhd,bsd->bqhs', qib, ki).astype(jnp.float32)
        score = jnp.einsum('bqh,bqhs->bqs', wib, jax.nn.relu(logits)) * idx_scale
        causal = key_pos[None, :] <= t[:, None]
        score = jnp.where(causal[None], score, -jnp.inf)
        _, idx = lax.top_k(score, k_sel)
        valid = idx <= t[None, :, None]
        ks = gather(k, idx)
        vs = gather(v, idx)
        s = jnp.einsum('bqgrd,bqkgd->bqgrk', qb, ks) * scale
        p = masked_softmax(s, valid[:, :, None, None, :])
        o = jnp.einsum('bqgrk,bqkgd->bqgrd', p.astype(v.dtype), vs)
        return o.reshape(bsz, Q_BLOCK, A_HEADS * HEAD_DIM)

    out = lax.map(block, jnp.arange(seq // Q_BLOCK))
    return out.transpose(1, 0, 2, 3).reshape(bsz, seq, A_HEADS * HEAD_DIM)

def swa_sink_attention(q, k, v, sinks):
    bsz, seq = q.shape[:2]
    nb = seq // Q_BLOCK
    grp = B_HEADS // B_KV_HEADS
    scale = HEAD_DIM ** -0.5
    qb = q.reshape(bsz, nb, Q_BLOCK, B_KV_HEADS, grp, HEAD_DIM)

    def band(z):
        zp = jnp.pad(z, ((0, 0), (Q_BLOCK, 0), (0, 0), (0, 0))).reshape(bsz, nb + 1, Q_BLOCK, B_KV_HEADS, HEAD_DIM)
        return jnp.concatenate([zp[:, :-1], zp[:, 1:]], axis=2)

    kb, vb = band(k), band(v)
    s = jnp.einsum('bnqgrd,bnkgd->bngrqk', qb, kb).astype(jnp.float32) * scale
    qi = jnp.arange(Q_BLOCK)[None, :, None]
    kj = jnp.arange(2 * Q_BLOCK)[None, None, :]
    blk = jnp.arange(nb)[:, None, None]
    diff = qi + Q_BLOCK - kj
    key_abs = (blk - 1) * Q_BLOCK + kj
    mask = (diff >= 0) & (diff < SWA_WINDOW) & (key_abs >= 0)
    s = jnp.where(mask[None, :, None, None], s, -jnp.inf)
    sink = sinks.astype(jnp.float32).reshape(1, 1, B_KV_HEADS, grp, 1, 1)
    m = jnp.maximum(jnp.max(s, axis=-1, keepdims=True), sink)
    p = jnp.exp(s - m)
    p = p / (jnp.sum(p, axis=-1, keepdims=True) + jnp.exp(sink - m))
    o = jnp.einsum('bngrqk,bnkgd->bnqgrd', p.astype(v.dtype), vb)
    return o.reshape(bsz, seq, B_HEADS * HEAD_DIM)

def nsa_compress(z, pe, w1, w2):
    bsz, seq = z.shape[:2]
    ch = z.reshape(bsz, seq // CMP_STRIDE, CMP_STRIDE, C_KV_HEADS, HEAD_DIM)
    blocks = jnp.concatenate([ch[:, :-1], ch[:, 1:]], axis=2) + pe[None, None, :, None, :]
    flat = blocks.transpose(0, 1, 3, 2, 4).reshape(bsz, seq // CMP_STRIDE - 1, C_KV_HEADS, CMP_LEN * HEAD_DIM)
    return jax.nn.silu(flat @ w1) @ w2

def nsa_attention(q, kc, vc, ks, vs, kw, vw, gates, n_sel):
    bsz, seq = q.shape[:2]
    n_cmp = kc.shape[1]
    n_slc = seq // SLC_BLOCK
    grp = C_HEADS // C_KV_HEADS
    scale = HEAD_DIM ** -0.5
    ratio = SLC_BLOCK // CMP_STRIDE
    pad_back = ratio * n_slc + ratio - n_cmp - 1
    cmp_end = jnp.arange(n_cmp) * CMP_STRIDE + (CMP_LEN - 1)
    blk_ids = jnp.arange(n_slc)
    w_overlap = jnp.where(jnp.arange(ratio) == 0, 1.0, 2.0).astype(jnp.float32)
    ks_blk = ks.reshape(bsz, n_slc, SLC_BLOCK, C_KV_HEADS, HEAD_DIM).transpose(0, 3, 1, 2, 4)
    vs_blk = vs.reshape(bsz, n_slc, SLC_BLOCK, C_KV_HEADS, HEAD_DIM).transpose(0, 3, 1, 2, 4)
    kw_pad = jnp.pad(kw, ((0, 0), (NSA_WINDOW, 0), (0, 0), (0, 0)))
    vw_pad = jnp.pad(vw, ((0, 0), (NSA_WINDOW, 0), (0, 0), (0, 0)))
    gather = jax.vmap(jax.vmap(lambda zb, ib: zb[ib]))
    j_w = jnp.arange(Q_BLOCK + NSA_WINDOW)
    diff_w = jnp.arange(Q_BLOCK)[:, None] + NSA_WINDOW - j_w[None, :]

    def block(i):
        t0 = i * Q_BLOCK
        t = t0 + jnp.arange(Q_BLOCK)
        qb = lax.dynamic_slice_in_dim(q, t0, Q_BLOCK, 1).reshape(bsz, Q_BLOCK, C_KV_HEADS, grp, HEAD_DIM)
        gb = lax.dynamic_slice_in_dim(gates, t0, Q_BLOCK, 1).reshape(bsz, Q_BLOCK, C_KV_HEADS, grp, 3)
        s_c = jnp.einsum('bqgrd,bngd->bqgrn', qb, kc) * scale
        mask_c = cmp_end[None, :] <= t[:, None]
        p_c = masked_softmax(s_c, mask_c[None, :, None, None, :])
        o_c = jnp.einsum('bqgrn,bngd->bqgrd', p_c.astype(vc.dtype), vc)
        imp = jnp.pad(jnp.sum(p_c, axis=3), ((0, 0), (0, 0), (0, 0), (1, pad_back)))
        imp_s = jnp.sum(imp[..., :ratio * n_slc].reshape(bsz, Q_BLOCK, C_KV_HEADS, n_slc, ratio) * w_overlap, axis=-1) + imp[..., ratio::ratio]
        cur = t // SLC_BLOCK
        admiss = blk_ids[None, :] <= cur[:, None]
        forced = (blk_ids[None, :] == 0) | (blk_ids[None, :] >= cur[:, None] - 1)
        imp_s = jnp.where((admiss & forced)[None, :, None, :], jnp.inf, imp_s)
        imp_s = jnp.where(admiss[None, :, None, :], imp_s, -jnp.inf)
        _, sel = lax.top_k(imp_s, n_sel)
        sel_t = sel.transpose(0, 2, 1, 3)
        k_sel = gather(ks_blk, sel_t)
        v_sel = gather(vs_blk, sel_t).reshape(bsz, C_KV_HEADS, Q_BLOCK, n_sel * SLC_BLOCK, HEAD_DIM)
        s_s = jnp.einsum('bqgrd,bgqnld->bqgrnl', qb, k_sel) * scale
        s_s = s_s.reshape(bsz, Q_BLOCK, C_KV_HEADS, grp, n_sel * SLC_BLOCK)
        tok = sel[..., None] * SLC_BLOCK + jnp.arange(SLC_BLOCK)
        mask_s = (tok <= t[None, :, None, None, None]).reshape(bsz, Q_BLOCK, C_KV_HEADS, 1, n_sel * SLC_BLOCK)
        p_s = masked_softmax(s_s, mask_s)
        o_s = jnp.einsum('bqgrm,bgqmd->bqgrd', p_s.astype(vs.dtype), v_sel)
        kwb = lax.dynamic_slice_in_dim(kw_pad, t0, Q_BLOCK + NSA_WINDOW, 1)
        vwb = lax.dynamic_slice_in_dim(vw_pad, t0, Q_BLOCK + NSA_WINDOW, 1)
        s_w = jnp.einsum('bqgrd,bkgd->bqgrk', qb, kwb) * scale
        mask_w = (diff_w >= 0) & (diff_w < NSA_WINDOW) & ((t0 - NSA_WINDOW + j_w)[None, :] >= 0)
        p_w = masked_softmax(s_w, mask_w[None, :, None, None, :])
        o_w = jnp.einsum('bqgrk,bkgd->bqgrd', p_w.astype(vw.dtype), vwb)
        o = gb[..., 0:1] * o_c + gb[..., 1:2] * o_s + gb[..., 2:3] * o_w
        return o.reshape(bsz, Q_BLOCK, C_HEADS * HEAD_DIM)

    out = lax.map(block, jnp.arange(seq // Q_BLOCK))
    return out.transpose(1, 0, 2, 3).reshape(bsz, seq, C_HEADS * HEAD_DIM)

def mla_attention(q_nope, q_rope, k_nope, k_rope, v):
    bsz, seq = q_nope.shape[:2]
    scale = (NOPE_DIM + ROPE_DIM) ** -0.5
    key_pos = jnp.arange(seq)

    def block(i):
        t0 = i * Q_BLOCK
        t = t0 + jnp.arange(Q_BLOCK)
        qn = lax.dynamic_slice_in_dim(q_nope, t0, Q_BLOCK, 1)
        qr = lax.dynamic_slice_in_dim(q_rope, t0, Q_BLOCK, 1)
        s = (jnp.einsum('bqhd,bshd->bhqs', qn, k_nope) + jnp.einsum('bqhd,bsd->bhqs', qr, k_rope)) * scale
        mask = key_pos[None, :] <= t[:, None]
        p = masked_softmax(s, mask[None, None])
        o = jnp.einsum('bhqs,bshd->bqhd', p.astype(v.dtype), v)
        return o.reshape(bsz, Q_BLOCK, D_HEADS * V_DIM)

    out = lax.map(block, jnp.arange(seq // Q_BLOCK))
    return out.transpose(1, 0, 2, 3).reshape(bsz, seq, D_HEADS * V_DIM)

def layer_ab(x, norm_g, w_in, a_qk_norm, a_kidx_norm, b_qk_norm, b_sinks, w_out):
    bsz, seq, _ = x.shape
    y = rms_norm(x, norm_g) @ w_in
    qa, ka, va, qi, ki, wi, za, qb, kb, vb, zb = split_cols(y, AB_SPLITS)
    pos = jnp.arange(seq)
    cos, sin = rope_tables(pos, HEAD_DIM)
    icos, isin = rope_tables(pos, IDX_DIM)

    def heads(z, n):
        return z.reshape(bsz, seq, n, HEAD_DIM)

    qa = apply_rope(rms_norm(heads(qa, A_HEADS), a_qk_norm[0]), cos, sin)
    ka = apply_rope(rms_norm(heads(ka, A_KV_HEADS), a_qk_norm[1]), cos, sin)
    qi = apply_rope(qi.reshape(bsz, seq, IDX_HEADS, IDX_DIM), icos, isin)
    ki = apply_rope(rms_norm(ki, a_kidx_norm)[:, :, None, :], icos, isin)[:, :, 0]
    k_sel = min(DSA_TOPK, seq // 4)
    oa = dsa_attention(qa, ka, heads(va, A_KV_HEADS), qi, ki, wi, k_sel)
    qb = apply_rope(rms_norm(heads(qb, B_HEADS), b_qk_norm[0]), cos, sin)
    kb = apply_rope(rms_norm(heads(kb, B_KV_HEADS), b_qk_norm[1]), cos, sin)
    ob = swa_sink_attention(qb, kb, heads(vb, B_KV_HEADS), b_sinks)
    mix = jnp.concatenate([oa * jax.nn.silu(za), ob * jax.nn.silu(zb)], axis=-1)
    return x + mix @ w_out

def layer_cd(x, norm_g, w_in, c_q_norm, c_k_norm, c_cmp_pe, c_cmp_w1, c_cmp_w2, d_q_lat_norm, d_kv_lat_norm, d_w_uq, d_w_ukv, d_nope_norm, d_rope_norm, w_out):
    bsz, seq, _ = x.shape
    y = rms_norm(x, norm_g) @ w_in
    qc, kc, vc, ks, vs, kw, vw, gc, zc, cq, ckv, kr, zd = split_cols(y, CD_SPLITS)
    pos = jnp.arange(seq)
    cos, sin = rope_tables(pos, HEAD_DIM)

    def heads(z, n):
        return z.reshape(bsz, seq, n, HEAD_DIM)

    qc = apply_rope(rms_norm(heads(qc, C_HEADS), c_q_norm), cos, sin)
    kc = nsa_compress(heads(kc, C_KV_HEADS), c_cmp_pe[0], c_cmp_w1[0], c_cmp_w2[0])
    vc = nsa_compress(heads(vc, C_KV_HEADS), c_cmp_pe[1], c_cmp_w1[1], c_cmp_w2[1])
    n_cmp = kc.shape[1]
    ccos, csin = rope_tables(jnp.arange(n_cmp) * CMP_STRIDE + (CMP_LEN - 1), HEAD_DIM)
    kc = apply_rope(rms_norm(kc, c_k_norm[0]), ccos, csin)
    ks = apply_rope(rms_norm(heads(ks, C_KV_HEADS), c_k_norm[1]), cos, sin)
    kw = apply_rope(rms_norm(heads(kw, C_KV_HEADS), c_k_norm[2]), cos, sin)
    gates = jax.nn.sigmoid(gc.reshape(bsz, seq, C_HEADS, 3))
    n_sel = min(SLC_TOPN, seq // SLC_BLOCK)
    oc = nsa_attention(qc, kc, vc, ks, heads(vs, C_KV_HEADS), kw, heads(vw, C_KV_HEADS), gates, n_sel)
    q = (rms_norm(cq, d_q_lat_norm) @ d_w_uq).reshape(bsz, seq, D_HEADS, NOPE_DIM + ROPE_DIM)
    kv = (rms_norm(ckv, d_kv_lat_norm) @ d_w_ukv).reshape(bsz, seq, D_HEADS, NOPE_DIM + V_DIM)
    rcos, rsin = rope_tables(pos, ROPE_DIM)
    q_nope = rms_norm(q[..., :NOPE_DIM], d_nope_norm[0])
    q_rope = apply_rope(rms_norm(q[..., NOPE_DIM:], d_rope_norm[0]), rcos, rsin)
    k_nope = rms_norm(kv[..., :NOPE_DIM], d_nope_norm[1])
    k_rope = apply_rope(rms_norm(kr[:, :, None, :], d_rope_norm[1]), rcos, rsin)[:, :, 0]
    od = mla_attention(q_nope, q_rope, k_nope, k_rope, kv[..., NOPE_DIM:])
    mix = jnp.concatenate([oc * jax.nn.silu(zc), od * jax.nn.silu(zd)], axis=-1)
    return x + mix @ w_out

def first_inputs(seed: int = 0) -> dict:
    key = jax.random.key(seed)
    k = jax.random.split(key, 22)
    f32 = jnp.float32

    def w(kk, shape, fan_in):
        return jax.random.normal(kk, shape, f32) * (fan_in ** -0.5)

    def gain(kk, shape):
        return 1.0 + 0.05 * jax.random.normal(kk, shape, f32)

    return {
        'x': jax.random.normal(k[0], (BATCH, SEQ, D_MODEL), f32),
        'ab_norm': gain(k[1], (N_EVEN, D_MODEL)),
        'ab_w_in': w(k[2], (N_EVEN, D_MODEL, AB_COLS), D_MODEL),
        'a_qk_norm': gain(k[3], (N_EVEN, 2, HEAD_DIM)),
        'a_kidx_norm': gain(k[4], (N_EVEN, IDX_DIM)),
        'b_qk_norm': gain(k[5], (N_EVEN, 2, HEAD_DIM)),
        'b_sinks': 0.5 * jax.random.normal(k[6], (N_EVEN, B_HEADS), f32),
        'ab_w_out': w(k[7], (N_EVEN, AB_WIDTH, D_MODEL), AB_WIDTH),
        'cd_norm': gain(k[8], (N_ODD, D_MODEL)),
        'cd_w_in': w(k[9], (N_ODD, D_MODEL, CD_COLS), D_MODEL),
        'c_q_norm': gain(k[10], (N_ODD, HEAD_DIM)),
        'c_k_norm': gain(k[11], (N_ODD, 3, HEAD_DIM)),
        'c_cmp_pe': 0.1 * jax.random.normal(k[12], (N_ODD, 2, CMP_LEN, HEAD_DIM), f32),
        'c_cmp_w1': w(k[13], (N_ODD, 2, CMP_LEN * HEAD_DIM, CMP_HIDDEN), CMP_LEN * HEAD_DIM),
        'c_cmp_w2': w(k[14], (N_ODD, 2, CMP_HIDDEN, HEAD_DIM), CMP_HIDDEN),
        'd_q_lat_norm': gain(k[15], (N_ODD, Q_LORA)),
        'd_kv_lat_norm': gain(k[16], (N_ODD, KV_LORA)),
        'd_w_uq': w(k[17], (N_ODD, Q_LORA, D_HEADS * (NOPE_DIM + ROPE_DIM)), Q_LORA),
        'd_w_ukv': w(k[18], (N_ODD, KV_LORA, D_HEADS * (NOPE_DIM + V_DIM)), KV_LORA),
        'd_nope_norm': gain(k[19], (N_ODD, 2, NOPE_DIM)),
        'd_rope_norm': gain(k[20], (N_ODD, 2, ROPE_DIM)),
        'cd_w_out': w(k[21], (N_ODD, CD_WIDTH, D_MODEL), CD_WIDTH),
    }

def first_block(x, ab_norm, ab_w_in, a_qk_norm, a_kidx_norm, b_qk_norm, b_sinks, ab_w_out, cd_norm, cd_w_in, c_q_norm, c_k_norm, c_cmp_pe, c_cmp_w1, c_cmp_w2, d_q_lat_norm, d_kv_lat_norm, d_w_uq, d_w_ukv, d_nope_norm, d_rope_norm, cd_w_out):
    for layer in range(DEPTH):
        j = layer // 2
        if layer % 2 == 0:
            x = layer_ab(x, ab_norm[j], ab_w_in[j], a_qk_norm[j], a_kidx_norm[j], b_qk_norm[j], b_sinks[j], ab_w_out[j])
        else:
            x = layer_cd(x, cd_norm[j], cd_w_in[j], c_q_norm[j], c_k_norm[j], c_cmp_pe[j], c_cmp_w1[j], c_cmp_w2[j], d_q_lat_norm[j], d_kv_lat_norm[j], d_w_uq[j], d_w_ukv[j], d_nope_norm[j], d_rope_norm[j], cd_w_out[j])
    return x


DEPTH_2 = 4

GRID_W = 64
CTX_LEN = 256
N_MIXERS = 4
AT_HEADS = 16
AT_KV_HEADS = 4
AT_GROUP = AT_HEADS // AT_KV_HEADS
AT_WIDTH = AT_HEADS * HEAD_DIM
AT_KV_WIDTH = AT_KV_HEADS * HEAD_DIM
NA_HEADS = 16
NA_WIDTH = NA_HEADS * HEAD_DIM
NA_WIN_ROWS = 8
NA_WIN_COLS = 16
CONV_WIDTH = 31
FT_GROUPS = 4
FT_GROUP_WIDTH = D_MODEL // FT_GROUPS
D_FF = 4 * D_MODEL
N_MOD = 6
EPS = 1e-6
N_AT_LAYERS = (DEPTH_2 + 3) // 4
N_NA_LAYERS = (DEPTH_2 + 2) // 4
N_CV_LAYERS = (DEPTH_2 + 1) // 4
N_FT_LAYERS = DEPTH_2 // 4


def rms_norm_2(x, g):
    xf = x.astype(jnp.float32)
    y = xf * lax.rsqrt(jnp.mean(xf * xf, axis=-1, keepdims=True) + EPS)
    return (y * g.astype(jnp.float32)).astype(x.dtype)

def layer_norm(x, g, b):
    xf = x.astype(jnp.float32)
    mu = jnp.mean(xf, axis=-1, keepdims=True)
    var = jnp.mean(jnp.square(xf - mu), axis=-1, keepdims=True)
    y = (xf - mu) * lax.rsqrt(var + EPS)
    return (y * g.astype(jnp.float32) + b.astype(jnp.float32)).astype(x.dtype)

def ada_mods(vec, w, b):
    m = jax.nn.silu(vec) @ w + b
    return [mi[..., None, :] for mi in jnp.split(m, N_MOD, axis=-1)]

def modulate(h, shift, scale):
    return h * (1.0 + scale) + shift

def rope_angles(n_tok):
    t = jnp.arange(n_tok)
    row = (t // GRID_W).astype(jnp.float32)
    col = (t % GRID_W).astype(jnp.float32)
    n_axis = HEAD_DIM // 4
    inv = ROPE_THETA ** (-jnp.arange(n_axis, dtype=jnp.float32) / n_axis)
    return jnp.concatenate([row[:, None] * inv, col[:, None] * inv], axis=-1)

def apply_rope_2(x, ang):
    xf = x.astype(jnp.float32).reshape(x.shape[:-1] + (HEAD_DIM // 2, 2))
    cos = jnp.cos(ang)[None, :, None, :]
    sin = jnp.sin(ang)[None, :, None, :]
    x1, x2 = xf[..., 0], xf[..., 1]
    out = jnp.stack([x1 * cos - x2 * sin, x1 * sin + x2 * cos], axis=-1)
    return out.reshape(x.shape).astype(x.dtype)

def gqa_attend(q, k, v):
    s = jnp.einsum('bqkgd,bnkd->bkgqn', q, k, preferred_element_type=jnp.float32)
    p = jax.nn.softmax(s, axis=-1).astype(v.dtype)
    return jnp.einsum('bkgqn,bnkd->bqkgd', p, v)

def gqa_mixer(hl, hc, ang, w_qkv, q_g, k_g, w_o, ctx_out):
    B, S, _ = hl.shape
    C = hc.shape[1]
    scale = HEAD_DIM ** -0.5
    ql, kl, vl = jnp.split(hl @ w_qkv, [AT_WIDTH, AT_WIDTH + AT_KV_WIDTH], axis=-1)
    ql = apply_rope_2(rms_norm_2(ql.reshape(B, S, AT_HEADS, HEAD_DIM), q_g), ang) * scale
    kl = apply_rope_2(rms_norm_2(kl.reshape(B, S, AT_KV_HEADS, HEAD_DIM), k_g), ang)
    vl = vl.reshape(B, S, AT_KV_HEADS, HEAD_DIM)
    kc, vc = jnp.split(hc @ w_qkv[:, AT_WIDTH:], 2, axis=-1)
    kc = rms_norm_2(kc.reshape(B, C, AT_KV_HEADS, HEAD_DIM), k_g)
    vc = vc.reshape(B, C, AT_KV_HEADS, HEAD_DIM)
    k_all = jnp.concatenate([kc, kl], axis=1)
    v_all = jnp.concatenate([vc, vl], axis=1)
    nb = S // Q_BLOCK
    qb = ql.reshape(B, nb, Q_BLOCK, AT_KV_HEADS, AT_GROUP, HEAD_DIM).transpose(1, 0, 2, 3, 4, 5)
    ob = lax.map(lambda q: gqa_attend(q, k_all, v_all), qb)
    yl = ob.transpose(1, 0, 2, 3, 4, 5).reshape(B, S, AT_WIDTH) @ w_o
    yc = None
    if ctx_out:
        qc = rms_norm_2((hc @ w_qkv[:, :AT_WIDTH]).reshape(B, C, AT_HEADS, HEAD_DIM), q_g) * scale
        oc = gqa_attend(qc.reshape(B, C, AT_KV_HEADS, AT_GROUP, HEAD_DIM), kc, vc)
        yc = oc.reshape(B, C, AT_WIDTH) @ w_o
    return yc, yl

def na_mixer(hl, hc, n_rows, w_qkv, rpb, w_o, ctx_out):
    B, S, _ = hl.shape
    C = hc.shape[1]
    scale = HEAD_DIM ** -0.5
    ql, kl, vl = jnp.split(hl @ w_qkv, 3, axis=-1)
    kc, vc = jnp.split(hc @ w_qkv[:, NA_WIDTH:], 2, axis=-1)
    kc = kc.reshape(B, C, NA_HEADS, HEAD_DIM)
    vc = vc.reshape(B, C, NA_HEADS, HEAD_DIM)
    wh = min(NA_WIN_ROWS, n_rows)
    ww = NA_WIN_COLS
    row_start = jnp.clip(jnp.arange(n_rows) - wh // 2, 0, n_rows - wh)
    cols = jnp.arange(GRID_W)
    col_idx = jnp.clip(cols - ww // 2, 0, GRID_W - ww)[:, None] + jnp.arange(ww)
    col_bias_idx = col_idx - cols[:, None] + (NA_WIN_COLS - 1)
    rpb_cols = rpb[:, :, col_bias_idx]
    qg = (ql * scale).reshape(B, n_rows, GRID_W, NA_HEADS, HEAD_DIM).transpose(1, 0, 2, 3, 4)
    kg = kl.reshape(B, n_rows, GRID_W, NA_HEADS, HEAD_DIM)
    vg = vl.reshape(B, n_rows, GRID_W, NA_HEADS, HEAD_DIM)

    def row_fn(args):
        r, q = args
        rs = row_start[r]
        k_nb = lax.dynamic_slice_in_dim(kg, rs, wh, axis=1)[:, :, col_idx]
        v_nb = lax.dynamic_slice_in_dim(vg, rs, wh, axis=1)[:, :, col_idx]
        s_nb = jnp.einsum('bqhd,biqjhd->bhqij', q, k_nb, preferred_element_type=jnp.float32)
        row_bias_idx = rs + jnp.arange(wh) - r + (NA_WIN_ROWS - 1)
        bias = rpb_cols[:, row_bias_idx].transpose(0, 2, 1, 3).astype(jnp.float32)
        s_nb = s_nb + bias[None]
        s_ctx = jnp.einsum('bqhd,bnhd->bhqn', q, kc, preferred_element_type=jnp.float32)
        s = jnp.concatenate([s_nb.reshape(B, NA_HEADS, GRID_W, wh * ww), s_ctx], axis=-1)
        p = jax.nn.softmax(s, axis=-1).astype(vg.dtype)
        p_nb = p[..., :wh * ww].reshape(B, NA_HEADS, GRID_W, wh, ww)
        p_ctx = p[..., wh * ww:]
        return (jnp.einsum('bhqij,biqjhd->bqhd', p_nb, v_nb)
                + jnp.einsum('bhqn,bnhd->bqhd', p_ctx, vc))

    o = lax.map(row_fn, (jnp.arange(n_rows), qg))
    yl = o.transpose(1, 0, 2, 3, 4).reshape(B, S, NA_WIDTH) @ w_o
    yc = None
    if ctx_out:
        qc = (hc @ w_qkv[:, :NA_WIDTH]).reshape(B, C, NA_HEADS, 1, HEAD_DIM) * scale
        yc = gqa_attend(qc, kc, vc).reshape(B, C, NA_WIDTH) @ w_o
    return yc, yl

def conv_module(h, w_pw1, b_pw1, w_dw, b_dw, ln_g, ln_b, w_pw2, b_pw2):
    a, g = jnp.split(h @ w_pw1 + b_pw1, 2, axis=-1)
    u = a * jax.nn.sigmoid(g)
    pad = CONV_WIDTH // 2
    u = lax.conv_general_dilated(u, w_dw[:, None, :], window_strides=(1,), padding=[(pad, pad)],
                                 dimension_numbers=('NWC', 'WIO', 'NWC'),
                                 feature_group_count=u.shape[-1]) + b_dw
    u = jax.nn.silu(layer_norm(u, ln_g, ln_b))
    return u @ w_pw2 + b_pw2

def fourier_mixer(h, w, b):
    B, n, D = h.shape
    hf = h.astype(jnp.float32).reshape(B, n, FT_GROUPS, FT_GROUP_WIDTH)
    z = jnp.fft.fft2(hf, axes=(1, 3), norm='ortho').real.astype(h.dtype).reshape(B, n, D)
    return z @ w + b

def sq_relu_mlp(h, w1, w2):
    return jnp.square(jax.nn.relu(h @ w1)) @ w2

def second_inputs(seed: int = 0) -> dict:
    key = jax.random.key(seed)
    ks = jax.random.split(key, 32)
    f32 = jnp.float32
    D = D_MODEL

    def nrm(k, shape, s):
        return jax.random.normal(k, shape, f32) * s

    def gain(k, shape):
        return 1.0 + 0.02 * jax.random.normal(k, shape, f32)

    return {
        'x': nrm(ks[0], (BATCH, SEQ, D), 1.0),
        'c': nrm(ks[1], (BATCH, D), 1.0),
        'ctx': nrm(ks[2], (BATCH, CTX_LEN, D), 1.0),
        'c_ctx': nrm(ks[3], (D,), 1.0),
        'ada_w': nrm(ks[4], (DEPTH_2, D, N_MOD * D), 0.5 * D ** -0.5),
        'ada_b': nrm(ks[5], (DEPTH_2, N_MOD * D), 0.02),
        'norm1_g': gain(ks[6], (DEPTH_2, D)),
        'norm2_g': gain(ks[7], (DEPTH_2, D)),
        'mlp_w1': nrm(ks[8], (DEPTH_2, D, D_FF), D ** -0.5),
        'mlp_w2': nrm(ks[9], (DEPTH_2, D_FF, D), D_FF ** -0.5),
        'final_g': gain(ks[10], (D,)),
        'at_w_qkv': nrm(ks[11], (N_AT_LAYERS, D, AT_WIDTH + 2 * AT_KV_WIDTH), D ** -0.5),
        'at_q_g': gain(ks[12], (N_AT_LAYERS, HEAD_DIM)),
        'at_k_g': gain(ks[13], (N_AT_LAYERS, HEAD_DIM)),
        'at_w_o': nrm(ks[14], (N_AT_LAYERS, AT_WIDTH, D), AT_WIDTH ** -0.5),
        'na_w_qkv': nrm(ks[15], (N_NA_LAYERS, D, 3 * NA_WIDTH), D ** -0.5),
        'na_rpb': nrm(ks[16], (N_NA_LAYERS, NA_HEADS, 2 * NA_WIN_ROWS - 1, 2 * NA_WIN_COLS - 1), 0.1),
        'na_w_o': nrm(ks[17], (N_NA_LAYERS, NA_WIDTH, D), NA_WIDTH ** -0.5),
        'cv_w_pw1': nrm(ks[18], (N_CV_LAYERS, D, 2 * D), D ** -0.5),
        'cv_b_pw1': nrm(ks[19], (N_CV_LAYERS, 2 * D), 0.02),
        'cv_w_dw': nrm(ks[20], (N_CV_LAYERS, CONV_WIDTH, D), CONV_WIDTH ** -0.5),
        'cv_b_dw': nrm(ks[21], (N_CV_LAYERS, D), 0.02),
        'cv_ln_g': gain(ks[22], (N_CV_LAYERS, D)),
        'cv_ln_b': nrm(ks[23], (N_CV_LAYERS, D), 0.02),
        'cv_w_pw2': nrm(ks[24], (N_CV_LAYERS, D, D), D ** -0.5),
        'cv_b_pw2': nrm(ks[25], (N_CV_LAYERS, D), 0.02),
        'ft_w': nrm(ks[26], (N_FT_LAYERS, D, D), D ** -0.5),
        'ft_b': nrm(ks[27], (N_FT_LAYERS, D), 0.02),
    }

def second_block(x, c, ctx, c_ctx, ada_w, ada_b, norm1_g, norm2_g, mlp_w1, mlp_w2, final_g,
              at_w_qkv, at_q_g, at_k_g, at_w_o, na_w_qkv, na_rpb, na_w_o,
              cv_w_pw1, cv_b_pw1, cv_w_dw, cv_b_dw, cv_ln_g, cv_ln_b, cv_w_pw2, cv_b_pw2,
              ft_w, ft_b):
    n_lat = x.shape[1]
    n_rows = n_lat // GRID_W
    ang = rope_angles(n_lat)
    h_ctx = ctx
    for i in range(DEPTH_2):
        kind = i % N_MIXERS
        occ = i // N_MIXERS
        ctx_later = any((j % N_MIXERS) in (0, 1) for j in range(i + 1, DEPTH_2))
        ctx_read = kind in (0, 1)
        ml = ada_mods(c, ada_w[i], ada_b[i])
        hl = modulate(rms_norm_2(x, norm1_g[i]), ml[0], ml[1])
        hc = None
        mc = None
        if ctx_read or ctx_later:
            mc = ada_mods(c_ctx, ada_w[i], ada_b[i])
            hc = modulate(rms_norm_2(h_ctx, norm1_g[i]), mc[0], mc[1])
        if kind == 0:
            yc, yl = gqa_mixer(hl, hc, ang, at_w_qkv[occ], at_q_g[occ], at_k_g[occ], at_w_o[occ], ctx_later)
        elif kind == 1:
            yc, yl = na_mixer(hl, hc, n_rows, na_w_qkv[occ], na_rpb[occ], na_w_o[occ], ctx_later)
        elif kind == 2:
            cv = (cv_w_pw1[occ], cv_b_pw1[occ], cv_w_dw[occ], cv_b_dw[occ], cv_ln_g[occ], cv_ln_b[occ],
                  cv_w_pw2[occ], cv_b_pw2[occ])
            yl = conv_module(hl, *cv)
            yc = conv_module(hc, *cv) if ctx_later else None
        else:
            yl = fourier_mixer(hl, ft_w[occ], ft_b[occ])
            yc = fourier_mixer(hc, ft_w[occ], ft_b[occ]) if ctx_later else None
        x = x + ml[2] * yl
        x = x + ml[5] * sq_relu_mlp(modulate(rms_norm_2(x, norm2_g[i]), ml[3], ml[4]), mlp_w1[i], mlp_w2[i])
        if ctx_later:
            h_ctx = h_ctx + mc[2] * yc
            h_ctx = h_ctx + mc[5] * sq_relu_mlp(modulate(rms_norm_2(h_ctx, norm2_g[i]), mc[3], mc[4]),
                                                mlp_w1[i], mlp_w2[i])
    return rms_norm_2(x, final_g)


_first_inputs = second_inputs


def second_inputs(seed=0):
    import zlib

    import numpy as np

    out = dict(_first_inputs(seed))
    spreads = {}
    factors = {'norm1_g': 8.0,
     'norm2_g': 3.32,
     'final_g': 8.685,
     'at_q_g': 8.0,
     'at_k_g': 8.0,
     'na_rpb': 8.0,
     'cv_b_pw1': 64.0,
     'cv_b_dw': 63.813,
     'cv_ln_g': 64.0,
     'cv_ln_b': 64.0,
     'cv_b_pw2': 63.909,
     'ft_b': 64.0}
    for name, (base, spread) in spreads.items():
        noise = np.random.default_rng([zlib.crc32(name.encode()), seed]).standard_normal(out[name].shape)
        drawn = base * np.exp(spread * noise) if base else spread * noise
        out[name] = __import__('jax').numpy.asarray(drawn.astype(out[name].dtype))
    for name, factor in factors.items():
        out[name] = (out[name] * factor).astype(out[name].dtype)
    return out


_narrow_inputs = second_inputs


def second_inputs(seed=0):

    out = dict(_narrow_inputs(seed))
    wider = {'final_g': 3.28, 'cv_ln_g': 3.4, 'cv_ln_b': 3.65, 'ft_b': 3.08}
    for name, times in wider.items():
        mean = out[name].mean()
        out[name] = (mean + times * (out[name] - mean)).astype(out[name].dtype)
    return out


def setup_inputs(seed=0):
    out = dict(first_inputs(seed))
    for name, value in second_inputs(seed + 1).items():
        if name != "x":
            out[name + "_2"] = value
    return out


def reference(
    x, ab_norm, ab_w_in, a_qk_norm, a_kidx_norm, b_qk_norm, b_sinks, ab_w_out, cd_norm, cd_w_in,
    c_q_norm, c_k_norm, c_cmp_pe, c_cmp_w1, c_cmp_w2, d_q_lat_norm, d_kv_lat_norm, d_w_uq,
    d_w_ukv, d_nope_norm, d_rope_norm, cd_w_out, c_2, ctx_2, c_ctx_2, ada_w_2, ada_b_2,
    norm1_g_2, norm2_g_2, mlp_w1_2, mlp_w2_2, final_g_2, at_w_qkv_2, at_q_g_2, at_k_g_2,
    at_w_o_2, na_w_qkv_2, na_rpb_2, na_w_o_2, cv_w_pw1_2, cv_b_pw1_2, cv_w_dw_2, cv_b_dw_2,
    cv_ln_g_2, cv_ln_b_2, cv_w_pw2_2, cv_b_pw2_2, ft_w_2, ft_b_2,
):
    x = first_block(
        x, ab_norm, ab_w_in, a_qk_norm, a_kidx_norm, b_qk_norm, b_sinks, ab_w_out, cd_norm,
        cd_w_in, c_q_norm, c_k_norm, c_cmp_pe, c_cmp_w1, c_cmp_w2, d_q_lat_norm, d_kv_lat_norm,
        d_w_uq, d_w_ukv, d_nope_norm, d_rope_norm, cd_w_out,
    )
    return second_block(
        x, c_2, ctx_2, c_ctx_2, ada_w_2, ada_b_2, norm1_g_2, norm2_g_2, mlp_w1_2, mlp_w2_2,
        final_g_2, at_w_qkv_2, at_q_g_2, at_k_g_2, at_w_o_2, na_w_qkv_2, na_rpb_2, na_w_o_2,
        cv_w_pw1_2, cv_b_pw1_2, cv_w_dw_2, cv_b_dw_2, cv_ln_g_2, cv_ln_b_2, cv_w_pw2_2,
        cv_b_pw2_2, ft_w_2, ft_b_2,
    )


_drawn_inputs = setup_inputs


def setup_inputs(seed=0):
    import zlib

    import numpy as np

    out = dict(_drawn_inputs(seed))
    spreads = {}
    factors = {}
    for name, (base, spread) in spreads.items():
        noise = np.random.default_rng([zlib.crc32(name.encode()), seed]).standard_normal(out[name].shape)
        drawn = base * np.exp(spread * noise) if base else spread * noise
        out[name] = jnp.asarray(drawn.astype(out[name].dtype))
    for name, factor in factors.items():
        out[name] = (out[name] * factor).astype(out[name].dtype)
    return out
```

```python
from contextlib import ExitStack

import numpy as np

import concourse.bass as bass
from concourse import mybir

F32 = mybir.dt.float32
BF16 = mybir.dt.bfloat16
ALU = mybir.AluOpType
ACT = mybir.ActivationFunctionType
AX = mybir.AxisListType.X

P = 128
D = 1024
KD = D // P
S = 512
C = 256
ST = S // P
HD = 64
FF = 4 * D
EPS = 1e-6
NEG = -1e30
RING = 3
SLOT = 4096
BANK = 512
PROJ_BANKS = 6
TOPK = S // 4
CMP_STRIDE, CMP_LEN, CMP_HID = 16, 32, 128
NCMP = S // CMP_STRIDE - 1
GRID = 64
ROWS = S // GRID
WIN = 16
TAPS = 31
GW = 256
PAIR_TILES, PAIR_ROWS = 11, 22
MLA_TILES, MLA_ROWS = 8, 16
MLA_W = 96


def rope_cos_sin(pos, dim):
    inv = np.power(np.float32(10000.0), -np.arange(0, dim, 2, dtype=np.float32) / np.float32(dim))
    ang = (pos.astype(np.float32)[:, None] * inv[None, :]).astype(np.float32)
    return np.cos(ang).T, np.sin(ang).T


def half_tables(pos, dim):
    c, s = rope_cos_sin(pos, dim)
    return np.concatenate([c, c]), np.concatenate([-s, s])


def swap_matrix(dim, half):
    m = np.zeros((dim, dim), np.float32)
    for f in range(dim):
        m[(f + half) % dim, f] = 1.0
    return m


def block_diag(*ms):
    n = sum(m.shape[0] for m in ms)
    out, at = np.zeros((n, n), np.float32), 0
    for m in ms:
        out[at:at + len(m), at:at + len(m)] = m
        at += len(m)
    return out


def pad_rows(a):
    out = np.zeros((P,) + a.shape[1:], np.float32)
    out[:len(a)] = a
    return out


def head_norm_constants(tiles, rows, segments):
    mean = np.zeros((P, tiles, rows), np.float32)
    spread = np.zeros((P, tiles, P), np.float32)
    for i in range(tiles):
        for j, (a, b) in enumerate(segments):
            mean[a:b, i, 2 * i + j] = 1.0 / (b - a)
            spread[2 * i + j, i, a:b] = 1.0
    return np.concatenate([mean.reshape(P, -1), spread.reshape(P, -1)], 1)


def constants():
    pos = np.arange(S)
    out = {}
    k, q = np.arange(P)[None, :], np.arange(P)[:, None]
    out["ident"] = np.eye(P, dtype=np.float32)
    out["diag_mask"] = np.where(k <= q, 0.0, NEG)
    out["prev_mask"] = np.where(k > q, 0.0, NEG)
    t = np.arange(S)[:, None]
    cmp_end = np.arange(NCMP)[None, :] * CMP_STRIDE + CMP_LEN - 1
    out["cmp_mask"] = np.where(cmp_end <= t, 0.0, NEG).reshape(ST, P, NCMP).transpose(1, 0, 2)
    c, s = half_tables(pos, HD)
    out["rope_ab"] = np.concatenate([np.concatenate([c, c]), np.concatenate([s, s]),
                                     block_diag(swap_matrix(64, 32), swap_matrix(64, 32))], 1)
    cc, cs = half_tables(np.arange(NCMP) * CMP_STRIDE + CMP_LEN - 1, HD)
    out["rope_cmp"] = np.concatenate([np.concatenate([cc, cc]), np.concatenate([cs, cs])], 1)
    rc, rs = half_tables(pos, 32)
    out["rope_mla"] = np.concatenate([
        pad_rows(np.concatenate([np.ones((64, S)), rc])), pad_rows(np.concatenate([np.zeros((64, S)), rs])),
        block_diag(np.zeros((64, 64)), swap_matrix(32, 16), np.zeros((32, 32)))], 1)
    row, col = (pos // GRID).astype(np.float32), (pos % GRID).astype(np.float32)
    inv = np.power(np.float32(10000.0), -np.arange(16, dtype=np.float32) / np.float32(16))
    ang = np.concatenate([row[:, None] * inv, col[:, None] * inv], -1).astype(np.float32).T
    ca, sa = np.repeat(np.cos(ang), 2, 0), np.repeat(np.sin(ang), 2, 0)
    sa[0::2] *= -1.0
    pairs = np.zeros((P, P), np.float32)
    for f in range(P):
        pairs[f ^ 1, f] = 1.0
    out["rope_at"] = np.concatenate([np.concatenate([ca, ca]), np.concatenate([sa, sa]), pairs], 1)
    out["hn_pair"] = head_norm_constants(PAIR_TILES, PAIR_ROWS, [(0, 64), (64, 128)])
    out["hn_mla"] = head_norm_constants(MLA_TILES, MLA_ROWS, [(0, 64), (64, 96)])
    cq, jk = np.arange(GRID)[:, None], np.arange(GRID)[None, :]
    start = np.clip(cq - WIN // 2, 0, GRID - WIN)
    inside = (jk >= start) & (jk < start + WIN)
    sel = np.zeros((32, GRID, GRID), np.float32)
    for u in range(2 * WIN - 1):
        sel[u] = inside & (jk - cq + WIN - 1 == u)
    sel[31] = np.where(inside, 0.0, NEG)
    out["na_select"] = sel.reshape(32, GRID * GRID)
    dd = np.outer(np.arange(GW), np.arange(GW)) % GW
    ss = np.outer(np.arange(S), np.arange(S)) % S
    scale = 1.0 / np.sqrt(np.float64(GW * S))
    out["dft_group"] = np.concatenate([np.cos(2 * np.pi * dd / GW) * scale, np.sin(2 * np.pi * dd / GW) * scale], 1)
    out["dft_seq"] = np.concatenate([np.cos(2 * np.pi * ss / S), -np.sin(2 * np.pi * ss / S)], 1)
    return {n: np.ascontiguousarray(a, dtype=np.float32) for n, a in out.items()}


VECTORS = [("ab_norm", KD), ("cd_norm", KD), ("qa_g", 1), ("ka_g", 1), ("ki_g", 1), ("qb_g", 1), ("kb_g", 1),
           ("qc_g", 1), ("kc_g", 1), ("ks_g", 1), ("kw_g", 1), ("pe_k", CMP_LEN), ("pe_v", CMP_LEN),
           ("qlat_g", 2), ("kvlat_g", 1), ("qd_g", 1), ("kd_g", 1), ("c", KD), ("c_ctx", KD), ("final_g", KD),
           ("at_q_g", 1), ("at_k_g", 1), ("cv_b1", 2 * KD), ("cv_w", KD * TAPS), ("cv_bd", KD), ("cv_lng", KD),
           ("cv_lnb", KD), ("cv_b2", KD), ("ft_b", KD)]
for _i in range(4):
    VECTORS += [(f"norm1_{_i}", KD), (f"norm2_{_i}", KD), (f"ada_b{_i}", 6 * KD)]
VCOL = {}
NVEC = 0
for _n, _w in VECTORS:
    VCOL[_n] = (NVEC, _w)
    NVEC += _w

SINKS = 8
IN_SHAPES = {
    "x": (KD, P, S), "ctx": (KD, P, C), "vectors": (P, NVEC), "sinks": (P, SINKS),
    "ab_in": (D, 2948), "ab_out": (D, D), "cd_in": (D, 2744), "cd_out": (D, D),
    "cmp_w1": (2, CMP_LEN * HD, CMP_HID), "cmp_w2": (2, CMP_HID, HD), "uq": (256, 768), "ukv": (128, 1024),
    "ada_w": (4, D, 6 * D), "mlp_w1": (4, D, FF), "mlp_w2": (4, FF, D), "at_qkv": (D, 1536), "at_o": (D, D),
    "na_qkv": (D, 3 * D), "na_rpb": (32, 16 * 15), "na_o": (D, D), "pw1": (D, 2 * D), "pw2": (D, D), "ft_w": (D, D),
}


class Tile:

    def __init__(self, pairs, out, taker, op, dst, arg=None):
        self.pairs, self.out, self.taker, self.op, self.dst, self.arg = pairs, out, taker, op, dst, arg


def build_program(nc, dram, out_dram, stages_kept=10000):
    ctx = ExitStack()
    with ctx:
        def sb(name, shape, dt=F32):
            return ctx.enter_context(nc.sbuf_tensor(name, shape, dt))

        def sem(name):
            return ctx.enter_context(nc.semaphore(name))

        ARENA = 26112
        X = sb("X", [P, KD, S])
        H = sb("H", [P, KD, S])
        CX = sb("CX", [P, KD, C])
        CH = sb("CH", [P, KD, C])
        ring = sb("ring", [P, RING, SLOT])
        arena = sb("arena", [P, ARENA])
        ident = sb("ident", [P, P])
        identb = sb("identb", [P, P], BF16)
        mean_d = sb("mean_d", [P, P])
        diagm = sb("diagm", [P, P], BF16)
        prevm = sb("prevm", [P, P], BF16)
        vec = sb("vec", [P, NVEC])
        mods = sb("mods", [P, 2, 6 * KD, 2])
        sgain = sb("sgain", [P, 2, 2, KD])
        cond = sb("cond", [P, KD, 2])
        sinks = sb("sinks", [P, SINKS])
        small = sb("small", [P, 64])
        sd = sb("sd", [P, S])
        rstd = sb("rstd", [P, S])
        eps = sb("eps", [P, 1])[:, :]
        psum = ctx.enter_context(nc.psum_tensor("psum", [P, 8 * BANK], F32))

        def bank(b, n=BANK, at=0):
            return psum[:, b * BANK + at:b * BANK + at + n]

        def V(name):
            a, w = VCOL[name]
            return vec[:, a:a + w]

        top = [0]

        def reserve(n, at=None):
            if at is not None:
                top[0] = at
            a = arena[:, top[0]:top[0] + n]
            top[0] += n
            assert top[0] <= ARENA, top[0]
            return a

        stage_of = {e: sem(f"{e}_stage") for e in ("pe", "act", "dve", "pool")}
        act_steps, dve_steps, pool_steps = sem("act_steps"), sem("dve_steps"), sem("pool_steps")
        inputs_in, tables_in = sem("inputs_in"), sem("tables_in")
        weights_in = [sem(f"weights_in{i}") for i in range(RING)]
        weights_used = sem("weights_used")
        tile_ready, act_took, dve_took = sem("tile_ready"), sem("act_took"), sem("dve_took")
        ada_ready, ada_taken = sem("ada_ready"), sem("ada_taken")
        squares_ready, mean_ready, sd_ready = sem("squares_ready"), sem("mean_ready"), sem("sd_ready")
        square_read, scaled_ready, norm_ready = sem("square_read"), sem("scaled_ready"), sem("norm_ready")
        centred = sem("centred")
        spread_ready, yn_ready, swap_ready = sem("spread_ready"), sem("yn_ready"), sem("swap_ready")
        cos_ready, rope_done = sem("cos_ready"), sem("rope_done")
        scores_ready, negmax_ready, probs_ready = sem("scores_ready"), sem("negmax_ready"), sem("probs_ready")
        exp_done, turned, turned_copied = sem("exp_done"), sem("turned"), sem("turned_copied")
        o_ready, o_taken = sem("o_ready"), sem("o_taken")
        pv_done = sem("pv_done")
        bias_in, bias_used = [sem("bias_in0"), sem("bias_in1")], sem("bias_used")
        idx_ready, relu_ready, idx_taken = sem("idx_ready"), sem("relu_ready"), sem("idx_taken")
        scratch_in, out_done = sem("scratch_in"), sem("out_done")
        misc_pe, misc_act, misc_dve = sem("misc_pe"), sem("misc_act"), sem("misc_dve")

        rpb_table = nc.dram_tensor("rpb_table", (16, GRID, 15, GRID), F32).ap()

        stages, blocks = [], []

        def block(view):
            shape = view.shape
            n = 1
            for d in shape[1:]:
                n *= d
            assert n <= SLOT, shape
            blocks.append((view, n))
            return len(blocks) - 1

        def slot(b, k):
            return ring[:, b % RING, 0:blocks[b][1]].rearrange("p (k n) -> p k n", k=k)

        ada_left = []

        def start_ada(layer):
            ada_left.extend((layer, j) for j in range(12))

        def next_ada():
            if not ada_left:
                return None
            layer, j = ada_left.pop(0)
            b = block(dram["ada_w"][layer, :, 512 * j:512 * j + 512].rearrange("(k p) n -> p k n", p=P))
            return b, layer, j

        def stage(kind, **kw):
            kw["kind"] = kind
            kw.setdefault("loads", [])
            stages.append(kw)
            return kw

        def wide(src, tiles_of, k=KD, cols=512, width=None, **kw):
            total = width or src.shape[1]
            groups_ = []
            for c0 in range(0, total, cols):
                c1 = min(total, c0 + cols)
                b = block(src[:, c0:c1].rearrange("(k p) n -> p k n", p=P))
                groups_.append([b, (c0, c1)])
                a = next_ada()
                groups_[-1].append(a)
            st = stage("project", groups=[], **kw)
            for b, (c0, c1), a in groups_:
                st["groups"].append((b, tiles_of(b, c0, c1), a))
            return st

        def t_tile(b, k, col, width, act, n, taker, op, dst, arg=None, part=0):
            w = slot(b, k)
            return Tile([(w[:, i, col:col + width], act[:, i, 0:n]) for i in range(k)],
                        (part, width, n), taker, op, dst, arg)

        def n_tile(b, k, col, width, act, tt, taker, op, dst, arg=None):
            w = slot(b, k)
            return Tile([(act[:, i, tt * P:tt * P + P], w[:, i, col:col + width]) for i in range(k)],
                        (0, P, width), taker, op, dst, arg)

        def norm(src, dst, n, gain, shift=None, sq=None):
            stage("norm", src=src, dst=dst, n=n, gain=gain, shift=shift)

        def residual_tiles(b, c0, c1, dst, act, n, gate):
            return [t_tile(b, KD, P * j, P, act, n, "dve", "resid", dst[:, c0 // P + j, 0:n],
                           gate(c0 // P + j) if gate else None) for j in range((c1 - c0) // P)]

        top[0] = 0
        WORK = 9728
        work = reserve(6144)
        rope_t = reserve(2 * S + P)
        hn_t = reserve(PAIR_TILES * (PAIR_ROWS + P))
        QA, KA, QI, KI = (reserve(n * S).rearrange("p (t s) -> p t s", s=S) for n in (4, 1, 2, 1))
        QB, KB, Z = (reserve(n * S).rearrange("p (t s) -> p t s", s=S) for n in (4, 1, 8))
        VAB = reserve(ST * 256).rearrange("p (t n) -> p t n", t=ST)
        WI = reserve(ST * 4).rearrange("p (t n) -> p t n", t=ST)
        dsa_mask = reserve(3 * S // 2).bitcast(BF16).rearrange("p (t s) -> p t s", t=3)

        norm(X, H, S, lambda k: V("ab_norm")[:, k:k + 1])
        start_ada(0)
        ab_cols = ([("copy", QA[:, t]) for t in range(4)] + [("copy", KA[:, 0])] + [("copy", QI[:, t]) for t in range(2)]
                   + [("copy", KI[:, 0])] + [("copy", QB[:, t]) for t in range(4)] + [("copy", KB[:, 0])]
                   + [("silu", Z[:, t]) for t in range(8)])

        def ab_tiles(b, c0, c1):
            out = [t_tile(b, KD, P * j, P, H, S, "act", *ab_cols[c0 // P + j])
                   for j in range(min(4, len(ab_cols) - c0 // P))]
            if c1 == 2948:
                for tt in range(ST):
                    out.append(n_tile(b, KD, P, 256, H, tt, "dve", "copy", VAB[:, tt, :]))
                    out.append(n_tile(b, KD, P + 256, 4, H, tt, "dve", "scale", WI[:, tt, :], 1.0 / 16))
            return out

        wide(dram["ab_in"], ab_tiles, loads=[(rope_t, dram["rope_ab"]), (hn_t, dram["hn_pair"])])

        def pair_constants(i, hn_t=hn_t):
            a = PAIR_TILES * PAIR_ROWS
            return (hn_t[:, i * PAIR_ROWS:(i + 1) * PAIR_ROWS], hn_t[0:PAIR_ROWS, a + i * P:a + (i + 1) * P])

        def headnorm(tiles, n, consts, rows, parts, swap=None, cos=None, sin=None, wk=None):
            stage("headnorm", tiles=tiles, n=n, consts=consts, rows=rows, parts=parts, swap=swap, cos=cos, sin=sin,
                  wk=wk)

        cos_t, sin_t, swap_t = rope_t[:, 0:S], rope_t[:, S:2 * S], rope_t[:, 2 * S:2 * S + P]
        headnorm([(QA[:, t], V("qa_g")) for t in range(4)] + [(KA[:, 0], V("ka_g")), (KI[:, 0], V("ki_g"))]
                 + [(QB[:, t], V("qb_g")) for t in range(4)] + [(KB[:, 0], V("kb_g"))]
                 + [(QI[:, t], None) for t in range(2)],
                 S, pair_constants, PAIR_ROWS, P, swap_t, cos_t, sin_t, work)
        stage("dsa", wk=work)

        def causal(qt):
            return 0, qt + 1

        def causal_pv():
            return [(kt, kt * P, S) for kt in range(ST)]

        def attention(passes, wk, keys_max):
            stage("attention", passes=passes, wk=wk, keys_max=keys_max)

        def attn_pass(q, k, v, keys, pv, last, dst=None, z=None, masks=None, upper=False, first=True, qts=ST, gate=None,
                      sink=None, clamp=False, bias=None, krows=P):
            return dict(q=q, k=k, v=v, keys=keys, pv=pv, last=last, dst=dst, z=z, masks=masks, upper=upper,
                        first=first, qts=qts, gate=gate, sink=sink, clamp=clamp, bias=bias, krows=krows)

        passes = []
        for t in range(4):
            for g in range(2):
                lo = 64 * g
                passes.append(attn_pass(
                    lambda qt, t=t, lo=lo: QA[lo:lo + 64, t, qt * P:qt * P + P],
                    lambda a, b, lo=lo: KA[lo:lo + 64, 0, a:b],
                    lambda kt, g=g: VAB[:, kt, 64 * g:64 * g + 64], causal, causal_pv(), g == 1, H[:, t], Z[:, t],
                    lambda qt: [(0, diagm[:, :])] if qt == 0 else [(0, dsa_mask[:, qt - 1, 0:(qt + 1) * P])],
                    upper=g == 1))
        band_pv = [(kt, qt * P, qt * P + P) for qt in range(ST) for kt in range(max(0, qt - 1), qt + 1)]
        for t in range(4):
            for g in range(2):
                lo = 64 * g
                passes.append(attn_pass(
                    lambda qt, t=t, lo=lo: QB[lo:lo + 64, t, qt * P:qt * P + P],
                    lambda a, b, lo=lo: KB[lo:lo + 64, 0, a:b],
                    lambda kt, g=g: VAB[:, kt, 128 + 64 * g:128 + 64 * g + 64],
                    lambda qt: (max(0, qt - 1), qt + 1), band_pv, g == 1, H[:, 4 + t], Z[:, 4 + t],
                    lambda qt: [(0, diagm[:, :])] if qt == 0 else [(0, prevm[:, :]), (P, diagm[:, :])],
                    upper=g == 1, sink=sinks[:, 4 * g + t:4 * g + t + 1]))
        attention(passes, work, 512)
        wide(dram["ab_out"], lambda b, c0, c1: residual_tiles(b, c0, c1, X, H, S, None))

        top[0] = 0
        work = reserve(6144)
        rope_t = reserve(2 * S + P)
        hn_t = reserve(PAIR_TILES * (PAIR_ROWS + P))
        CQ, CKV, KR, Z2 = (reserve(n * S).rearrange("p (t s) -> p t s", s=S) for n in (2, 1, 1, 8))
        shared = top[0]
        QC, KC, VC, KS, KW = (reserve(n * S).rearrange("p (t s) -> p t s", s=S) for n in (4, 1, 1, 1, 1))
        VSW = reserve(ST * 256).rearrange("p (t n) -> p t n", t=ST)
        GC = reserve(ST * 24).rearrange("p (t n) -> p t n", t=ST)
        KCT, VCN = reserve(32), reserve(P)
        cmpm = reserve(ST * NCMP).rearrange("p (t n) -> p t n", t=ST)
        rope_c = reserve(2 * NCMP)
        cmpmb = reserve(ST * 16).bitcast(BF16).rearrange("p (t n) -> p t n", t=ST)
        norm(X, H, S, lambda k: V("cd_norm")[:, k:k + 1])
        cd_cols = ([("copy", QC[:, t]) for t in range(4)] + [("copy", KC[:, 0]), ("copy", VC[:, 0]), ("copy", KS[:, 0]),
                   ("copy", KW[:, 0])] + [("copy", CQ[:, t]) for t in range(2)] + [("copy", CKV[:, 0])]
                   + [("silu", Z2[:, t]) for t in range(8)])

        def cd_tiles(b, c0, c1):
            if c0 == 2560:
                return []
            out = [t_tile(b, KD, P * j, P, H, S, "act", *cd_cols[c0 // P + j])
                   for j in range(min(4, len(cd_cols) - c0 // P))]
            return out

        def cd_all(b, c0, c1):
            out = []
            if c0 < 2048:
                return cd_tiles(b, c0, c1)
            if c0 == 2048:
                out = [t_tile(b, KD, P * j, P, H, S, "act", *cd_cols[16 + j]) for j in range(3)]
                out.append(t_tile(b, KD, 384, 32, H, S, "act", "copy", KR[64:96, 0], part=64))
                for tt in range(ST):
                    out.append(n_tile(b, KD, 416, 24, H, tt, "act", "sigmoid", GC[:, tt, :]))
                return out
            for tt in range(ST):
                out.append(n_tile(b, KD, 0, 256, H, tt, "act", "copy", VSW[:, tt, :]))
            return out

        groups_ = []
        for c0, c1 in ((0, 512), (512, 1024), (1024, 1536), (1536, 2048), (2048, 2488), (2488, 2744)):
            b = block(dram["cd_in"][:, c0:c1].rearrange("(k p) n -> p k n", p=P))
            groups_.append((b, (c0, c1), next_ada()))
        stage("project", groups=[(b, cd_all(b, *c), a) for b, c, a in groups_],
              loads=[(rope_t, dram["rope_ab"]), (hn_t, dram["hn_pair"]), (cmpm.rearrange("p t n -> p (t n)"),
                     dram["cmp_mask"].rearrange("p t n -> p (t n)")), (rope_c, dram["rope_cmp"])])
        cos_t, sin_t, swap_t = rope_t[:, 0:S], rope_t[:, S:2 * S], rope_t[:, 2 * S:2 * S + P]

        def pair_constants2(i, hn_t=hn_t):
            a = PAIR_TILES * PAIR_ROWS
            return (hn_t[:, i * PAIR_ROWS:(i + 1) * PAIR_ROWS], hn_t[0:PAIR_ROWS, a + i * P:a + (i + 1) * P])

        cmp_blocks = []
        for kv in range(2):
            cmp_blocks.append(block(dram["cmp_w1"][kv].rearrange("(l d) m -> d l m", d=HD)))
            cmp_blocks.append(block(dram["cmp_w2"][kv]))
        stage("compress", wk=work, wblocks=cmp_blocks)
        headnorm([(QC[:, t], V("qc_g")) for t in range(4)] + [(KS[:, 0], V("ks_g")), (KW[:, 0], V("kw_g"))],
                 S, pair_constants2, PAIR_ROWS, P, swap_t, cos_t, sin_t, work)
        headnorm([(KCT[:, 0:NCMP], V("kc_g"))], NCMP, pair_constants2, PAIR_ROWS, P, swap_t, rope_c[:, 0:NCMP],
                 rope_c[:, NCMP:2 * NCMP], work)
        passes = []
        for t in range(4):
            for g in range(2):
                lo, h = 64 * g, 4 * g + t
                q = lambda qt, t=t, lo=lo: QC[lo:lo + 64, t, qt * P:qt * P + P]
                passes.append(attn_pass(
                    q, lambda a, b, lo=lo: KCT[lo:lo + 64, a:min(b, NCMP)],
                    lambda kt, g=g: VCN[0:NCMP, 64 * g:64 * g + 64], lambda qt: (0, 1), [(0, 0, S)], False,
                    masks=lambda qt: [(0, cmpmb[:, qt, 0:NCMP])], upper=g == 1, clamp=True, krows=NCMP,
                    gate=lambda qt, h=h: GC[:, qt, 3 * h:3 * h + 1]))
                for br, (kk, v0) in enumerate(((KS, 0), (KW, 128))):
                    passes.append(attn_pass(
                        q, lambda a, b, lo=lo, kk=kk: kk[lo:lo + 64, 0, a:b],
                        lambda kt, g=g, v0=v0: VSW[:, kt, v0 + 64 * g:v0 + 64 * g + 64], causal, causal_pv(),
                        g == 1 and br == 1, H[:, t], Z2[:, t],
                        lambda qt: [(qt * P, diagm[:, :])], upper=g == 1, first=False,
                        gate=lambda qt, h=h, br=br: GC[:, qt, 3 * h + br + 1:3 * h + br + 2]))
        attention(passes, work, 512)
        top[0] = shared
        QD, KDT = (reserve(8 * S).rearrange("p (t s) -> p t s", s=S) for _ in range(2))
        VD = reserve(ST * 512).rearrange("p (t n) -> p t n", t=ST)

        def lat_constants(i):
            return None

        stage("latnorm", wk=work, loads=[(rope_t, dram["rope_mla"]), (hn_t[:, 0:MLA_TILES * (MLA_ROWS + P)], dram["hn_mla"])],
              CQ=CQ, CKV=CKV)
        b0 = block(dram["uq"].rearrange("(k p) n -> p k n", p=P))
        a0 = next_ada()
        b1 = block(dram["ukv"])
        a1 = next_ada()
        w1v = ring[:, b1 % RING, 0:1024].rearrange("p (k n) -> p k n", k=1)
        tl0 = [t_tile(b0, 2, MLA_W * h, MLA_W, CQ, S, "act", "copy", QD[0:MLA_W, h]) for h in range(8)]
        tl1 = [Tile([(w1v[:, 0, 64 * h:64 * h + 64], CKV[:, 0, :])], (0, 64, S), "act", "copy", KDT[0:64, h])
               for h in range(8)]
        tl1 += [Tile([(CKV[:, 0, tt * P:tt * P + P], w1v[:, 0, 512:1024])], (0, P, 512), "act", "copy", VD[:, tt, :])
                for tt in range(ST)]
        stage("project", groups=[(b0, tl0, a0), (b1, tl1, a1)],
              extra=[(KDT[64:96, h], KR[64:96, 0]) for h in range(8)])

        def mla_constants(i, hn_t=hn_t):
            a = MLA_TILES * MLA_ROWS
            return (hn_t[0:MLA_W, i * MLA_ROWS:(i + 1) * MLA_ROWS], hn_t[0:MLA_ROWS, a + i * P:a + i * P + MLA_W])

        for tiles in ([(QD[0:MLA_W, h], V("qd_g")) for h in range(8)], [(KDT[0:MLA_W, h], V("kd_g")) for h in range(8)]):
            headnorm(tiles, S, mla_constants, MLA_ROWS, MLA_W, rope_t[0:MLA_W, 2 * S:2 * S + MLA_W], rope_t[:, 0:S],
                     rope_t[:, S:2 * S], work)
        passes = []
        for h in range(8):
            passes.append(attn_pass(
                lambda qt, h=h: QD[0:MLA_W, h, qt * P:qt * P + P], lambda a, b, h=h: KDT[0:MLA_W, h, a:b],
                lambda kt, h=h: VD[:, kt, 64 * h:64 * h + 64], causal, causal_pv(), h % 2 == 1, H[:, 4 + h // 2],
                Z2[:, 4 + h // 2], lambda qt: [(qt * P, diagm[:, :])], upper=h % 2 == 1))
        attention(passes, work, 512)
        wide(dram["cd_out"], lambda b, c0, c1: residual_tiles(b, c0, c1, X, H, S, None))
        while ada_left:
            stage("project", groups=[(None, [], next_ada())])

        def mod(layer, chunk, v):
            return lambda k: mods[:, layer % 2, chunk * KD + k, v:v + 1]

        def sg(half, v):
            return lambda k: sgain[:, half, v, k:k + 1]

        def mlp(layer, with_ctx):
            norm(X, H, S, sg(1, 0), mod(layer, 3, 0))
            if with_ctx:
                norm(CX, CH, C, sg(1, 1), mod(layer, 3, 1))
            start_ada(layer + 1) if layer < 3 else None
            top[0] = 0
            hid = reserve(32 * S).rearrange("p (t s) -> p t s", s=S)
            hidc = reserve(32 * C).rearrange("p (t s) -> p t s", s=C) if with_ctx else None

            def up(b, c0, c1):
                out = []
                for j in range(4):
                    out.append(t_tile(b, KD, P * j, P, H, S, "act", "relu2", hid[:, c0 // P + j]))
                    if with_ctx:
                        out.append(t_tile(b, KD, P * j, P, CH, C, "act", "relu2", hidc[:, c0 // P + j]))
                return out

            wide(dram["mlp_w1"][layer], up)
            groups = []
            for half in range(2):
                for kb in range(4):
                    b = block(dram["mlp_w2"][layer, 1024 * kb:1024 * kb + 1024, 512 * half:512 * half + 512]
                              .rearrange("(k p) n -> p k n", p=P))
                    groups.append((half, kb, b, next_ada()))
            stage("down", groups=groups, hid=hid, hidc=hidc, gate=mod(layer, 5, 0), gatec=mod(layer, 5, 1))

        def prep(layer, with_ctx):
            stage("prep", layer=layer)

        prep(0, True)
        norm(X, H, S, sg(0, 0), mod(0, 0, 0))
        norm(CX, CH, C, sg(0, 1), mod(0, 0, 1))
        top[0] = 0
        work = reserve(WORK)
        rope_t = reserve(2 * S + P)
        hn_t = reserve(PAIR_TILES * (PAIR_ROWS + P))
        Q = reserve(8 * S).rearrange("p (t s) -> p t s", s=S)
        QX = reserve(8 * C).rearrange("p (t s) -> p t s", s=C)
        K2 = reserve(2 * (S + C)).rearrange("p (t s) -> p t s", s=S + C)
        V2 = reserve(6 * 256).rearrange("p (t n) -> p t n", t=6)

        def at_tiles(b, c0, c1):
            out = []
            if c0 < 1024:
                for j in range(4):
                    out.append(t_tile(b, KD, P * j, P, H, S, "act", "copy", Q[:, c0 // P + j]))
                    out.append(t_tile(b, KD, P * j, P, CH, C, "act", "copy", QX[:, c0 // P + j]))
                return out
            for j in range(2):
                out.append(t_tile(b, KD, P * j, P, H, S, "act", "copy", K2[:, j, 0:S]))
                out.append(t_tile(b, KD, P * j, P, CH, C, "act", "copy", K2[:, j, S:S + C]))
            for tt in range(6):
                src, t0 = (H, tt) if tt < ST else (CH, tt - ST)
                out.append(n_tile(b, KD, 256, 256, src, t0, "act", "copy", V2[:, tt, :]))
            return out

        wide(dram["at_qkv"], at_tiles, loads=[(rope_t, dram["rope_at"]), (hn_t, dram["hn_pair"])])

        def pair_constants3(i, hn_t=hn_t):
            a = PAIR_TILES * PAIR_ROWS
            return (hn_t[:, i * PAIR_ROWS:(i + 1) * PAIR_ROWS], hn_t[0:PAIR_ROWS, a + i * P:a + (i + 1) * P])

        headnorm([(Q[:, t], V("at_q_g")) for t in range(8)] + [(K2[:, t, 0:S], V("at_k_g")) for t in range(2)], S,
                 pair_constants3, PAIR_ROWS, P, rope_t[:, 2 * S:2 * S + P], rope_t[:, 0:S], rope_t[:, S:2 * S], work)
        headnorm([(QX[:, t], V("at_q_g")) for t in range(8)] + [(K2[:, t, S:S + C], V("at_k_g")) for t in range(2)], C,
                 pair_constants3, PAIR_ROWS, P, None, None, None, work)
        passes = []
        for t in range(8):
            for g in range(2):
                lo, vc = 64 * g, 64 * (2 * (t // 4) + g)
                passes.append(attn_pass(
                    lambda qt, t=t, lo=lo: Q[lo:lo + 64, t, qt * P:qt * P + P],
                    lambda a, b, t=t, lo=lo: K2[lo:lo + 64, t // 4, a:b], lambda kt, vc=vc: V2[:, kt, vc:vc + 64],
                    lambda qt: (0, 6), [(kt, 0, S) for kt in range(6)], g == 1, H[:, t], None, upper=g == 1))
        for t in range(8):
            for g in range(2):
                lo, vc = 64 * g, 64 * (2 * (t // 4) + g)
                passes.append(attn_pass(
                    lambda qt, t=t, lo=lo: QX[lo:lo + 64, t, qt * P:qt * P + P],
                    lambda a, b, t=t, lo=lo: K2[lo:lo + 64, t // 4, S + a:S + b],
                    lambda kt, vc=vc: V2[:, 4 + kt, vc:vc + 64],
                    lambda qt: (0, 2), [(kt, 0, C) for kt in range(2)], g == 1, CH[:, t], None, upper=g == 1, qts=2))
        attention(passes, work, 768)

        def at_out(b, c0, c1):
            out = []
            out += residual_tiles(b, c0, c1, X, H, S, mod(0, 2, 0))
            out += residual_tiles(b, c0, c1, CX, CH, C, mod(0, 2, 1))
            return out

        wide(dram["at_o"], at_out)
        mlp(0, True)
        prep(1, True)
        norm(X, H, S, sg(0, 0), mod(1, 0, 0))
        norm(CX, CH, C, sg(0, 1), mod(1, 0, 1))
        top[0] = 0
        work = reserve(7680)
        QN = reserve(8 * S).rearrange("p (t s) -> p t s", s=S)
        KN = reserve(8 * (S + C)).rearrange("p (t s) -> p t s", s=S + C)
        VN = reserve(6 * 1024).rearrange("p (t n) -> p t n", t=6)
        na_sel, na_rpb = KN.rearrange("p t s -> p (t s)")[:, 0:4096], VN.rearrange("p t s -> p (t s)")[:, 0:240]
        na_tab = QN.rearrange("p t s -> p (t s)")
        stage("rpb", sel=na_sel, rpb=na_rpb, tab=na_tab, load_first=True)

        def na_tiles(b, c0, c1):
            out = []
            for j in range(4):
                if c0 < 1024:
                    out.append(t_tile(b, KD, P * j, P, H, S, "act", "scale", QN[:, c0 // P + j], 0.125))
                elif c0 < 2048:
                    kt = c0 // P - 8 + j
                    out.append(t_tile(b, KD, P * j, P, H, S, "act", "copy", KN[:, kt, 0:S]))
                    out.append(t_tile(b, KD, P * j, P, CH, C, "act", "copy", KN[:, kt, S:S + C]))
            if c0 >= 2048:
                for tt in range(6):
                    src, t0 = (H, tt) if tt < ST else (CH, tt - ST)
                    out.append(n_tile(b, KD, 0, 512, src, t0, "act", "copy", VN[:, tt, c0 - 2048:c0 - 1536]))
            return out

        wide(dram["na_qkv"], na_tiles)
        bias_buf = CX.rearrange("p t s -> p (t s)").rearrange("p (b n) -> p b n", b=2)
        passes = []
        for t in range(8):
            for g in range(2):
                lo = 64 * g
                h = 2 * t + g
                passes.append(attn_pass(
                    lambda qt, t=t, lo=lo: QN[lo:lo + 64, t, qt * P:qt * P + P],
                    lambda a, b, t=t, lo=lo: KN[lo:lo + 64, t, a:b], lambda kt, h=h: VN[:, kt, 64 * h:64 * h + 64],
                    lambda qt: (0, 6), [(kt, 0, S) for kt in range(6)], g == 1, H[:, t], None, upper=g == 1,
                    bias=lambda qt, h=h: bias_buf[:, h % 2, (7 - 2 * qt) * GRID:(7 - 2 * qt) * GRID + S]))
        attention(passes, work, 768)
        wide(dram["na_o"], lambda b, c0, c1: residual_tiles(b, c0, c1, X, H, S, mod(1, 2, 0)))
        mlp(1, False)
        prep(2, False)
        norm(X, H, S, sg(0, 0), mod(2, 0, 0))
        top[0] = 0
        UP = S + TAPS - 1
        U = reserve(KD * UP).rearrange("p (t s) -> p t s", s=UP)
        SIG = reserve(KD * S).rearrange("p (t s) -> p t s", s=S)
        CV = reserve(KD * S).rearrange("p (t s) -> p t s", s=S)
        work = reserve(4096)
        wide(dram["pw1"][:, D:2 * D], lambda b, c0, c1: [
            t_tile(b, KD, P * j, P, H, S, "act", "sigmoidb", SIG[:, c0 // P + j],
                   V("cv_b1")[:, KD + c0 // P + j:KD + c0 // P + j + 1]) for j in range(4)], pads=U)
        wide(dram["pw1"][:, 0:D], lambda b, c0, c1: [
            t_tile(b, KD, P * j, P, H, S, "dve", "glu", U[:, c0 // P + j, TAPS // 2:TAPS // 2 + S],
                   (V("cv_b1")[:, c0 // P + j:c0 // P + j + 1], SIG[:, c0 // P + j])) for j in range(4)])
        stage("conv", U=U, CV=CV)
        stage("layernorm", src=CV, dst=H, sq=SIG)
        wide(dram["pw2"], lambda b, c0, c1: [
            t_tile(b, KD, P * j, P, H, S, "dve", "residb", X[:, c0 // P + j],
                   (V("cv_b2")[:, c0 // P + j:c0 // P + j + 1], mod(2, 2, 0)(c0 // P + j), SIG[:, j % 2]))
            for j in range(4)])
        mlp(2, False)
        prep(3, False)
        norm(X, H, S, sg(0, 0), mod(3, 0, 0))
        top[0] = 0
        FA = reserve(ST * 4 * 512).rearrange("p (t g n) -> p t g n", t=ST, g=4)
        dg = reserve(2 * 512).rearrange("p (k n) -> p k n", k=2)
        dq = reserve(ST * 2 * S).rearrange("p (k n) -> p k n", k=ST)
        tmpf = reserve(2 * S).rearrange("p (t s) -> p t s", s=S)
        stage("idle", loads=[(dg, dram["dft_group"].rearrange("(k p) n -> p k n", p=P)),
                             (dq, dram["dft_seq"].rearrange("(k p) n -> p k n", p=P))])
        tl = [Tile([(H[:, 2 * g + k, tt * P:tt * P + P], dg[:, k, :]) for k in range(2)], (0, P, 512), "act", "copy",
                   FA[:, tt, g, :]) for g in range(4) for tt in range(ST)]
        stage("project", groups=[(None, tl, None)])
        tl = []
        for g in range(4):
            for d2 in range(2):
                prs = []
                for tt in range(ST):
                    prs.append((FA[:, tt, g, d2 * P:d2 * P + P], dq[:, tt, 0:S]))
                    prs.append((FA[:, tt, g, GW + d2 * P:GW + d2 * P + P], dq[:, tt, S:2 * S]))
                tl.append(Tile(prs, (0, P, S), "act", "copy", H[:, 2 * g + d2]))
        stage("project", groups=[(None, tl, None)])
        wide(dram["ft_w"], lambda b, c0, c1: [
            t_tile(b, KD, P * j, P, H, S, "dve", "residb", X[:, c0 // P + j],
                   (V("ft_b")[:, c0 // P + j:c0 // P + j + 1], mod(3, 2, 0)(c0 // P + j), tmpf[:, j % 2]))
            for j in range(4)])
        mlp(3, False)
        norm(X, H, S, lambda k: V("final_g")[:, k:k + 1])
        assert not ada_left

        del stages[stages_kept:]

        used = []
        for st in stages:
            if st["kind"] == "project":
                for b, _, a in st["groups"]:
                    used += ([b] if b is not None else []) + ([a[0]] if a else [])
            elif st["kind"] == "down":
                for _, _, b, a in st["groups"]:
                    used += [b] + ([a[0]] if a else [])
            elif st["kind"] == "compress":
                used += st["wblocks"]
        assert used == list(range(len(used))), used[:60]

        tables_before = []
        n_tab = 0
        for st in stages:
            tables_before.append(n_tab)
            n_tab += 16 * (2 if st["kind"] == "rpb" else len(st["loads"]))
        N_INPUTS = 11
        sd_count = misc_count = 0
        for st in stages:
            st["sd0"], st["pe0"] = sd_count, misc_count
            sd_count += dict(norm=1, headnorm=2, latnorm=1, layernorm=1).get(st["kind"], 0)
            misc_count += dict(compress=4, down=8, rpb=16, layernorm=1).get(st["kind"], 0)

        def gate(eng, own, s):
            if s > 0:
                for name, sm in stage_of.items():
                    eng.wait_ge(sm, s)
            else:
                eng.wait_ge(inputs_in, 16 * N_INPUTS)
            if tables_before[s]:
                eng.wait_ge(tables_in, tables_before[s])

        nc_block = ctx.enter_context(nc.Block())

        @nc_block.sync
        def _(sp):
            for dst, src in ((X[:, :, :], dram["x"].rearrange("k p s -> p k s")), (vec[:, :], dram["vectors"]),
                             (ident[:, :], dram["ident"]), (arena[:, 0:P], dram["diag_mask"]),
                             (arena[:, P:2 * P], dram["prev_mask"]),
                             (sinks[:, :], dram["sinks"]), (CX[:, :, :], dram["ctx"].rearrange("k p s -> p k s"))):
                sp.dma_start(dst, src).then_inc(inputs_in, 16)
            for b in range(len(used)):
                view, n = blocks[b]
                if b >= RING:
                    sp.wait_ge(weights_used, b - RING + 1)
                k = view.shape[1] if len(view.shape) == 3 else 1
                rows = view.shape[0]
                dst = ring[0:rows, b % RING, 0:n]
                if len(view.shape) == 3:
                    dst = dst.rearrange("p (k n) -> p k n", k=k)
                sp.dma_start(dst, view).then_inc(weights_in[b % RING], 16)
                if rows == HD:
                    sp.dma_start(ring[HD:2 * HD, b % RING, 0:n].rearrange("p (k n) -> p k n", k=k),
                                 view).then_inc(weights_in[b % RING], 16)

        slot_count = [0] * RING
        landed = []
        for b in range(len(used)):
            slot_count[b % RING] += 32 if blocks[b][0].shape[0] == HD else 16
            landed.append(slot_count[b % RING])

        n_units = sum(sum(p["qts"] for p in st["passes"]) for st in stages if st["kind"] == "attention")

        def units_of(st):
            return [(pi, qt) for pi, p in enumerate(st["passes"]) for qt in range(p["qts"])]

        def attn_buffers(st):
            km = st["keys_max"]
            probs = [st["wk"][:, i * km:(i + 1) * km] for i in range(2)]
            turned_b = [st["wk"][:, 2 * km + i * km * 4:2 * km + (i + 1) * km * 4].rearrange("p (t s) -> p t s", s=S)
                        for i in range(2)]
            return probs, turned_b

        def unit_keys(p, qt):
            a, b = p["keys"](qt)
            n = (b - a) * P if p["krows"] == P else p["krows"]
            return a, b, n

        @nc_block.tensor
        def _(pe):
            tiles_made, takers = [0], []
            taken = {"act": 0, "dve": 0}
            n = dict(block=0, ada=0, norm=0, sq=0, mean=0, spread=0, swap=0, unit=0, pair=0, pas=0, idx=0, down=0,
                     yn=0, rope=0, centred=0, misc=0)

            def weights(b):
                pe.wait_ge(weights_in[b % RING], landed[b])

            def ada(a):
                b, layer, j = a
                weights(b)
                w = slot(b, KD)
                if n["ada"] >= 1:
                    pe.wait_ge(ada_taken, n["ada"])
                for m in range(4):
                    for k in range(KD):
                        last = nc.tensor.matmul(bank(7)[:, 2 * m:2 * m + 2], w[:, k, P * m:P * m + P], cond[:, k, :],
                                                start=(m == 0 and k == 0), stop=(k == KD - 1), skip_group_check=True)
                last.then_inc(ada_ready, 1)
                n["ada"] += 1
                pe.wait_ge(ada_ready, n["ada"])
                pe.sem_inc(weights_used, 1)

            def project(st):
                first = True
                for b, tiles, a in st["groups"]:
                    if b is not None:
                        weights(b)
                    for i, t in enumerate(tiles):
                        part, rows, cols = t.out
                        at = tiles_made[0]
                        if at >= PROJ_BANKS:
                            s_, c_ = takers[at - PROJ_BANKS]
                            pe.wait_ge(s_, c_)
                        out = psum[part:part + rows, (at % PROJ_BANKS) * BANK:(at % PROJ_BANKS) * BANK + cols]
                        for k, (lhs, rhs) in enumerate(t.pairs):
                            last = nc.tensor.matmul(out, lhs, rhs, start=(k == 0), stop=(k == len(t.pairs) - 1))
                        last.then_inc(tile_ready, 1)
                        tiles_made[0] += 1
                        taken[t.taker] += 1
                        takers.append((act_took if t.taker == "act" else dve_took, taken[t.taker]))
                    if b is not None:
                        pe.wait_ge(tile_ready, tiles_made[0])
                        pe.sem_inc(weights_used, 1)
                    if a:
                        ada(a)

            def down(st):
                hid, hidc = st["hid"], st["hidc"]
                for half, kb, b, a in st["groups"]:
                    weights(b)
                    w = slot(b, KD)
                    if kb == 0 and half:
                        pe.wait_ge(dve_took, taken["dve"])
                    for m in range(4):
                        for k in range(KD):
                            last = nc.tensor.matmul(bank(m), w[:, k, P * m:P * m + P], hid[:, KD * kb + k, :],
                                                    start=(kb == 0 and k == 0), stop=(kb == 3 and k == KD - 1))
                        if hidc is not None:
                            for k in range(KD):
                                last = nc.tensor.matmul(bank(4 + m // 2, C, C * (m % 2)), w[:, k, P * m:P * m + P],
                                                        hidc[:, KD * kb + k, :], start=(kb == 0 and k == 0 and m % 2 == 0),
                                                        stop=(kb == 3 and k == KD - 1), skip_group_check=True)
                    last.then_inc(misc_pe, 1)
                    n["misc"] += 1
                    pe.wait_ge(misc_pe, n["misc"])
                    pe.sem_inc(weights_used, 1)
                    if kb == 3:
                        pe.sem_inc(tile_ready, 1)
                        tiles_made[0] += 1
                        taken["dve"] += 1
                        takers.append((dve_took, taken["dve"]))
                    if a:
                        ada(a)

            def norm_sum(st):
                for k in range(KD):
                    pe.wait_ge(squares_ready, n["sq"] + k + 1)
                    last = nc.tensor.matmul(bank(6, st["n"]), mean_d[:, :], st["dst"][:, k, 0:st["n"]],
                                            start=(k == 0), stop=(k == KD - 1))
                last.then_inc(mean_ready, 1)
                n["sq"] += KD

            def headnorm(st):
                N, parts, rows = st["n"], st["parts"], st["rows"]
                normed = [t for t in st["tiles"] if t[1] is not None]
                sqb = st["wk"][:, 0:2 * S].rearrange("p (b s) -> p b s", b=2)
                for i in range(len(normed)):
                    pe.wait_ge(squares_ready, n["sq"] + i + 1)
                    last = nc.tensor.matmul(bank(0, N)[0:rows], st["consts"](i)[0], sqb[0:parts, i % 2, 0:N],
                                            start=(i == 0), stop=(i == len(normed) - 1))
                    last.then_inc(square_read, 1)
                n["sq"] += len(normed)
                rs = st["wk"][0:rows, 3 * S:3 * S + N]
                ynb = st["wk"][0:parts, 4 * S:6 * S].rearrange("p (b s) -> p b s", b=2)
                for i, (data, g) in enumerate(st["tiles"]):
                    if g is not None:
                        if i == 0:
                            pe.wait_ge(sd_ready, st["sd0"] + 2)
                        if i >= 2:
                            pe.wait_ge(yn_ready, n["yn"] + i - 1)
                        nc.tensor.matmul(bank(1 + i % 2, N)[0:parts], st["consts"](i)[1], rs, start=True,
                                         stop=True).then_inc(spread_ready, 1)
                    if st["swap"] is not None and i >= 1:
                        swap(st, i - 1)
                if st["swap"] is not None:
                    swap(st, len(st["tiles"]) - 1)
                    n["rope"] += len(st["tiles"])
                n["yn"] += len(normed)

            def swap(st, i):
                N, parts = st["n"], st["parts"]
                data, g = st["tiles"][i]
                normed_so_far = sum(t[1] is not None for t in st["tiles"][:i + 1])
                ynb = st["wk"][0:parts, 4 * S:6 * S].rearrange("p (b s) -> p b s", b=2)
                if g is not None:
                    pe.wait_ge(yn_ready, n["yn"] + normed_so_far)
                    src = ynb[:, i % 2, 0:N]
                else:
                    src = data
                if i >= 2:
                    pe.wait_ge(rope_done, n["rope"] + i - 1)
                nc.tensor.matmul(bank(3 + i % 2, N)[0:parts], st["swap"], src, start=True,
                                 stop=True).then_inc(swap_ready, 1)

            def attention(st):
                units = units_of(st)
                probs, turned_b = attn_buffers(st)
                base, pair0, pas0 = n["unit"], n["pair"], n["pas"]
                pairs = [0]

                def scores(u):
                    pi, qt = units[u]
                    p = st["passes"][pi]
                    a, b, nk = unit_keys(p, qt)
                    if u >= 2:
                        pe.wait_ge(exp_done, base + u - 1)
                    buf = (u % 2) * 2 * BANK
                    masks = p["masks"](qt) if p["masks"] else []
                    for c0 in range(0, nk, BANK):
                        c1 = min(nk, c0 + BANK)
                        last = nc.tensor.matmul(psum[:, buf + c0:buf + c1], p["q"](qt), p["k"](a * P + c0, a * P + c1),
                                                start=True, stop=not masks)
                    for m, (c0, mask) in enumerate(masks):
                        last = nc.tensor.matmul(psum[:, buf + c0:buf + c0 + mask.shape[1]], identb[:, :], mask,
                                                start=False, stop=m == len(masks) - 1)
                    last.then_inc(scores_ready, 1)

                def turn(u):
                    pi, qt = units[u]
                    p = st["passes"][pi]
                    a, b, nk = unit_keys(p, qt)
                    pe.wait_ge(probs_ready, base + u + 1)
                    if u >= 1:
                        pe.wait_ge(turned_copied, base + u)
                    for j in range(b - a):
                        w = min(P, nk - j * P)
                        last = nc.tensor.transpose(psum[0:w, 4 * BANK + j * P:4 * BANK + j * P + P],
                                                   probs[u % 2][:, j * P:j * P + w], ident[:, :])
                    last.then_inc(turned, 1)

                def weigh(pi):
                    p = st["passes"][pi]
                    u_last = sum(q["qts"] for q in st["passes"][:pi + 1]) - 1
                    pe.wait_ge(turned_copied, base + u_last + 1)
                    pr = pairs[0]
                    if p["first"] and not p["upper"] and pr >= 2:
                        pe.wait_ge(o_taken, pair0 + pr - 1)
                    lo = 64 if p["upper"] else 0
                    for i, (kt, q0, q1) in enumerate(p["pv"]):
                        last = nc.tensor.matmul(
                            psum[lo:lo + 64, (6 + pr % 2) * BANK + q0:(6 + pr % 2) * BANK + q1], p["v"](kt),
                            turned_b[pi % 2][0:p["krows"], kt, q0:q1], start=(i == 0 and p["first"]),
                            stop=(i == len(p["pv"]) - 1 and (pi + 1 == len(st["passes"]) or st["passes"][pi + 1]["first"])),
                            skip_group_check=True)
                    last.then_inc(pv_done, 1)
                    if p["last"]:
                        pairs[0] += 1

                U = len(units)
                for u in range(U + 3):
                    if u < U:
                        scores(u)
                    if 2 <= u < U + 2:
                        turn(u - 2)
                    if u >= 3:
                        pi, qt = units[u - 3]
                        if qt == st["passes"][pi]["qts"] - 1:
                            weigh(pi)
                n["unit"] += U
                n["pair"] += pairs[0]
                n["pas"] += len(st["passes"])

            def dsa(st):
                for qt in range(1, ST):
                    nk = (qt + 1) * P
                    for h in range(4):
                        if n["idx"] >= 2:
                            pe.wait_ge(relu_ready, n["idx"] - 1)
                        lo = 64 * (h % 2)
                        nc.tensor.matmul(bank(n["idx"] % 2, nk), QI[lo:lo + 64, h // 2, qt * P:qt * P + P],
                                         KI[lo:lo + 64, 0, 0:nk], start=True, stop=True).then_inc(idx_ready, 1)
                        n["idx"] += 1

            def compress(st):
                wk = st["wk"]
                F = wk[:, 0:2 * CMP_LEN * NCMP].rearrange("p (v l n) -> p v l n", v=2, l=CMP_LEN)
                hid = wk[:, 2048:2048 + 4 * NCMP].rearrange("p (v g n) -> p v g n", v=2, g=2)
                for v in range(2):
                    b1, b2 = st["wblocks"][2 * v:2 * v + 2]
                    weights(b1)
                    weights(b2)
                    pe.wait_ge(misc_dve, v + 1)
                    w1 = slot(b1, CMP_LEN)
                    for g in range(2):
                        for l in range(CMP_LEN):
                            last = nc.tensor.matmul(bank(g, NCMP), w1[64 * g:64 * g + 64, l, :],
                                                    F[64 * g:64 * g + 64, v, l, :], start=(l == 0), stop=(l == CMP_LEN - 1))
                    last.then_inc(misc_pe, 1)
                    n["misc"] += 1
                    pe.wait_ge(misc_act, 2 * v + 1)
                    w2 = ring[:, b2 % RING, 0:HD]
                    for g in range(2):
                        if v == 0:
                            last = nc.tensor.matmul(psum[64 * g:64 * g + 64, 2 * BANK:2 * BANK + NCMP], w2, hid[:, v, g, :],
                                                    start=True, stop=True)
                        else:
                            last = nc.tensor.matmul(psum[0:NCMP, 3 * BANK + 64 * g:3 * BANK + 64 * g + 64],
                                                    hid[:, v, g, :], w2, start=(g == 0), stop=True, skip_group_check=True)
                    last.then_inc(misc_pe, 1)
                    n["misc"] += 1
                    pe.wait_ge(misc_pe, n["misc"])
                    pe.sem_inc(weights_used, 2)

            def latnorm(st):
                sqb = st["wk"][:, 0:3 * S].rearrange("p (b s) -> p b s", b=3)
                for i in range(3):
                    pe.wait_ge(squares_ready, n["sq"] + i + 1)
                    last = nc.tensor.matmul(bank(0 if i < 2 else 1), mean_d[:, :], sqb[:, i, :], start=(i != 1),
                                            stop=(i != 0))
                last.then_inc(mean_ready, 1)
                n["sq"] += 3

            def rpb(st):
                for m in range(2):
                    for c in range(8):
                        if n["idx"] >= 0 and m * 8 + c >= 2:
                            pe.wait_ge(misc_act, 4 + m * 8 + c - 1)
                        nc.tensor.matmul(bank(c % 2)[0:120], st["rpb"][0:32, 120 * m:120 * m + 120],
                                         st["sel"][0:32, 512 * c:512 * c + 512], start=True, stop=True).then_inc(misc_pe, 1)
                        n["misc"] += 1

            def layernorm(st):
                for k in range(KD):
                    last = nc.tensor.matmul(bank(0), mean_d[:, :], st["src"][:, k, :], start=(k == 0), stop=(k == KD - 1))
                last.then_inc(misc_pe, 1)
                n["misc"] += 1
                for k in range(KD):
                    pe.wait_ge(squares_ready, n["sq"] + k + 1)
                    last = nc.tensor.matmul(bank(1), mean_d[:, :], st["sq"][:, k, :], start=(k == 0), stop=(k == KD - 1))
                last.then_inc(mean_ready, 1)
                n["sq"] += KD

            work_of = dict(project=project, down=down, norm=norm_sum, headnorm=headnorm, attention=attention, dsa=dsa,
                           compress=compress, latnorm=latnorm, rpb=rpb, layernorm=layernorm)
            for s, st in enumerate(stages):
                gate(pe, "pe", s)
                if st["kind"] == "rpb":
                    pe.wait_ge(tables_in, tables_before[s] + 32)
                f = work_of.get(st["kind"])
                if f:
                    f(st)
                pe.sem_inc(stage_of["pe"], 1)


        @nc_block.scalar
        def _(act):
            steps = [0]
            n = dict(tile=0, sq=0, mean=0, unit=0, read=0, scaled=0, idx=0, misc_pe=0, misc_act=0, norm=0)

            def step(ins):
                ins.then_inc(act_steps, 1)
                steps[0] += 1

            def settle():
                if steps[0]:
                    act.wait_ge(act_steps, steps[0])

            def project(st):
                if st.get("pads") is not None:
                    pads = st["pads"]
                for b, tiles, a in st["groups"]:
                    for t in tiles:
                        n["tile"] += 1
                        if t.taker != "act":
                            continue
                        act.wait_ge(tile_ready, n["tile"])
                        part, rows, cols = t.out
                        at = (n["tile"] - 1) % PROJ_BANKS * BANK
                        src = psum[part:part + rows, at:at + cols]
                        if t.op == "copy":
                            nc.scalar.activation(t.dst, src, ACT.Copy).then_inc(act_took, 1)
                        elif t.op == "scale":
                            nc.scalar.activation(t.dst, src, ACT.Copy, scale=t.arg).then_inc(act_took, 1)
                        elif t.op == "silu":
                            nc.scalar.activation(t.dst, src, ACT.Silu).then_inc(act_took, 1)
                        elif t.op == "sigmoid":
                            nc.scalar.activation(t.dst, src, ACT.Sigmoid).then_inc(act_took, 1)
                        elif t.op == "sigmoidb":
                            nc.scalar.activation(t.dst, src, ACT.Sigmoid, bias=t.arg).then_inc(act_took, 1)
                        elif t.op == "relu2":
                            step(nc.scalar.activation(t.dst, src, ACT.Relu))
                            settle()
                            nc.scalar.activation(t.dst, t.dst, ACT.Square).then_inc(act_took, 1)
                        n["read"] += 1
                for dst, src in st.get("extra", []):
                    step(nc.scalar.activation(dst, src, ACT.Copy))
                if n["read"]:
                    act.wait_ge(act_took, n["read"])

            def down(st):
                n["tile"] += 2

            def norm(st):
                N = st["n"]
                for k in range(KD):
                    nc.scalar.activation(st["dst"][:, k, 0:N], st["src"][:, k, 0:N], ACT.Square).then_inc(squares_ready, 1)
                n["norm"] += 1
                act.wait_ge(mean_ready, n["norm"])
                nc.scalar.activation(sd[:, 0:N], bank(6, N), ACT.Sqrt, bias=eps).then_inc(sd_ready, 1)
                if st["shift"] is not None:
                    for k in range(KD):
                        act.wait_ge(scaled_ready, n["scaled"] + k + 1)
                        step(nc.scalar.activation(st["dst"][:, k, 0:N], st["dst"][:, k, 0:N], ACT.Identity,
                                                  bias=st["shift"](k)))
                n["scaled"] += KD

            def headnorm(st):
                N, parts, rows = st["n"], st["parts"], st["rows"]
                normed = [t for t in st["tiles"] if t[1] is not None]
                sqb = st["wk"][:, 0:2 * S].rearrange("p (b s) -> p b s", b=2)
                for i, (data, g) in enumerate(normed):
                    if i >= 2:
                        act.wait_ge(square_read, n["sq"] + i - 1)
                    nc.scalar.activation(sqb[0:parts, i % 2, 0:N], data, ACT.Square).then_inc(squares_ready, 1)
                n["sq"] += len(normed)
                act.wait_ge(square_read, n["sq"])
                nc.scalar.activation(st["wk"][0:rows, 2 * S:2 * S + N], bank(0, N)[0:rows], ACT.Sqrt,
                                     bias=eps[0:rows]).then_inc(sd_ready, 1)

            def attention(st):
                units = units_of(st)
                probs, _ = attn_buffers(st)
                base = n["unit"]
                for u, (pi, qt) in enumerate(units):
                    p = st["passes"][pi]
                    a, b, nk = unit_keys(p, qt)
                    act.wait_ge(negmax_ready, base + u + 1)
                    if u >= 2:
                        act.wait_ge(turned, base + u - 1)
                    c = base + u
                    if p["sink"] is not None:
                        step(nc.scalar.activation(small[:, 24 + c % 4:25 + c % 4], p["sink"], ACT.Exp,
                                                  bias=small[:, c % 4:c % 4 + 1]))
                    nc.scalar.activation(probs[u % 2][:, 0:nk], psum[:, (u % 2) * 2 * BANK:(u % 2) * 2 * BANK + nk],
                                         ACT.Exp, bias=small[:, c % 4:c % 4 + 1],
                                         accum_out=small[:, 8 + c % 4:9 + c % 4]).then_inc(exp_done, 1)
                n["unit"] += len(units)
                if any(p["bias"] is not None for p in st["passes"]):
                    pass

            def dsa(st):
                wk = st["wk"]
                for qt in range(1, ST):
                    nk = (qt + 1) * P
                    for h in range(4):
                        act.wait_ge(idx_ready, n["idx"] + 1)
                        if n["idx"] >= 2:
                            act.wait_ge(idx_taken, n["idx"] - 1)
                        i = n["idx"] % 2
                        nc.scalar.activation(wk[:, i * S:i * S + nk], bank(i, nk), ACT.Relu).then_inc(relu_ready, 1)
                        n["idx"] += 1

            def compress(st):
                wk = st["wk"]
                hid = wk[:, 2048:2048 + 4 * NCMP].rearrange("p (v g n) -> p v g n", v=2, g=2)
                for v in range(2):
                    act.wait_ge(misc_pe, 2 * v + 1)
                    nc.scalar.activation(hid[:, v], psum[:, 0:2 * BANK].rearrange("p (g n) -> p g n", g=2)[:, :, 0:NCMP],
                                         ACT.Silu).then_inc(misc_act, 1)
                    act.wait_ge(misc_pe, 2 * v + 2)
                    if v == 0:
                        nc.scalar.activation(KCT[:, 0:NCMP], bank(2, NCMP), ACT.Copy).then_inc(misc_act, 1)
                    else:
                        nc.scalar.activation(VCN[0:NCMP, :], bank(3, P)[0:NCMP], ACT.Copy).then_inc(misc_act, 1)
                act.wait_ge(misc_act, 4)
                n["misc_pe"] += 4

            def latnorm(st):
                sqb = st["wk"][:, 0:3 * S].rearrange("p (b s) -> p b s", b=3)
                for i in range(3):
                    nc.scalar.activation(sqb[:, i, :], CQ[:, i, :] if i < 2 else CKV[:, 0, :],
                                         ACT.Square).then_inc(squares_ready, 1)
                n["norm"] += 1
                act.wait_ge(mean_ready, n["norm"])
                step(nc.scalar.activation(st["wk"][:, 3 * S:4 * S], bank(0), ACT.Sqrt, bias=eps, scale=float(D // 256)))
                nc.scalar.activation(st["wk"][:, 4 * S:5 * S], bank(1), ACT.Sqrt, bias=eps,
                                     scale=float(D // 128)).then_inc(sd_ready, 1)

            def rpb(st):
                for m in range(2):
                    for c in range(8):
                        act.wait_ge(misc_pe, st["pe0"] + m * 8 + c + 1)
                        if m == 1 and c == 0:
                            act.wait_ge(scratch_in, 128)
                        nc.scalar.activation(st["tab"][0:120, 512 * c:512 * c + 512], bank(c % 2)[0:120],
                                             ACT.Copy).then_inc(misc_act, 1)
                    act.wait_ge(misc_act, 4 + 8 * (m + 1))
                    for h in range(8):
                        act.dma_start(rpb_table[8 * m + h].rearrange("c r j -> r c j"),
                                      st["tab"][15 * h:15 * h + 15, :].rearrange("p (c j) -> p c j", c=GRID)
                                      ).then_inc(scratch_in, 16)
                act.wait_ge(scratch_in, 256)

            def layernorm(st):
                for k in range(KD):
                    act.wait_ge(centred, k + 1)
                    nc.scalar.activation(st["sq"][:, k, :], st["src"][:, k, :], ACT.Square).then_inc(squares_ready, 1)
                n["norm"] += 1
                act.wait_ge(mean_ready, n["norm"])
                nc.scalar.activation(sd[:, :], bank(1), ACT.Sqrt, bias=eps).then_inc(sd_ready, 1)
                for k in range(KD):
                    act.wait_ge(scaled_ready, n["scaled"] + k + 1)
                    step(nc.scalar.activation(st["dst"][:, k, :], st["dst"][:, k, :], ACT.Silu,
                                              bias=V("cv_lnb")[:, k:k + 1], scale=V("cv_lng")[:, k:k + 1]))
                n["scaled"] += KD

            work_of = dict(project=project, down=down, norm=norm, headnorm=headnorm, attention=attention, dsa=dsa,
                           compress=compress, latnorm=latnorm, rpb=rpb, layernorm=layernorm)
            act.wait_ge(inputs_in, 16 * 7)
            for v, name in enumerate(("c", "c_ctx")):
                step(nc.scalar.activation(cond[:, :, v], V(name), ACT.Silu))
            step(nc.scalar.activation(identb[:, :], ident[:, :], ACT.Copy))
            step(nc.scalar.activation(diagm[:, :], arena[:, 0:P], ACT.Copy))
            step(nc.scalar.activation(prevm[:, :], arena[:, P:2 * P], ACT.Copy))
            settle()
            act.sem_inc(inputs_in, 32)
            for s, st in enumerate(stages):
                gate(act, "act", s)
                if st["kind"] == "rpb":
                    act.dma_start(st["sel"][0:32, :], dram["na_select"]).then_inc(tables_in, 16)
                    act.dma_start(st["rpb"][0:32, :], dram["na_rpb"]).then_inc(tables_in, 16)
                for dst, src in st["loads"]:
                    act.dma_start(dst, src).then_inc(tables_in, 16)
                f = work_of.get(st["kind"])
                if f:
                    f(st)
                settle()
                act.sem_inc(stage_of["act"], 1)

        @nc_block.vector
        def _(dve):
            steps = [0]
            n = dict(tile=0, took=0, ada=0, unit=0, pair=0, spread=0, swap=0, cos=0, sd=0, idx=0, scaled=0, rope=0, yn=0)

            def step(ins):
                ins.then_inc(dve_steps, 1)
                steps[0] += 1

            def settle():
                dve.wait_ge(dve_steps, steps[0])

            def chain(ins):
                step(ins)
                settle()

            def ada(a):
                b, layer, j = a
                dve.wait_ge(ada_ready, n["ada"] + 1)
                bias = V(f"ada_b{layer}")[:, 4 * j:4 * j + 4].unsqueeze(2).to_broadcast([P, 4, 2])
                nc.vector.tensor_tensor(mods[:, layer % 2, 4 * j:4 * j + 4, :],
                                        bank(7)[:, 0:8].rearrange("p (m v) -> p m v", v=2), bias,
                                        ALU.add).then_inc(ada_taken, 1)
                n["ada"] += 1

            def project(st):
                if st.get("pads") is not None:
                    U = st["pads"]
                    step(nc.vector.memset(U[:, :, 0:TAPS // 2], 0.0))
                    step(nc.vector.memset(U[:, :, TAPS // 2 + S:], 0.0))
                for b, tiles, a in st["groups"]:
                    for t in tiles:
                        n["tile"] += 1
                        if t.taker != "dve":
                            continue
                        dve.wait_ge(tile_ready, n["tile"])
                        part, rows, cols = t.out
                        at = (n["tile"] - 1) % PROJ_BANKS * BANK
                        src = psum[part:part + rows, at:at + cols]
                        if t.op == "copy":
                            nc.vector.tensor_copy(t.dst, src).then_inc(dve_took, 1)
                        elif t.op == "scale":
                            nc.vector.tensor_scalar(t.dst, src, t.arg, None, ALU.mult).then_inc(dve_took, 1)
                        elif t.op == "resid" and t.arg is None:
                            nc.vector.tensor_tensor(t.dst, src, t.dst, ALU.add).then_inc(dve_took, 1)
                        elif t.op == "resid":
                            nc.vector.scalar_tensor_tensor(t.dst, src, t.arg, t.dst, ALU.mult,
                                                           ALU.add).then_inc(dve_took, 1)
                        elif t.op == "glu":
                            nc.vector.scalar_tensor_tensor(t.dst, src, t.arg[0], t.arg[1], ALU.add,
                                                           ALU.mult).then_inc(dve_took, 1)
                        elif t.op == "residb":
                            chain(nc.vector.tensor_scalar(t.arg[2], src, t.arg[0], t.arg[1], ALU.add, ALU.mult))
                            nc.vector.tensor_tensor(t.dst, t.arg[2], t.dst, ALU.add).then_inc(dve_took, 1)
                            dve.wait_ge(dve_took, n["took"] + 1)
                        n["took"] += 1
                    if a:
                        ada(a)
                if n["took"]:
                    dve.wait_ge(dve_took, n["took"])
                if n["ada"]:
                    dve.wait_ge(ada_taken, n["ada"])

            def down(st):
                for half, kb, b, a in st["groups"]:
                    if kb == 3:
                        n["tile"] += 1
                        dve.wait_ge(tile_ready, n["tile"])
                        for m in range(4):
                            o = 4 * half + m
                            step(nc.vector.scalar_tensor_tensor(X[:, o, :], bank(m), st["gate"](o), X[:, o, :], ALU.mult,
                                                                ALU.add))
                            if st["hidc"] is not None:
                                step(nc.vector.scalar_tensor_tensor(CX[:, o, :], bank(4 + m // 2, C, C * (m % 2)),
                                                                    st["gatec"](o), CX[:, o, :], ALU.mult, ALU.add))
                        settle()
                        dve.sem_inc(dve_took, 1)
                        n["took"] += 1
                    if a:
                        ada(a)
                if n["ada"]:
                    dve.wait_ge(ada_taken, n["ada"])

            def norm(st):
                N = st["n"]
                dve.wait_ge(sd_ready, n["sd"] + 1)
                chain(nc.vector.reciprocal(rstd[:, 0:N], sd[:, 0:N]))
                for k in range(KD):
                    nc.vector.scalar_tensor_tensor(st["dst"][:, k, 0:N], st["src"][:, k, 0:N], st["gain"](k),
                                                   rstd[:, 0:N], ALU.mult, ALU.mult).then_inc(scaled_ready, 1)
                n["sd"] += 1
                n["scaled"] += KD
                dve.wait_ge(scaled_ready, n["scaled"])

            def headnorm(st):
                N, parts, rows, wk = st["n"], st["parts"], st["rows"], st["wk"]
                ynb = wk[0:parts, 4 * S:6 * S].rearrange("p (b s) -> p b s", b=2)
                t1b = wk[0:parts, 6 * S:8 * S].rearrange("p (b s) -> p b s", b=2)
                t2b = wk[0:parts, 8 * S:10 * S].rearrange("p (b s) -> p b s", b=2)
                dve.wait_ge(sd_ready, n["sd"] + 1)
                nc.vector.reciprocal(wk[0:rows, 3 * S:3 * S + N], wk[0:rows, 2 * S:2 * S + N]).then_inc(sd_ready, 1)
                n["sd"] += 2
                T = len(st["tiles"])
                rope = st["swap"] is not None

                def scale(i):
                    data, g = st["tiles"][i]
                    if g is None:
                        return
                    dve.wait_ge(spread_ready, n["spread"] + 1)
                    if rope and i >= 2:
                        dve.wait_ge(rope_done, n["rope"] + i - 1)
                    out = ynb[:, i % 2, 0:N] if rope else data
                    nc.vector.scalar_tensor_tensor(out, data, g[0:parts], bank(1 + i % 2, N)[0:parts], ALU.mult,
                                                   ALU.mult).then_inc(yn_ready, 1)
                    n["spread"] += 1

                def rotate(i):
                    data, g = st["tiles"][i]
                    dve.wait_ge(swap_ready, n["swap"] + 1)
                    if i >= 2:
                        dve.wait_ge(rope_done, n["rope"] + i - 1)
                    step(nc.vector.tensor_tensor(t2b[:, i % 2, 0:N], bank(3 + i % 2, N)[0:parts], st["sin"][0:parts, 0:N],
                                                 ALU.mult))
                    settle()
                    dve.wait_ge(cos_ready, n["cos"] + 1)
                    nc.vector.tensor_tensor(data, t1b[:, i % 2, 0:N], t2b[:, i % 2, 0:N], ALU.add).then_inc(rope_done, 1)
                    n["swap"] += 1
                    n["cos"] += 1

                for i in range(T + 1):
                    if i < T:
                        scale(i)
                    if rope and i >= 1:
                        rotate(i - 1)
                n["yn"] = n["spread"]
                if rope:
                    n["rope"] += T
                    dve.wait_ge(rope_done, n["rope"])
                dve.wait_ge(yn_ready, n["yn"])

            def attention(st):
                units = units_of(st)
                probs, turned_b = attn_buffers(st)
                base, pair0 = n["unit"], n["pair"]
                pairs = [0]

                def negmax(u):
                    pi, qt = units[u]
                    p = st["passes"][pi]
                    a, b, nk = unit_keys(p, qt)
                    c = (base + u) % 4
                    s0 = (u % 2) * 2 * BANK
                    dve.wait_ge(scores_ready, base + u + 1)
                    if p["bias"] is not None:
                        h = pi
                        if qt == 0:
                            dve.wait_ge(bias_in[h % 2], 32 * (h // 2 + 1))
                        chain(nc.vector.tensor_tensor(psum[:, s0:s0 + S], psum[:, s0:s0 + S], p["bias"](qt), ALU.add))
                        if qt == p["qts"] - 1:
                            dve.sem_inc(bias_used, 1)
                    if p["sink"] is None and not p["clamp"]:
                        nc.vector.tensor_reduce(small[:, c:c + 1], psum[:, s0:s0 + nk], AX, ALU.max,
                                                negate=True).then_inc(negmax_ready, 1)
                        return
                    chain(nc.vector.tensor_reduce(small[:, 32 + c:33 + c], psum[:, s0:s0 + nk], AX, ALU.max))
                    other = p["sink"] if p["sink"] is not None else -1e29
                    nc.vector.tensor_scalar(small[:, c:c + 1], small[:, 32 + c:33 + c], other, -1.0, ALU.max,
                                            ALU.mult).then_inc(negmax_ready, 1)

                def scale(u):
                    pi, qt = units[u]
                    p = st["passes"][pi]
                    a, b, nk = unit_keys(p, qt)
                    c = (base + u) % 4
                    dve.wait_ge(exp_done, base + u + 1)
                    total = small[:, 8 + c:9 + c]
                    if p["sink"] is not None:
                        chain(nc.vector.tensor_tensor(small[:, 16 + c:17 + c], total, small[:, 24 + c:25 + c], ALU.add))
                        total = small[:, 16 + c:17 + c]
                    elif p["clamp"]:
                        chain(nc.vector.tensor_scalar(small[:, 16 + c:17 + c], total, 1e-30, None, ALU.max))
                        total = small[:, 16 + c:17 + c]
                    chain(nc.vector.reciprocal(small[:, 20 + c:21 + c], total))
                    by = small[:, 20 + c:21 + c]
                    if p["gate"] is not None:
                        nc.vector.tensor_scalar(probs[u % 2][:, 0:nk], probs[u % 2][:, 0:nk], by, p["gate"](qt), ALU.mult,
                                                ALU.mult).then_inc(probs_ready, 1)
                    else:
                        nc.vector.tensor_scalar(probs[u % 2][:, 0:nk], probs[u % 2][:, 0:nk], by, None,
                                                ALU.mult).then_inc(probs_ready, 1)

                def copy(u):
                    pi, qt = units[u]
                    p = st["passes"][pi]
                    a, b, nk = unit_keys(p, qt)
                    rows = min(P, p["krows"])
                    dve.wait_ge(turned, base + u + 1)
                    if qt == 0 and pi >= 2:
                        dve.wait_ge(pv_done, pv0 + pi - 1)
                    src = psum[0:rows, 4 * BANK:4 * BANK + (b - a) * P].rearrange("p (t s) -> p t s", s=P)
                    nc.vector.tensor_copy(turned_b[pi % 2][0:rows, a:b, qt * P:qt * P + P], src).then_inc(turned_copied, 1)

                def take(pi):
                    p = st["passes"][pi]
                    if not p["last"]:
                        return
                    dve.wait_ge(pv_done, pv0 + pi + 1)
                    N = p["qts"] * P
                    src = bank(6 + pairs[0] % 2, N)
                    if p["z"] is not None:
                        nc.vector.tensor_tensor(p["dst"][:, 0:N], src, p["z"][:, 0:N], ALU.mult).then_inc(o_taken, 1)
                    else:
                        nc.vector.tensor_copy(p["dst"][:, 0:N], src).then_inc(o_taken, 1)
                    pairs[0] += 1

                pv0 = n.get("pv", 0)
                U = len(units)
                for u in range(U + 5):
                    if u < U:
                        negmax(u)
                    if 1 <= u < U + 1:
                        scale(u - 1)
                    if 2 <= u < U + 2:
                        copy(u - 2)
                    if u >= 5:
                        pi, qt = units[u - 5]
                        if qt == st["passes"][pi]["qts"] - 1:
                            take(pi)
                n["pv"] = pv0 + len(st["passes"])
                n["unit"] += U
                n["pair"] += pairs[0]
                dve.wait_ge(o_taken, n["pair"])

            def dsa(st):
                wk = st["wk"]
                acc = [wk[:, 2 * S:3 * S], wk[:, 3 * S:4 * S]]
                best = small[:, 40:48]
                for qt in range(1, ST):
                    nk = (qt + 1) * P
                    for h in range(4):
                        i = n["idx"] % 2
                        dve.wait_ge(relu_ready, n["idx"] + 1)
                        w = WI[:, qt, h:h + 1]
                        if h == 0:
                            ins = nc.vector.tensor_scalar(acc[0][:, 0:nk], wk[:, 0 + i * S:i * S + nk], w, None, ALU.mult)
                        else:
                            ins = nc.vector.scalar_tensor_tensor(acc[h % 2][:, 0:nk], wk[:, i * S:i * S + nk], w,
                                                                 acc[1 - h % 2][:, 0:nk], ALU.mult, ALU.add)
                        ins.then_inc(idx_taken, 1)
                        n["idx"] += 1
                        dve.wait_ge(idx_taken, n["idx"])
                    chain(nc.vector.tensor_tensor(acc[1][:, qt * P:nk], acc[1][:, qt * P:nk], diagm[:, :], ALU.add))
                    for r in range(TOPK // 8):
                        chain(nc.vector.max(best, acc[1][:, 0:nk]))
                        chain(nc.vector.match_replace(acc[1][:, 0:nk], best, acc[1][:, 0:nk], -3e38))
                    chain(nc.vector.tensor_scalar(dsa_mask[:, qt - 1, 0:nk], acc[1][:, 0:nk], -2e38, NEG, ALU.is_ge,
                                                  ALU.mult))

            def compress(st):
                wk = st["wk"]
                F = wk[:, 0:2 * CMP_LEN * NCMP].rearrange("p (v l n) -> p v l n", v=2, l=CMP_LEN)
                for v, (src, pe_) in enumerate(((KC, "pe_k"), (VC, "pe_v"))):
                    for half in range(2):
                        win = src[:, 0, 16 * half:16 * half + 16 * NCMP].rearrange("p (n l) -> p l n", l=16)
                        add = V(pe_)[:, 16 * half:16 * half + 16].unsqueeze(2).to_broadcast([P, 16, NCMP])
                        ins = nc.vector.tensor_tensor(F[:, v, 16 * half:16 * half + 16, :], win, add, ALU.add)
                        if half:
                            ins.then_inc(misc_dve, 1)
                        else:
                            step(ins)
                step(nc.vector.tensor_copy(cmpmb[:, :, 0:NCMP], cmpm[:, :, :]))
                dve.wait_ge(misc_dve, 2)

            def latnorm(st):
                wk = st["wk"]
                dve.wait_ge(sd_ready, n["sd"] + 1)
                chain(nc.vector.reciprocal(wk[:, 5 * S:7 * S], wk[:, 3 * S:5 * S]))
                for i in range(2):
                    step(nc.vector.scalar_tensor_tensor(CQ[:, i, :], CQ[:, i, :], V("qlat_g")[:, i:i + 1],
                                                        wk[:, 5 * S:6 * S], ALU.mult, ALU.mult))
                step(nc.vector.scalar_tensor_tensor(CKV[:, 0, :], CKV[:, 0, :], V("kvlat_g"), wk[:, 6 * S:7 * S],
                                                    ALU.mult, ALU.mult))
                n["sd"] += 1

            def prep(st):
                L = st["layer"]
                for half, name in ((0, f"norm1_{L}"), (1, f"norm2_{L}")):
                    for v in range(2):
                        step(nc.vector.scalar_tensor_tensor(
                            sgain[:, half, v, :], mods[:, L % 2, (3 * half + 1) * KD:(3 * half + 2) * KD, v], 1.0, V(name),
                            ALU.add, ALU.mult))

            def conv(st):
                U, CV = st["U"], st["CV"]
                for tap in range(TAPS):
                    for k in range(KD):
                        w = V("cv_w")[:, k * TAPS + tap:k * TAPS + tap + 1]
                        if tap == 0:
                            step(nc.vector.tensor_scalar(CV[:, k, :], U[:, k, 0:S], w, V("cv_bd")[:, k:k + 1], ALU.mult,
                                                         ALU.add))
                        else:
                            dve.wait_ge(dve_steps, steps[0] - KD + 1)
                            step(nc.vector.scalar_tensor_tensor(CV[:, k, :], U[:, k, tap:tap + S], w, CV[:, k, :],
                                                                ALU.mult, ALU.add))

            def layernorm(st):
                dve.wait_ge(misc_pe, st["pe0"] + 1)
                for k in range(KD):
                    nc.vector.tensor_tensor(st["src"][:, k, :], st["src"][:, k, :], bank(0), ALU.subtract).then_inc(centred, 1)
                dve.wait_ge(centred, KD)
                dve.wait_ge(sd_ready, n["sd"] + 1)
                chain(nc.vector.reciprocal(rstd[:, :], sd[:, :]))
                for k in range(KD):
                    nc.vector.tensor_tensor(st["dst"][:, k, :], st["src"][:, k, :], rstd[:, :],
                                            ALU.mult).then_inc(scaled_ready, 1)
                n["sd"] += 1
                n["scaled"] += KD
                dve.wait_ge(scaled_ready, n["scaled"])

            work_of = dict(project=project, down=down, norm=norm, headnorm=headnorm, attention=attention, dsa=dsa,
                           compress=compress, latnorm=latnorm, prep=prep, conv=conv, layernorm=layernorm)
            step(nc.vector.memset(mean_d[:, :], 1.0 / D))
            step(nc.vector.memset(small[:, :], 0.0))
            step(nc.vector.memset(eps, EPS))
            dve.wait_ge(inputs_in, 16 * 7)
            for name, by in (("qa_g", 0.125), ("qb_g", 0.125), ("qc_g", 0.125), ("at_q_g", 0.125),
                             ("qd_g", float(MLA_W) ** -0.5)):
                step(nc.vector.tensor_scalar(V(name), V(name), by, None, ALU.mult))
            settle()
            dve.sem_inc(inputs_in, 32)
            for s, st in enumerate(stages):
                gate(dve, "dve", s)
                f = work_of.get(st["kind"])
                if f:
                    f(st)
                settle()
                dve.sem_inc(stage_of["dve"], 1)

        @nc_block.gpsimd
        def _(pool):
            n = dict(yn=0, rope=0, swap=0)
            for s, st in enumerate(stages):
                gate(pool, "pool", s)
                if st["kind"] == "headnorm":
                    N, parts, wk = st["n"], st["parts"], st["wk"]
                    ynb = wk[0:parts, 4 * S:6 * S].rearrange("p (b s) -> p b s", b=2)
                    t1b = wk[0:parts, 6 * S:8 * S].rearrange("p (b s) -> p b s", b=2)
                    for i, (data, g) in enumerate(st["tiles"]):
                        if st["swap"] is None:
                            n["yn"] += 1
                            continue
                        if g is not None:
                            n["yn"] += 1
                            pool.wait_ge(yn_ready, n["yn"])
                            src = ynb[:, i % 2, 0:N]
                        else:
                            src = data
                        if i >= 2:
                            pool.wait_ge(rope_done, n["rope"] + i - 1)
                        nc.gpsimd.tensor_tensor(t1b[:, i % 2, 0:N], src, st["cos"][0:parts, 0:N],
                                                ALU.mult).then_inc(cos_ready, 1)
                        n["swap"] += 1
                    if st["swap"] is not None:
                        n["rope"] += len(st["tiles"])
                        pool.wait_ge(cos_ready, n["swap"])
                if st["kind"] == "attention" and st["passes"][0]["bias"] is not None:
                    for h in range(16):
                        if h >= 2:
                            pool.wait_ge(bias_used, h - 1)
                        flat = rpb_table[h].rearrange("c r j -> c (r j)")
                        pool.dma_start(bias_buf[0:GRID, h % 2, 0:15 * GRID], flat).then_inc(bias_in[h % 2], 16)
                        pool.dma_start(bias_buf[GRID:2 * GRID, h % 2, GRID:16 * GRID], flat).then_inc(bias_in[h % 2], 16)
                pool.sem_inc(stage_of["pool"], 1)
            for name, sm in stage_of.items():
                pool.wait_ge(sm, len(stages))
            if n_tab:
                pool.wait_ge(tables_in, n_tab)
            pool.dma_start(out_dram.rearrange("k p s -> p k s"), H[:, :, :]).then_inc(out_done, 16)
            pool.wait_ge(out_done, 16)


AB_SPLITS = (512, 128, 128, 256, 64, 4, 512, 512, 128, 128, 512)
CD_SPLITS = (512, 128, 128, 128, 128, 128, 128, 24, 512, 256, 128, 32, 512)


def pair_order(heads, width=HD):
    return np.concatenate([np.arange(h * width, (h + 1) * width) for h in heads])


def laid_out(i):
    grouped = [h for t in range(4) for h in (t, t + 4)]
    at_heads = [h for t in range(4) for h in (t, t + 4)] + [h for t in range(4) for h in (8 + t, 12 + t)]
    half, full = pair_order(grouped), pair_order(at_heads)
    qa, ka, va, qi, ki, wi, za, qb, kb, vb, zb = np.split(i["ab_w_in"][0], np.cumsum(AB_SPLITS)[:-1], axis=1)
    qc, kc, vc, ks, vs, kw, vw, gc, zc, cq, ckv, kr, zd = np.split(i["cd_w_in"][0], np.cumsum(CD_SPLITS)[:-1], axis=1)
    ukv = i["d_w_ukv"][0].reshape(128, 8, 2, 64)
    out = {
        "x": i["x"][0].T.reshape(KD, P, S), "ctx": i["ctx_2"][0].T.reshape(KD, P, C),
        "sinks": np.tile(i["b_sinks"][0][None, :], (P, 1)),
        "ab_in": np.concatenate([qa[:, half], ka, qi, ki, ki, qb[:, half], kb, za[:, half], zb[:, half], va, vb, wi], 1),
        "ab_out": np.concatenate([i["ab_w_out"][0][:512][half], i["ab_w_out"][0][512:][half]]),
        "cd_in": np.concatenate([qc[:, half], kc, vc, ks, kw, cq, ckv, zc[:, half], zd, kr, gc, vs, vw], 1),
        "cd_out": np.concatenate([i["cd_w_out"][0][:512][half], i["cd_w_out"][0][512:]]),
        "cmp_w1": i["c_cmp_w1"][0], "cmp_w2": i["c_cmp_w2"][0], "uq": i["d_w_uq"][0],
        "ukv": np.concatenate([ukv[:, :, 0].reshape(128, 512), ukv[:, :, 1].reshape(128, 512)], 1),
        "ada_w": i["ada_w_2"], "mlp_w1": i["mlp_w1_2"], "mlp_w2": i["mlp_w2_2"],
        "at_qkv": np.concatenate([i["at_w_qkv_2"][0][:, :1024][:, full], i["at_w_qkv_2"][0][:, 1024:]], 1),
        "at_o": i["at_w_o_2"][0][full], "na_qkv": i["na_w_qkv_2"][0], "na_o": i["na_w_o_2"][0],
        "pw1": i["cv_w_pw1_2"][0], "pw2": i["cv_w_pw2_2"][0], "ft_w": i["ft_w_2"][0],
    }
    rpb = np.ones((32, 16 * 15), np.float32)
    rpb[:31] = i["na_rpb_2"][0].reshape(240, 31).T
    out["na_rpb"] = rpb

    def cols(a):
        return np.asarray(a).reshape(-1, P).T

    def twice(a):
        return np.concatenate([a, a])[:, None]

    def heads96(a, b):
        return np.concatenate([a, b, np.zeros(32, np.float32)])[:, None]

    pe = i["c_cmp_pe"][0]
    v = {
        "ab_norm": cols(i["ab_norm"][0]), "cd_norm": cols(i["cd_norm"][0]), "qa_g": twice(i["a_qk_norm"][0, 0]),
        "ka_g": twice(i["a_qk_norm"][0, 1]), "ki_g": twice(i["a_kidx_norm"][0]), "qb_g": twice(i["b_qk_norm"][0, 0]),
        "kb_g": twice(i["b_qk_norm"][0, 1]), "qc_g": twice(i["c_q_norm"][0]), "kc_g": twice(i["c_k_norm"][0, 0]),
        "ks_g": twice(i["c_k_norm"][0, 1]), "kw_g": twice(i["c_k_norm"][0, 2]),
        "pe_k": np.concatenate([pe[0].T, pe[0].T]), "pe_v": np.concatenate([pe[1].T, pe[1].T]),
        "qlat_g": cols(i["d_q_lat_norm"][0]), "kvlat_g": cols(i["d_kv_lat_norm"][0]),
        "qd_g": heads96(i["d_nope_norm"][0, 0], i["d_rope_norm"][0, 0]),
        "kd_g": heads96(i["d_nope_norm"][0, 1], i["d_rope_norm"][0, 1]),
        "c": cols(i["c_2"][0]), "c_ctx": cols(i["c_ctx_2"]), "final_g": cols(i["final_g_2"]),
        "at_q_g": twice(i["at_q_g_2"][0]), "at_k_g": twice(i["at_k_g_2"][0]), "cv_b1": cols(i["cv_b_pw1_2"][0]),
        "cv_w": i["cv_w_dw_2"][0].T.reshape(KD, P, TAPS).transpose(1, 0, 2).reshape(P, KD * TAPS),
        "cv_bd": cols(i["cv_b_dw_2"][0]), "cv_lng": cols(i["cv_ln_g_2"][0]), "cv_lnb": cols(i["cv_ln_b_2"][0]),
        "cv_b2": cols(i["cv_b_pw2_2"][0]), "ft_b": cols(i["ft_b_2"][0]),
    }
    for n in range(4):
        v[f"norm1_{n}"], v[f"norm2_{n}"] = cols(i["norm1_g_2"][n]), cols(i["norm2_g_2"][n])
        v[f"ada_b{n}"] = cols(i["ada_b_2"][n])
    out["vectors"] = np.concatenate([v[n] for n, _ in VECTORS], 1)
    for n, shape in IN_SHAPES.items():
        assert out[n].shape == shape, (n, out[n].shape)
    out.update(constants())
    return {n: np.ascontiguousarray(a) for n, a in out.items()}


def kernel(**inputs):
    import concourse.bacc as bacc
    from concourse.bass_utils import run_bass_kernel_spmd

    arrays = laid_out({n: np.asarray(a) for n, a in inputs.items()})
    nc = bacc.Bacc("TRN2", target_bir_lowering=False, num_devices=1)
    dram = {n: nc.dram_tensor(f"in_{n}", a.shape, mybir.dt.from_np(a.dtype), kind="ExternalInput").ap()
            for n, a in arrays.items()}
    out = nc.dram_tensor("out_x", (KD, P, S), F32, kind="ExternalOutput").ap()
    build_program(nc, dram, out)
    r = run_bass_kernel_spmd(nc, [{f"in_{n}": a for n, a in arrays.items()}], core_ids=[0])
    return np.ascontiguousarray(r.results[0]["out_x"].reshape(D, S).T)[None]
```

```python
from contextlib import ExitStack

import numpy as np

import concourse.bass as bass
from concourse import mybir

F32 = mybir.dt.float32
BF16 = mybir.dt.bfloat16
ALU = mybir.AluOpType
ACT = mybir.ActivationFunctionType
AX = mybir.AxisListType.X

P = 128
D = 1024
KD = D // P
S = 512
C = 256
ST = S // P
HD = 64
FF = 4 * D
EPS = 1e-6
NEG = -1e30
RING = 3
SLOT = 4096
BANK = 512
PROJ_BANKS = 6
TOPK = S // 4
CMP_STRIDE, CMP_LEN, CMP_HID = 16, 32, 128
CMP_HALF = CMP_LEN // 2
NCMP = S // CMP_STRIDE - 1
GRID = 64
ROWS = S // GRID
WIN = 16
TAPS = 31
Q_BUFS = 4
CHUNK = 256
CONV_PE = 3
GW = 256
PAIR_TILES, PAIR_ROWS = 11, 22
MLA_TILES, MLA_ROWS = 8, 16
MLA_W = 96


def rope_cos_sin(pos, dim):
    inv = np.power(np.float32(10000.0), -np.arange(0, dim, 2, dtype=np.float32) / np.float32(dim))
    ang = (pos.astype(np.float32)[:, None] * inv[None, :]).astype(np.float32)
    return np.cos(ang).T, np.sin(ang).T


def half_tables(pos, dim):
    c, s = rope_cos_sin(pos, dim)
    return np.concatenate([c, c]), np.concatenate([-s, s])


def swap_matrix(dim, half):
    m = np.zeros((dim, dim), np.float32)
    for f in range(dim):
        m[(f + half) % dim, f] = 1.0
    return m


def block_diag(*ms):
    n = sum(m.shape[0] for m in ms)
    out, at = np.zeros((n, n), np.float32), 0
    for m in ms:
        out[at:at + len(m), at:at + len(m)] = m
        at += len(m)
    return out


def pad_rows(a):
    out = np.zeros((P,) + a.shape[1:], np.float32)
    out[:len(a)] = a
    return out


def head_norm_constants(tiles, rows, segments):
    mean = np.zeros((P, tiles, rows), np.float32)
    spread = np.zeros((P, tiles, P), np.float32)
    for i in range(tiles):
        for j, (a, b) in enumerate(segments):
            mean[a:b, i, 2 * i + j] = 1.0 / (b - a)
            spread[2 * i + j, i, a:b] = 1.0
    return np.concatenate([mean.reshape(P, -1), spread.reshape(P, -1)], 1)


def constants():
    pos = np.arange(S)
    out = {}
    k, q = np.arange(P)[None, :], np.arange(P)[:, None]
    out["ident"] = np.eye(P, dtype=np.float32)
    out["diag_mask"] = np.where(k <= q, 0.0, NEG)
    out["prev_mask"] = np.where(k > q, 0.0, NEG)
    t = np.arange(S)[:, None]
    cmp_end = np.arange(NCMP)[None, :] * CMP_STRIDE + CMP_LEN - 1
    out["cmp_mask"] = np.where(cmp_end <= t, 0.0, NEG).reshape(ST, P, NCMP).transpose(1, 0, 2)
    c, s = half_tables(pos, HD)
    out["rope_ab"] = np.concatenate([np.concatenate([c, c]), np.concatenate([s, s]),
                                     block_diag(swap_matrix(64, 32), swap_matrix(64, 32))], 1)
    cc, cs = half_tables(np.arange(NCMP) * CMP_STRIDE + CMP_LEN - 1, HD)
    out["rope_cmp"] = np.concatenate([np.concatenate([cc, cc]), np.concatenate([cs, cs])], 1)
    rc, rs = half_tables(pos, 32)
    out["rope_mla"] = np.concatenate([
        pad_rows(np.concatenate([np.ones((64, S)), rc])), pad_rows(np.concatenate([np.zeros((64, S)), rs])),
        block_diag(np.zeros((64, 64)), swap_matrix(32, 16), np.zeros((32, 32)))], 1)
    row, col = (pos // GRID).astype(np.float32), (pos % GRID).astype(np.float32)
    inv = np.power(np.float32(10000.0), -np.arange(16, dtype=np.float32) / np.float32(16))
    ang = np.concatenate([row[:, None] * inv, col[:, None] * inv], -1).astype(np.float32).T
    ca, sa = np.repeat(np.cos(ang), 2, 0), np.repeat(np.sin(ang), 2, 0)
    sa[0::2] *= -1.0
    pairs = np.zeros((P, P), np.float32)
    for f in range(P):
        pairs[f ^ 1, f] = 1.0
    out["rope_at"] = np.concatenate([np.concatenate([ca, ca]), np.concatenate([sa, sa]), pairs], 1)
    out["hn_pair"] = head_norm_constants(PAIR_TILES, PAIR_ROWS, [(0, 64), (64, 128)])
    out["hn_mla"] = head_norm_constants(MLA_TILES, MLA_ROWS, [(0, 64), (64, 96)])
    cq, jk = np.arange(GRID)[:, None], np.arange(GRID)[None, :]
    start = np.clip(cq - WIN // 2, 0, GRID - WIN)
    inside = (jk >= start) & (jk < start + WIN)
    sel = np.zeros((32, GRID, GRID), np.float32)
    for u in range(2 * WIN - 1):
        sel[u] = inside & (jk - cq + WIN - 1 == u)
    sel[31] = np.where(inside, 0.0, NEG)
    out["na_select"] = sel.reshape(32, GRID * GRID)
    dd = np.outer(np.arange(GW), np.arange(GW)) % GW
    ss = np.outer(np.arange(S), np.arange(S)) % S
    scale = 1.0 / np.sqrt(np.float64(GW * S))
    out["dft_group"] = np.concatenate([np.cos(2 * np.pi * dd / GW) * scale, np.sin(2 * np.pi * dd / GW) * scale], 1)
    out["dft_seq"] = np.concatenate([np.cos(2 * np.pi * ss / S), -np.sin(2 * np.pi * ss / S)], 1)
    return {n: np.ascontiguousarray(a, dtype=np.float32) for n, a in out.items()}


VECTORS = [("ab_norm", KD), ("cd_norm", KD), ("qa_g", 1), ("ka_g", 1), ("ki_g", 1), ("qb_g", 1), ("kb_g", 1),
           ("qc_g", 1), ("kc_g", 1), ("ks_g", 1), ("kw_g", 1), ("pe_k", CMP_LEN), ("pe_v", CMP_LEN),
           ("qlat_g", 2), ("kvlat_g", 1), ("qd_g", 1), ("kd_g", 1), ("c", KD), ("c_ctx", KD), ("final_g", KD),
           ("at_q_g", 1), ("at_k_g", 1), ("cv_b1", 2 * KD), ("cv_w", KD * TAPS), ("cv_bd", KD), ("cv_lng", KD),
           ("cv_lnb", KD), ("cv_b2", KD), ("ft_b", KD)]
for _i in range(4):
    VECTORS += [(f"norm1_{_i}", KD), (f"norm2_{_i}", KD), (f"ada_b{_i}", 6 * KD)]
VCOL = {}
NVEC = 0
for _n, _w in VECTORS:
    VCOL[_n] = (NVEC, _w)
    NVEC += _w

IDX_COLS = 3 * P + 4
CONV_BANK = 8 - CONV_PE
SINKS = 4
IN_SHAPES = {
    "x": (KD, P, S), "ctx": (KD, P, C), "vectors": (P, NVEC), "sinks": (P, SINKS),
    "ab_in": (D, 2948), "ab_out": (D, D), "cd_in": (D, 2744), "cd_out": (D, D),
    "cmp_w1": (2, CMP_LEN * HD, CMP_HID), "cmp_w2": (2, CMP_HID, HD), "uq": (256, 768), "ukv": (128, 1024),
    "ada_w": (4, D, 6 * D), "mlp_w1": (4, D, FF), "mlp_w2": (4, FF, D), "at_qkv": (D, 1536), "at_o": (D, D),
    "na_qkv": (D, 3 * D), "na_rpb": (32, 16 * 15), "na_o": (D, D), "pw1": (D, 2 * D), "pw2": (D, D), "ft_w": (D, D),
}


class Tile:

    def __init__(self, pairs, out, taker, op, dst, arg=None, tile=None, first=0):
        self.first = first
        self.tile = tile
        self.pairs, self.out, self.taker, self.op, self.dst, self.arg = pairs, out, taker, op, dst, arg


def build_program(nc, dram, out_dram, stages_kept=10000):
    ctx = ExitStack()
    with ctx:
        def sb(name, shape, dt=F32):
            return ctx.enter_context(nc.sbuf_tensor(name, shape, dt))

        def sem(name):
            return ctx.enter_context(nc.semaphore(name))

        ARENA = 24960
        X = sb("X", [P, KD, S])
        H = sb("H", [P, KD, S])
        CX = sb("CX", [P, KD, C])
        CH = sb("CH", [P, KD, C])
        ring = sb("ring", [P, RING, SLOT])
        arena = sb("arena", [P, ARENA + 2 * BANK])
        partial = arena[:, ARENA:ARENA + 2 * BANK].rearrange("p (v n) -> p v n", v=2)
        ident = sb("ident", [P, P])
        identb = sb("identb", [P, P], BF16)
        half_select = sb("half_select", [P, 2, P], BF16)
        mean_d = sb("mean_d", [P, P])
        diagm = sb("diagm", [P, P], BF16)
        prevm = sb("prevm", [P, P], BF16)
        vec = sb("vec", [P, NVEC])
        mods = sb("mods", [P, 2, 6 * KD, 2])
        sgain = sb("sgain", [P, 2, 2, KD])
        cond = sb("cond", [P, KD, 2])
        sinks = sb("sinks", [P, SINKS])
        small = sb("small", [P, 64])
        ones = sb("ones", [P, 1])
        unused = sb("unused", [P, 1])
        sd = sb("sd", [P, S])
        rstd = sb("rstd", [P, S])
        eps = sb("eps", [P, 1])[:, :]
        q_diagonal = sd[:, :].rearrange("p (b n) -> p b n", b=Q_BUFS)
        psum = ctx.enter_context(nc.psum_tensor("psum", [P, 8 * BANK], F32))

        def bank(b, n=BANK, at=0):
            return psum[:, b * BANK + at:b * BANK + at + n]

        def V(name):
            a, w = VCOL[name]
            return vec[:, a:a + w]

        top = [0]

        def reserve(n, at=None):
            if at is not None:
                top[0] = at
            a = arena[:, top[0]:top[0] + n]
            top[0] += n
            assert top[0] <= ARENA, top[0]
            return a

        stage_of = {e: sem(f"{e}_stage") for e in ("pe", "act", "dve", "pool")}
        act_steps, dve_steps, pool_steps = sem("act_steps"), sem("dve_steps"), sem("pool_steps")
        inputs_in, tables_in = sem("inputs_in"), sem("tables_in")
        weights_in = [sem(f"weights_in{i}") for i in range(RING)]
        tile_ready, act_took, dve_took = sem("tile_ready"), sem("act_took"), sem("dve_took")
        ada_summed, ada_ready, ada_taken = sem("ada_summed"), sem("ada_ready"), sem("ada_taken")
        squares_ready, mean_ready, sd_ready = sem("squares_ready"), sem("mean_ready"), sem("sd_ready")
        square_read, scaled_ready, norm_ready = sem("square_read"), sem("scaled_ready"), sem("norm_ready")
        centred, sumsq_ready = sem("centred"), sem("sumsq_ready")
        spread_ready, yn_ready, swap_ready = sem("spread_ready"), sem("yn_ready"), sem("swap_ready")
        cos_ready, rope_done = sem("cos_ready"), sem("rope_done")
        scores_ready, negmax_ready, probs_ready = sem("scores_ready"), sem("negmax_ready"), sem("probs_ready")
        exp_done, turned = sem("exp_done"), sem("turned")
        copied = sem("copied")
        o_ready, o_taken = sem("o_ready"), sem("o_taken")
        pv_done = sem("pv_done")
        bias_in, bias_used = [sem("bias_in0"), sem("bias_in1")], sem("bias_used")
        idx_ready, relu_ready, idx_taken = sem("idx_ready"), sem("relu_ready"), sem("idx_taken")
        scratch_in, out_done = sem("scratch_in"), sem("out_done")
        q_ready, context_in = sem("q_ready"), sem("context_in")
        rstd_diagonal, rstd_ready = sem("rstd_diagonal"), sem("rstd_ready")
        glu_done, taps_ready, taps_used = sem("glu_done"), sem("taps_ready"), sem("taps_used")
        misc_pe, misc_act, misc_dve = sem("misc_pe"), sem("misc_act"), sem("misc_dve")

        rpb_table = nc.dram_tensor("rpb_table", (16, GRID, 15, GRID), F32).ap()

        stages, blocks = [], []

        def block(view, upper=None):
            shape = view.shape
            n = 1
            for d in shape[1:]:
                n *= d
            assert n <= SLOT, shape
            blocks.append((view, n, upper))
            return len(blocks) - 1

        def slot(b, k):
            return ring[:, b % RING, 0:blocks[b][1]].rearrange("p (k n) -> p k n", k=k)

        def ada_vectors(layer, j):
            return 2 if layer == 0 or (layer == 1 and j < 4) else 1

        ada_left = []

        def start_ada(layer):
            ada_left.extend((layer, j) for j in range(12))

        def next_ada():
            if not ada_left:
                return None
            layer, j = ada_left.pop(0)
            b = block(dram["ada_w"][layer, :, 512 * j:512 * j + 512].rearrange("(k p) n -> p k n", p=P))
            return b, layer, j

        def stage(kind, **kw):
            kw["kind"] = kind
            kw.setdefault("loads", [])
            stages.append(kw)
            return kw

        def wide(src, tiles_of, k=KD, cols=512, width=None, rides_from=0, **kw):
            total = width or src.shape[1]
            groups_ = []
            for c0 in range(0, total, cols):
                c1 = min(total, c0 + cols)
                b = block(src[:, c0:c1].rearrange("(k p) n -> p k n", p=P))
                groups_.append([b, (c0, c1)])
                a = next_ada() if c0 // cols >= rides_from else None
                groups_[-1].append(a)
            st = stage("project", groups=[], **kw)
            for b, (c0, c1), a in groups_:
                st["groups"].append((b, tiles_of(b, c0, c1), a))
            return st

        def t_tile(b, k, col, width, act, n, taker, op, dst, arg=None, part=0, tile=None):
            w = slot(b, k)
            return Tile([(w[:, i, col:col + width], act[:, i, 0:n]) for i in range(k)],
                        (part, width, n), taker, op, dst, arg, tile)

        def n_tile(b, k, col, width, act, tt, taker, op, dst, arg=None):
            w = slot(b, k)
            return Tile([(act[:, i, tt * P:tt * P + P], w[:, i, col:col + width]) for i in range(k)],
                        (0, P, width), taker, op, dst, arg)

        def norm(src, dst, n, gain, shift=None, sq=None):
            stage("norm", src=src, dst=dst, n=n, gain=gain, shift=shift, sq=sq)

        low_arena = arena[:, 0:KD * S].rearrange("p (t s) -> p t s", s=S)

        def residual_tiles(b, c0, c1, dst, act, n, gate):
            return [t_tile(b, KD, P * j, P, act, n, "dve", "resid", dst[:, c0 // P + j, 0:n],
                           gate(c0 // P + j) if gate else None, tile=c0 // P + j) for j in range((c1 - c0) // P)]

        top[0] = 0
        WORK = 7680
        work = reserve(6144)
        rope_t = reserve(2 * S + P)
        hn_t = reserve(PAIR_TILES * (PAIR_ROWS + P))
        QA, KA, QI, KI = (reserve(n * S).rearrange("p (t s) -> p t s", s=S) for n in (4, 1, 2, 1))
        QB, KB, Z = (reserve(n * S).rearrange("p (t s) -> p t s", s=S) for n in (4, 1, 8))
        VAB = reserve(ST * 256).rearrange("p (t n) -> p t n", t=ST)
        WI = reserve(ST * 4).rearrange("p (t n) -> p t n", t=ST)
        dsa_mask = reserve(3 * S // 2).bitcast(BF16).rearrange("p (t s) -> p t s", t=3)

        norm(X, H, S, lambda k: V("ab_norm")[:, k:k + 1])
        b = block(dram["ab_in"][:, 0:IDX_COLS].rearrange("(k p) n -> p k n", p=P))
        stage("project", groups=[(b, [t_tile(b, KD, P * j, P, H, S, "act", "copy", dst)
                                      for j, dst in enumerate((QI[:, 0], QI[:, 1], KI[:, 0]))]
                                  + [n_tile(b, KD, 3 * P, 4, H, tt, "act", "scale", WI[:, tt, :], 1.0 / 16)
                                     for tt in range(ST)], None)],
              loads=[(rope_t, dram["rope_ab"]), (hn_t, dram["hn_pair"])])
        ab_cols = ([("copy", QA[:, t]) for t in range(4)] + [("copy", KA[:, 0])] + [("copy", QB[:, t]) for t in range(4)]
                   + [("copy", KB[:, 0])] + [("silu", Z[:, t]) for t in range(8)])

        def ab_tiles(b, c0, c1):
            out = [t_tile(b, KD, P * j, P, H, S, "act", *ab_cols[c0 // P + j])
                   for j in range(min(4, len(ab_cols) - c0 // P))]
            if len(out) < 4:
                out += [n_tile(b, KD, 256, 256, H, tt, "act", "copy", VAB[:, tt, :]) for tt in range(ST)]
            return out

        def pair_constants(i, hn_t=hn_t):
            a = PAIR_TILES * PAIR_ROWS
            return (hn_t[:, i * PAIR_ROWS:(i + 1) * PAIR_ROWS], hn_t[0:PAIR_ROWS, a + i * P:a + (i + 1) * P])

        def headnorm(tiles, n, consts, rows, parts, swap=None, cos=None, sin=None, wk=None):
            stage("headnorm", tiles=tiles, n=n, consts=consts, rows=rows, parts=parts, swap=swap, cos=cos, sin=sin,
                  wk=wk)

        cos_t, sin_t, swap_t = rope_t[:, 0:S], rope_t[:, S:2 * S], rope_t[:, 2 * S:2 * S + P]
        headnorm([(KI[:, 0], V("ki_g"))] + [(QI[:, t], None) for t in range(2)], S, pair_constants, PAIR_ROWS, P, swap_t,
                 cos_t, sin_t, work)
        stage("dsa", wk=work)
        start_ada(0)
        wide(dram["ab_in"][:, IDX_COLS:], ab_tiles, beside=True, rides_from=4)
        headnorm([(QA[:, t], V("qa_g")) for t in range(4)] + [(KA[:, 0], V("ka_g"))]
                 + [(QB[:, t], V("qb_g")) for t in range(4)] + [(KB[:, 0], V("kb_g"))],
                 S, pair_constants, PAIR_ROWS, P, swap_t, cos_t, sin_t, work)

        def causal(qt):
            return 0, qt + 1

        def causal_pv():
            return [(kt, kt * P, S) for kt in range(ST)]

        def attention(passes, wk, keys_max, loads=()):
            stage("attention", passes=passes, wk=wk, keys_max=keys_max, loads=list(loads))

        def attn_pass(q, k, v, keys, pv, dst=None, z=None, masks=None, first=True, last=True, n=S, gate=None, sink=None,
                      clamp=False, bias=None, krows=P, split=True):
            return dict(q=q, k=k, v=v, keys=keys, pv=pv, dst=dst, z=z, masks=masks, first=first, last=last, n=n,
                        units=2 * n // P, gate=gate, sink=sink, clamp=clamp, bias=bias, krows=krows, split=split)

        passes = []
        for t in range(4):
            passes.append(attn_pass(
                lambda g, q0, q1, t=t: QA[:, t, q0:q1], lambda g, k0, k1: KA[:, 0, k0:k1],
                lambda g, kt: VAB[:, kt, HD * g:HD * g + HD], causal, causal_pv(), H[:, t], Z[:, t],
                lambda qt: [(0, diagm[:, :])] if qt == 0 else [(0, dsa_mask[:, qt - 1, 0:(qt + 1) * P])]))
        band_pv = [(kt, qt * P, qt * P + P) for qt in range(ST) for kt in range(max(0, qt - 1), qt + 1)]
        for t in range(4):
            passes.append(attn_pass(
                lambda g, q0, q1, t=t: QB[:, t, q0:q1], lambda g, k0, k1: KB[:, 0, k0:k1],
                lambda g, kt: VAB[:, kt, 128 + HD * g:128 + HD * g + HD], lambda qt: (max(0, qt - 1), qt + 1), band_pv,
                H[:, 4 + t], Z[:, 4 + t],
                lambda qt: [(0, diagm[:, :])] if qt == 0 else [(0, prevm[:, :]), (P, diagm[:, :])],
                sink=sinks[:, t:t + 1]))
        attention(passes, work, 512)
        wide(dram["ab_out"], lambda b, c0, c1: residual_tiles(b, c0, c1, X, H, S, None))

        top[0] = 0
        work = reserve(6144)
        rope_t = reserve(2 * S + P)
        CQ, CKV, KR, Z2 = (reserve(n * S).rearrange("p (t s) -> p t s", s=S) for n in (2, 1, 1, 8))
        shared = top[0] + MLA_TILES * (MLA_ROWS + P)
        hn_t = reserve(PAIR_TILES * (PAIR_ROWS + P))
        QC, KC, VC, KS, KW = (reserve(n * S).rearrange("p (t s) -> p t s", s=S) for n in (4, 1, 1, 1, 1))
        VSW = reserve(ST * 256).rearrange("p (t n) -> p t n", t=ST)
        GC = reserve(ST * 24).rearrange("p (t n) -> p t n", t=ST)
        GH = reserve(2 * ST * 12).rearrange("p (e t n) -> p e t n", e=2, t=ST)
        KCT, VCN = reserve(32), reserve(P)
        cmpm = reserve(ST * NCMP).rearrange("p (t n) -> p t n", t=ST)
        rope_c = reserve(2 * NCMP)
        cmpmb = reserve(ST * 16).bitcast(BF16).rearrange("p (t n) -> p t n", t=ST)
        norm(X, H, S, lambda k: V("cd_norm")[:, k:k + 1], sq=low_arena)
        cd_cols = ([("copy", QC[:, t]) for t in range(4)] + [("copy", KC[:, 0]), ("copy", VC[:, 0]), ("copy", KS[:, 0]),
                   ("copy", KW[:, 0])] + [("copy", CQ[:, t]) for t in range(2)] + [("copy", CKV[:, 0])]
                   + [("silu", Z2[:, t]) for t in range(8)])

        def cd_tiles(b, c0, c1):
            if c0 == 2560:
                return []
            out = [t_tile(b, KD, P * j, P, H, S, "act", *cd_cols[c0 // P + j])
                   for j in range(min(4, len(cd_cols) - c0 // P))]
            return out

        def cd_all(b, c0, c1):
            out = []
            if c0 < 2048:
                return cd_tiles(b, c0, c1)
            if c0 == 2048:
                out = [t_tile(b, KD, P * j, P, H, S, "act", *cd_cols[16 + j]) for j in range(3)]
                out.append(t_tile(b, KD, 384, 32, H, S, "act", "copy", KR[64:96, 0], part=64))
                for tt in range(ST):
                    out.append(n_tile(b, KD, 416, 24, H, tt, "act", "sigmoid", GC[:, tt, :]))
                return out
            for tt in range(ST):
                out.append(n_tile(b, KD, 0, 256, H, tt, "act", "copy", VSW[:, tt, :]))
            return out

        groups_ = []
        for c0, c1 in ((0, 512), (512, 1024), (1024, 1536), (1536, 2048), (2048, 2488), (2488, 2744)):
            b = block(dram["cd_in"][:, c0:c1].rearrange("(k p) n -> p k n", p=P))
            groups_.append((b, (c0, c1), next_ada()))
        stage("project", groups=[(b, cd_all(b, *c), a) for b, c, a in groups_],
              loads=[(rope_t, dram["rope_ab"]), (hn_t, dram["hn_pair"]), (cmpm.rearrange("p t n -> p (t n)"),
                     dram["cmp_mask"].rearrange("p t n -> p (t n)")), (rope_c, dram["rope_cmp"])])
        cos_t, sin_t, swap_t = rope_t[:, 0:S], rope_t[:, S:2 * S], rope_t[:, 2 * S:2 * S + P]

        def pair_constants2(i, hn_t=hn_t):
            a = PAIR_TILES * PAIR_ROWS
            return (hn_t[:, i * PAIR_ROWS:(i + 1) * PAIR_ROWS], hn_t[0:PAIR_ROWS, a + i * P:a + (i + 1) * P])

        cmp_blocks = []
        for kv in range(2):
            cmp_blocks.append(block(dram["cmp_w1"][kv, 0:CMP_HALF * HD].rearrange("(l d) m -> d l m", d=HD),
                                    dram["cmp_w1"][kv, CMP_HALF * HD:].rearrange("(l d) m -> d l m", d=HD)))
            cmp_blocks.append(block(dram["cmp_w2"][kv]))
        stage("compress", wk=work, wblocks=cmp_blocks)
        headnorm([(QC[:, t], V("qc_g")) for t in range(4)] + [(KS[:, 0], V("ks_g")), (KW[:, 0], V("kw_g"))],
                 S, pair_constants2, PAIR_ROWS, P, swap_t, cos_t, sin_t, work)
        headnorm([(KCT[:, 0:NCMP], V("kc_g"))], NCMP, pair_constants2, PAIR_ROWS, P, swap_t, rope_c[:, 0:NCMP],
                 rope_c[:, NCMP:2 * NCMP], work)
        passes = []
        for t in range(4):
            q = lambda g, q0, q1, t=t: QC[:, t, q0:q1]
            passes.append(attn_pass(
                q, lambda g, k0, k1: KCT[:, k0:min(k1, NCMP)],
                lambda g, kt: VCN[0:NCMP, HD * g:HD * g + HD], lambda qt: (0, 1), [(0, 0, S)],
                masks=lambda qt: [(0, cmpmb[:, qt, 0:NCMP])], last=False, clamp=True, krows=NCMP,
                gate=lambda j, t=t: GH[:, j % 2, j // 2, 3 * t:3 * t + 1]))
            for br, (kk, v0) in enumerate(((KS, 0), (KW, 128))):
                passes.append(attn_pass(
                    q, lambda g, k0, k1, kk=kk: kk[:, 0, k0:k1],
                    lambda g, kt, v0=v0: VSW[:, kt, v0 + HD * g:v0 + HD * g + HD], causal, causal_pv(), H[:, t], Z2[:, t],
                    lambda qt: [(qt * P, diagm[:, :])], first=False, last=br == 1,
                    gate=lambda j, t=t, br=br: GH[:, j % 2, j // 2, 3 * t + br + 1:3 * t + br + 2]))
        attention(passes, work, 512)
        top[0] = shared
        QD, KDT = (reserve(8 * S).rearrange("p (t s) -> p t s", s=S) for _ in range(2))
        VD = reserve(ST * 512).rearrange("p (t n) -> p t n", t=ST)

        def lat_constants(i):
            return None

        stage("latnorm", wk=work, loads=[(rope_t, dram["rope_mla"]), (hn_t[:, 0:MLA_TILES * (MLA_ROWS + P)], dram["hn_mla"])],
              CQ=CQ, CKV=CKV)
        b0 = block(dram["uq"].rearrange("(k p) n -> p k n", p=P))
        a0 = next_ada()
        b1 = block(dram["ukv"])
        a1 = next_ada()
        w1v = ring[:, b1 % RING, 0:1024].rearrange("p (k n) -> p k n", k=1)
        tl0 = [t_tile(b0, 2, MLA_W * h, MLA_W, CQ, S, "act", "copy", QD[0:MLA_W, h]) for h in range(8)]
        tl1 = [Tile([(w1v[:, 0, 64 * h:64 * h + 64], CKV[:, 0, :])], (0, 64, S), "act", "copy", KDT[0:64, h])
               for h in range(8)]
        tl1 += [Tile([(CKV[:, 0, tt * P:tt * P + P], w1v[:, 0, 512:1024])], (0, P, 512), "act", "copy", VD[:, tt, :])
                for tt in range(ST)]
        stage("project", groups=[(b0, tl0, a0), (b1, tl1, a1)],
              extra=[(KDT[64:96, h], KR[64:96, 0]) for h in range(8)])

        def mla_constants(i, hn_t=hn_t):
            a = MLA_TILES * MLA_ROWS
            return (hn_t[0:MLA_W, i * MLA_ROWS:(i + 1) * MLA_ROWS], hn_t[0:MLA_ROWS, a + i * P:a + i * P + MLA_W])

        for tiles in ([(QD[0:MLA_W, h], V("qd_g")) for h in range(8)], [(KDT[0:MLA_W, h], V("kd_g")) for h in range(8)]):
            headnorm(tiles, S, mla_constants, MLA_ROWS, MLA_W, rope_t[0:MLA_W, 2 * S:2 * S + MLA_W], rope_t[:, 0:S],
                     rope_t[:, S:2 * S], work)
        passes = []
        for t in range(4):
            passes.append(attn_pass(
                lambda g, q0, q1, t=t: QD[0:MLA_W, 2 * t + g, q0:q1], lambda g, k0, k1, t=t: KDT[0:MLA_W, 2 * t + g, k0:k1],
                lambda g, kt, t=t: VD[:, kt, HD * (2 * t + g):HD * (2 * t + g) + HD], causal, causal_pv(), H[:, 4 + t],
                Z2[:, 4 + t], lambda qt: [(qt * P, diagm[:, :])], split=False))
        attention(passes, work, 512)
        wide(dram["cd_out"], lambda b, c0, c1: residual_tiles(b, c0, c1, X, H, S, None))
        while ada_left:
            stage("project", groups=[(None, [], next_ada())])

        def mod(layer, chunk, v):
            return lambda k: mods[:, layer % 2, chunk * KD + k, v:v + 1]

        def sg(half, v):
            return lambda k: sgain[:, half, v, k:k + 1]

        def mlp(layer, with_ctx, loads=(), after_tables=False):
            norm(X, H, S, sg(1, 0), mod(layer, 3, 0), sq=low_arena)
            if with_ctx:
                norm(CX, CH, C, sg(1, 1), mod(layer, 3, 1))
            start_ada(layer + 1) if layer < 3 else None
            top[0] = 0
            hid = reserve(32 * S).rearrange("p (t s) -> p t s", s=S)
            hidc = reserve(32 * C).rearrange("p (t s) -> p t s", s=C) if with_ctx else None

            def up(b, c0, c1):
                out = []
                out += [t_tile(b, KD, P * j, P, H, S, "act", "relu2", hid[:, c0 // P + j]) for j in range(4)]
                if with_ctx:
                    out += [t_tile(b, KD, P * j, P, CH, C, "act", "relu2", hidc[:, c0 // P + j]) for j in range(4)]
                return out

            wide(dram["mlp_w1"][layer], up, after_tables=after_tables)
            groups = []
            for half in range(2):
                for kb in range(4):
                    b = block(dram["mlp_w2"][layer, 1024 * kb:1024 * kb + 1024, 512 * half:512 * half + 512]
                              .rearrange("(k p) n -> p k n", p=P))
                    groups.append((half, kb, b, next_ada()))
            stage("down", groups=groups, hid=hid, hidc=hidc, gate=mod(layer, 5, 0), gatec=mod(layer, 5, 1),
                  loads=list(loads))

        def prep(layer, with_ctx):
            stage("prep", layer=layer, needs=[(0, 0), (1, 0)] + ([(0, 1)] if with_ctx else [])
                  + ([(1, 1)] if layer == 0 else []))

        prep(0, True)
        norm(X, H, S, sg(0, 0), mod(0, 0, 0), sq=low_arena)
        norm(CX, CH, C, sg(0, 1), mod(0, 0, 1))
        top[0] = 0
        work = reserve(WORK)
        rope_t = reserve(2 * S + P)
        hn_t = reserve(PAIR_TILES * (PAIR_ROWS + P))
        Q = reserve(8 * S).rearrange("p (t s) -> p t s", s=S)
        QX = reserve(8 * C).rearrange("p (t s) -> p t s", s=C)
        K2 = reserve(2 * (S + C)).rearrange("p (t s) -> p t s", s=S + C)
        V2 = reserve(6 * 256).rearrange("p (t n) -> p t n", t=6)
        na_sel, na_rpb = reserve(GRID * GRID), reserve(16 * 15)

        def at_tiles(b, c0, c1):
            out = []
            if c0 < 1024:
                out += [t_tile(b, KD, P * j, P, H, S, "act", "copy", Q[:, c0 // P + j]) for j in range(4)]
                out += [t_tile(b, KD, P * j, P, CH, C, "act", "copy", QX[:, c0 // P + j]) for j in range(4)]
                return out
            for j in range(2):
                out.append(t_tile(b, KD, P * j, P, H, S, "act", "copy", K2[:, j, 0:S]))
                out.append(t_tile(b, KD, P * j, P, CH, C, "act", "copy", K2[:, j, S:S + C]))
            for tt in range(6):
                src, t0 = (H, tt) if tt < ST else (CH, tt - ST)
                out.append(n_tile(b, KD, 256, 256, src, t0, "act", "copy", V2[:, tt, :]))
            return out

        wide(dram["at_qkv"], at_tiles, loads=[(rope_t, dram["rope_at"]), (hn_t, dram["hn_pair"])])

        def pair_constants3(i, hn_t=hn_t):
            a = PAIR_TILES * PAIR_ROWS
            return (hn_t[:, i * PAIR_ROWS:(i + 1) * PAIR_ROWS], hn_t[0:PAIR_ROWS, a + i * P:a + (i + 1) * P])

        headnorm([(Q[:, t], V("at_q_g")) for t in range(8)] + [(K2[:, t, 0:S], V("at_k_g")) for t in range(2)], S,
                 pair_constants3, PAIR_ROWS, P, rope_t[:, 2 * S:2 * S + P], rope_t[:, 0:S], rope_t[:, S:2 * S], work)
        headnorm([(QX[:, t], V("at_q_g")) for t in range(8)] + [(K2[:, t, S:S + C], V("at_k_g")) for t in range(2)], C,
                 pair_constants3, PAIR_ROWS, P, None, None, None, work)
        passes = []
        for t in range(8):
            passes.append(attn_pass(
                lambda g, q0, q1, t=t: Q[:, t, q0:q1],
                lambda g, k0, k1, t=t: K2[:, t // 4, k0:k1],
                lambda g, kt, t=t: V2[:, kt, HD * (2 * (t // 4) + g):HD * (2 * (t // 4) + g) + HD],
                lambda qt: (0, 6), [(kt, 0, S) for kt in range(6)], H[:, t]))
        for t in range(8):
            passes.append(attn_pass(
                lambda g, q0, q1, t=t: QX[:, t, q0:q1],
                lambda g, k0, k1, t=t: K2[:, t // 4, S + k0:S + k1],
                lambda g, kt, t=t: V2[:, 4 + kt, HD * (2 * (t // 4) + g):HD * (2 * (t // 4) + g) + HD],
                lambda qt: (0, 2), [(kt, 0, C) for kt in range(2)], CH[:, t], n=C))
        attention(passes, work, 768, [(na_sel[0:32], dram["na_select"]), (na_rpb[0:32], dram["na_rpb"])])
        stage("rpb", sel=na_sel, rpb=na_rpb,
              tab=arena[:, KD * S:KD * S + 2 * GRID * GRID].rearrange("p (m n) -> p m n", m=2))

        def at_out(b, c0, c1):
            out = []
            out += residual_tiles(b, c0, c1, X, H, S, mod(0, 2, 0))
            out += residual_tiles(b, c0, c1, CX, CH, C, mod(0, 2, 1))
            return out

        wide(dram["at_o"], at_out)
        mlp(0, True, after_tables=True)
        prep(1, True)
        norm(X, H, S, sg(0, 0), mod(1, 0, 0), sq=H)
        norm(CX, CH, C, sg(0, 1), mod(1, 0, 1))
        top[0] = 0
        work = reserve(7680)
        QN = reserve(8 * S).rearrange("p (t s) -> p t s", s=S)
        KN = reserve(8 * (S + C)).rearrange("p (t s) -> p t s", s=S + C)
        VN = reserve(6 * 1024).rearrange("p (t n) -> p t n", t=6)
        def na_tiles(b, c0, c1):
            out = []
            for j in range(4):
                if c0 < 1024:
                    out.append(t_tile(b, KD, P * j, P, H, S, "act", "scale", QN[:, c0 // P + j], 0.125))
                elif c0 < 2048:
                    kt = c0 // P - 8 + j
                    out.append(t_tile(b, KD, P * j, P, H, S, "act", "copy", KN[:, kt, 0:S]))
                    out.append(t_tile(b, KD, P * j, P, CH, C, "act", "copy", KN[:, kt, S:S + C]))
            if c0 >= 2048:
                for tt in range(6):
                    src, t0 = (H, tt) if tt < ST else (CH, tt - ST)
                    out.append(n_tile(b, KD, 0, 512, src, t0, "act", "copy", VN[:, tt, c0 - 2048:c0 - 1536]))
            return out

        wide(dram["na_qkv"], na_tiles)
        bias_buf = CX.rearrange("p t s -> p (t s)").rearrange("p (b n) -> p b n", b=2)
        passes = []
        for t in range(8):
            passes.append(attn_pass(
                lambda g, q0, q1, t=t: QN[:, t, q0:q1], lambda g, k0, k1, t=t: KN[:, t, k0:k1],
                lambda g, kt, t=t: VN[:, kt, HD * (2 * t + g):HD * (2 * t + g) + HD],
                lambda qt: (0, 6), [(kt, 0, S) for kt in range(6)], H[:, t],
                bias=lambda j, t=t: bias_buf[:, t % 2, (ROWS - 1 - j) * GRID:(ROWS - 1 - j) * GRID + S]))
        attention(passes, work, 768)
        wide(dram["na_o"], lambda b, c0, c1: residual_tiles(b, c0, c1, X, H, S, mod(1, 2, 0)))
        mlp(1, False)
        prep(2, False)
        norm(X, H, S, sg(0, 0), mod(2, 0, 0), sq=H)
        top[0] = 0
        UP = S + TAPS - 1
        U = reserve(KD * UP).rearrange("p (t s) -> p t s", s=UP)
        SIG = reserve(KD * S).rearrange("p (t s) -> p t s", s=S)
        CV = reserve(KD * S).rearrange("p (t s) -> p t s", s=S)
        work = reserve(4096)
        wide(dram["pw1"][:, D:2 * D], lambda b, c0, c1: [
            t_tile(b, KD, P * j, P, H, S, "act", "sigmoidb", SIG[:, c0 // P + j],
                   V("cv_b1")[:, KD + c0 // P + j:KD + c0 // P + j + 1]) for j in range(4)], pads=U)
        wide(dram["pw1"][:, 0:D], lambda b, c0, c1: [
            t_tile(b, KD, P * j, P, H, S, "act", "plus", U[:, c0 // P + j, TAPS // 2:TAPS // 2 + S],
                   V("cv_b1")[:, c0 // P + j:c0 // P + j + 1]) for j in range(4)])
        stage("conv", U=U, CV=CV, sig=SIG, taps=work[:, 0:TAPS * P].rearrange("p (t n) -> p t n", t=TAPS))
        stage("layernorm", src=CV, dst=H, sq=SIG)
        wide(dram["pw2"], lambda b, c0, c1: [
            t_tile(b, KD, P * j, P, H, S, "dve", "residb", X[:, c0 // P + j],
                   (V("cv_b2")[:, c0 // P + j:c0 // P + j + 1], mod(2, 2, 0)(c0 // P + j), SIG[:, j % 2]), tile=c0 // P + j)
            for j in range(4)])
        dg = reserve(2 * 512, at=32 * S).rearrange("p (k n) -> p k n", k=2)
        dq = reserve(ST * 2 * S).rearrange("p (k n) -> p k n", k=ST)
        mlp(2, False, loads=[(dg, dram["dft_group"].rearrange("(k p) n -> p k n", p=P)),
                             (dq, dram["dft_seq"].rearrange("(k p) n -> p k n", p=P))])
        prep(3, False)
        norm(X, H, S, sg(0, 0), mod(3, 0, 0), sq=H)
        top[0] = 0
        FA = reserve(ST * 4 * 512).rearrange("p (t g n) -> p t g n", t=ST, g=4)
        tmpf = reserve(2 * S).rearrange("p (t s) -> p t s", s=S)
        tl = [Tile([(H[:, 2 * g + k, tt * P:tt * P + P], dg[:, k, :]) for k in range(2)], (0, P, 512), "act", "copy",
                   FA[:, tt, g, :], first=2 * g) for g in range(4) for tt in range(ST)]
        stage("project", groups=[(None, tl, None)])
        tl = []
        for g in range(4):
            for d2 in range(2):
                prs = []
                for tt in range(ST):
                    prs.append((FA[:, tt, g, d2 * P:d2 * P + P], dq[:, tt, 0:S]))
                    prs.append((FA[:, tt, g, GW + d2 * P:GW + d2 * P + P], dq[:, tt, S:2 * S]))
                tl.append(Tile(prs, (0, P, S), "act", "copy", H[:, 2 * g + d2]))
        stage("project", groups=[(None, tl, None)])
        wide(dram["ft_w"], lambda b, c0, c1: [
            t_tile(b, KD, P * j, P, H, S, "dve", "residb", X[:, c0 // P + j],
                   (V("ft_b")[:, c0 // P + j:c0 // P + j + 1], mod(3, 2, 0)(c0 // P + j), tmpf[:, j % 2]), tile=c0 // P + j)
            for j in range(4)])
        mlp(3, False)
        norm(X, H, S, lambda k: V("final_g")[:, k:k + 1], sq=H)
        assert not ada_left

        del stages[stages_kept:]

        used = []
        freed_by = []
        n_tiles = n_ada = n_normed = n_squares = 0
        n_took = dict(act=0, dve=0)
        x_done = {}
        for s_, st in enumerate(stages):
            before = stages[s_ - 1]["kind"] if s_ else None
            st["norm0"], st["sq0"] = n_normed, n_squares
            if st["kind"] == "project":
                st["chases"] = before in ("norm", "layernorm")
                two = before == "norm" and stages[s_ - 1]["n"] == C
                st["norm_x"] = n_normed - KD * (2 if two else 1)
                st["norm_c"] = n_normed - KD if two else None
                hid_done = []
                for b, tiles, a in st["groups"]:
                    for t in tiles:
                        n_tiles += 1
                        n_took[t.taker] += 1
                        if t.op in ("resid", "residb") and t.out[2] == S:
                            x_done[t.tile] = n_took["dve"]
                        hid_done.append(n_took["act"])
                    if b is not None:
                        used.append(b)
                        freed_by.append((tile_ready, n_tiles))
                    if a:
                        n_ada += 1
                        used.append(a[0])
                        freed_by.append((ada_summed, n_ada))
            elif st["kind"] == "down":
                st["hid_done"] = hid_done
                for half, kb, b, a in st["groups"]:
                    n_tiles += 4 if kb == 3 else 1
                    used.append(b)
                    freed_by.append((tile_ready, n_tiles))
                    if kb == 3:
                        for m in range(4):
                            n_took["dve"] += 1
                            x_done[4 * half + m] = n_took["dve"]
                    if a:
                        n_ada += 1
                        used.append(a[0])
                        freed_by.append((ada_summed, n_ada))
            elif st["kind"] == "conv":
                st["u_done"] = list(hid_done)
            elif st["kind"] == "compress":
                used += st["wblocks"]
                freed_by += [(misc_pe, 3), (misc_pe, 5), (misc_pe, 4), (misc_pe, 6)]
            elif st["kind"] in ("norm", "layernorm"):
                n_normed += KD
                n_squares += KD
                st["x_done"] = dict(x_done)
            elif st["kind"] == "headnorm":
                n_squares += sum(t[1] is not None for t in st["tiles"])
            elif st["kind"] == "latnorm":
                n_squares += 3
        assert used == list(range(len(used))), used[:60]

        tables_before = []
        n_tab = 0
        for st in stages:
            tables_before.append(n_tab)
            n_tab += 16 * len(st["loads"])
        N_INPUTS = 10
        sd_count = misc_count = 0
        for st in stages:
            st["sd0"], st["pe0"] = sd_count, misc_count
            sd_count += dict(norm=1, headnorm=2, latnorm=1, layernorm=1).get(st["kind"], 0)
            misc_count += dict(compress=7, rpb=16, layernorm=1).get(st["kind"], 0)

        def gate(eng, own, s):
            if s > 0:
                for name, sm in stage_of.items():
                    eng.wait_ge(sm, s)
            else:
                eng.wait_ge(inputs_in, 16 * N_INPUTS)
            if tables_before[s]:
                eng.wait_ge(tables_in, tables_before[s])

        nc_block = ctx.enter_context(nc.Block())

        @nc_block.sync
        def _(sp):
            for dst, src in ((X[:, :, :], dram["x"].rearrange("k p s -> p k s")), (vec[:, :], dram["vectors"]),
                             (ident[:, :], dram["ident"]), (arena[:, 0:P], dram["diag_mask"]),
                             (arena[:, P:2 * P], dram["prev_mask"]),
                             (sinks[:, :], dram["sinks"])):
                sp.dma_start(dst, src).then_inc(inputs_in, 16)
            for b in range(len(used)):
                if b == RING:
                    sp.dma_start(CX[:, :, :], dram["ctx"].rearrange("k p s -> p k s")).then_inc(context_in, 16)
                view, n, upper = blocks[b]
                if b >= RING:
                    sp.wait_ge(*freed_by[b - RING])
                k = view.shape[1] if len(view.shape) == 3 else 1
                rows = view.shape[0]
                dst = ring[0:rows, b % RING, 0:n]
                if len(view.shape) == 3:
                    dst = dst.rearrange("p (k n) -> p k n", k=k)
                sp.dma_start(dst, view).then_inc(weights_in[b % RING], 16)
                if upper is not None:
                    sp.dma_start(ring[HD:2 * HD, b % RING, 0:n].rearrange("p (k n) -> p k n", k=k),
                                 upper).then_inc(weights_in[b % RING], 16)

        slot_count = [0] * RING
        landed = []
        for b in range(len(used)):
            slot_count[b % RING] += 32 if blocks[b][2] is not None else 16
            landed.append(slot_count[b % RING])

        def units_of(st):
            return [(pi, j) for pi, p in enumerate(st["passes"]) for j in range(p["units"])]

        def attn_buffers(st):
            km = st["keys_max"]
            nb = 4 if km <= BANK else 2
            probs = [st["wk"][:, i * km:(i + 1) * km] for i in range(nb)]
            return probs, st["wk"][:, nb * km:nb * km + km // P * 4 * CHUNK].rearrange(
                "p (c t g s) -> p c t g s", c=2, g=2, s=CHUNK)

        def depths(st):
            if st["keys_max"] <= BANK:
                return dict(nb=4, wide=BANK, nt=2, scale=1, turn=3)
            return dict(nb=2, wide=2 * BANK, nt=1, scale=1, turn=2)

        def unit_rows(p, j):
            if p["split"]:
                return None, HD * j, HD * j + HD
            return j % 2, P * (j // 2), P * (j // 2) + P

        def unit_keys(p, j):
            a, b = p["keys"](unit_rows(p, j)[1] // P)
            n = (b - a) * P if p["krows"] == P else p["krows"]
            return a, b, n

        def relu_buffer(wk, qt, h):
            at = 2 * S + 4 * P * sum(t + 1 for t in range(1, qt)) + h * (qt + 1) * P
            return wk[:, at:at + (qt + 1) * P]

        @nc_block.tensor
        def _(pe):
            tiles_made = [0]
            bank_freed = {}
            pending = []
            taken = {"act": 0, "dve": 0}
            n = dict(block=0, ada=0, norm=0, sq=0, mean=0, spread=0, swap=0, unit=0, pair=0, pas=0, idx=0, down=0,
                     yn=0, rope=0, sumsq=0, misc=0, split=0)

            def weights(b):
                pe.wait_ge(weights_in[b % RING], landed[b])

            def modulation(a):
                layer, j = a[1], a[2]
                pe.wait_ge(ada_summed, n["ada"] + 1)
                if n["ada"] >= 1:
                    pe.wait_ge(ada_taken, n["ada"])
                vs = ada_vectors(layer, j)
                for v in range(vs):
                    for m in range(4):
                        last = nc.tensor.matmul(bank(7)[:, 2 * m + v:2 * m + v + 1], partial[:, v, P * m:P * m + P],
                                                ones[:, :], start=(v == 0 and m == 0), stop=(v == vs - 1 and m == 3),
                                                skip_group_check=True)
                last.then_inc(ada_ready, 1)
                n["ada"] += 1

            def ride(a):
                if pending:
                    modulation(pending.pop())
                if a:
                    pending.append(a)

            def project(st):
                waited = 0
                for b, tiles, a in st["groups"]:
                    if b is not None:
                        weights(b)
                    for t in tiles:
                        part, rows, cols = t.out
                        at = tiles_made[0] % PROJ_BANKS
                        if at in bank_freed:
                            pe.wait_ge(*bank_freed[at])
                        out = psum[part:part + rows, at * BANK:at * BANK + cols]
                        for k, (lhs, rhs) in enumerate(t.pairs):
                            if st["chases"] and waited < t.first + k + 1:
                                waited = t.first + k + 1
                                pe.wait_ge(norm_ready, st["norm_x"] + waited)
                            if st["chases"] and cols == C and waited <= KD and st["norm_c"] is not None:
                                waited = KD + 1
                                pe.wait_ge(norm_ready, st["norm_c"] + KD)
                            last = nc.tensor.matmul(out, lhs, rhs, start=(k == 0), stop=(k == len(t.pairs) - 1))
                        last.then_inc(tile_ready, 1)
                        tiles_made[0] += 1
                        taken[t.taker] += 1
                        bank_freed[at] = (act_took if t.taker == "act" else dve_took, taken[t.taker])
                    ride(a)

            def down(st):
                hid, hidc = st["hid"], st["hidc"]
                for half, kb, b, a in st["groups"]:
                    weights(b)
                    w = slot(b, KD)
                    for m in range(4):
                        if kb == 0:
                            for bk in {m, 4 + m // 2} if hidc is not None else {m}:
                                if bk in bank_freed:
                                    pe.wait_ge(*bank_freed[bk])
                        for k in range(KD):
                            if half == 0 and m == 0:
                                kt = KD * kb + k
                                pe.wait_ge(act_took, st["hid_done"][kt if hidc is None else 8 * (kt // 4) + 4 + kt % 4])
                            last = nc.tensor.matmul(bank(m), w[:, k, P * m:P * m + P], hid[:, KD * kb + k, :],
                                                    start=(kb == 0 and k == 0), stop=(kb == 3 and k == KD - 1))
                        if hidc is not None:
                            for k in range(KD):
                                last = nc.tensor.matmul(bank(4 + m // 2, C, C * (m % 2)), w[:, k, P * m:P * m + P],
                                                        hidc[:, KD * kb + k, :], start=(kb == 0 and k == 0 and m % 2 == 0),
                                                        stop=(kb == 3 and k == KD - 1), skip_group_check=True)
                        if kb == 3 or m == 3:
                            last.then_inc(tile_ready, 1)
                            tiles_made[0] += 1
                        if kb == 3:
                            taken["dve"] += 1
                            bank_freed[m] = bank_freed[4 + m // 2] = (dve_took, taken["dve"])
                    ride(a)

            def norm_sum(st):
                if st["sd0"]:
                    pe.wait_ge(sd_ready, st["sd0"])
                    pe.wait_ge(norm_ready, st["norm0"])
                if st["sq"] is not None:
                    pe.wait_ge(sumsq_ready, n["sumsq"] + 1)
                    for i in range(ST):
                        last = nc.tensor.matmul(bank(6)[:, i:i + 1], st["sq"][:, 0, P * i:P * i + P], mean_d[:, 0:1],
                                                start=(i == 0), stop=(i == ST - 1), skip_group_check=True)
                    last.then_inc(mean_ready, 1)
                    n["sumsq"] += 1
                    pe.wait_ge(rstd_diagonal, n["sumsq"])
                    nc.tensor.matmul(bank(6), mean_d[:, :], rstd[:, :], start=True, stop=True).then_inc(rstd_ready, 1)
                    n["sq"] += KD
                    return
                for k in range(KD):
                    pe.wait_ge(squares_ready, n["sq"] + k + 1)
                    last = nc.tensor.matmul(bank(6, st["n"]), mean_d[:, :], st["dst"][:, k, 0:st["n"]],
                                            start=(k == 0), stop=(k == KD - 1))
                last.then_inc(mean_ready, 1)
                n["sq"] += KD

            def headnorm(st):
                N, parts, rows = st["n"], st["parts"], st["rows"]
                normed = [t for t in st["tiles"] if t[1] is not None]
                sqb = st["wk"][:, 0:2 * S].rearrange("p (b s) -> p b s", b=2)
                for i in range(len(normed)):
                    pe.wait_ge(squares_ready, n["sq"] + i + 1)
                    last = nc.tensor.matmul(bank(0, N)[0:rows], st["consts"](i)[0], sqb[0:parts, i % 2, 0:N],
                                            start=(i == 0), stop=(i == len(normed) - 1))
                    last.then_inc(square_read, 1)
                n["sq"] += len(normed)
                rs = st["wk"][0:rows, 3 * S:3 * S + N]
                ynb = st["wk"][0:parts, 4 * S:6 * S].rearrange("p (b s) -> p b s", b=2)
                for i, (data, g) in enumerate(st["tiles"]):
                    if g is not None:
                        if i == 0:
                            pe.wait_ge(sd_ready, st["sd0"] + 2)
                        if i >= 2:
                            pe.wait_ge(yn_ready, n["yn"] + i - 1)
                        nc.tensor.matmul(bank(1 + i % 2, N)[0:parts], st["consts"](i)[1], rs, start=True,
                                         stop=True).then_inc(spread_ready, 1)
                    if st["swap"] is not None and i >= 1:
                        swap(st, i - 1)
                if st["swap"] is not None:
                    swap(st, len(st["tiles"]) - 1)
                    n["rope"] += len(st["tiles"])
                n["yn"] += len(normed)

            def swap(st, i):
                N, parts = st["n"], st["parts"]
                data, g = st["tiles"][i]
                normed_so_far = sum(t[1] is not None for t in st["tiles"][:i + 1])
                ynb = st["wk"][0:parts, 4 * S:6 * S].rearrange("p (b s) -> p b s", b=2)
                if g is not None:
                    pe.wait_ge(yn_ready, n["yn"] + normed_so_far)
                    src = ynb[:, i % 2, 0:N]
                else:
                    src = data
                if i >= 2:
                    pe.wait_ge(rope_done, n["rope"] + i - 1)
                nc.tensor.matmul(bank(3 + i % 2, N)[0:parts], st["swap"], src, start=True,
                                 stop=True).then_inc(swap_ready, 1)

            def attention(st):
                units = units_of(st)
                probs, turned_b = attn_buffers(st)
                d = depths(st)
                base, pair0 = n["unit"], n["pair"]
                pairs = [0]

                def scores(u):
                    pi, j = units[u]
                    p = st["passes"][pi]
                    a, b, nk = unit_keys(p, j)
                    head, q0, q1 = unit_rows(p, j)
                    if u >= d["nb"]:
                        pe.wait_ge(exp_done, base + u - d["nb"] + 1)
                    if head is None:
                        pe.wait_ge(q_ready, n["split"] + 1)
                        n["split"] += 1
                    buf = (u % d["nb"]) * d["wide"]
                    masks = p["masks"](q0 // P) if p["masks"] else []
                    for c0 in range(0, nk, BANK):
                        c1 = min(nk, c0 + BANK)
                        q = p["q"](head, q0, q1) if head is not None else q_diagonal[:, u % Q_BUFS, :]
                        last = nc.tensor.matmul(psum[:, buf + c0:buf + c1], q, p["k"](head, a * P + c0, a * P + c1),
                                                start=True, stop=not masks)
                    for m, (c0, mask) in enumerate(masks):
                        rows_of = half_select[:, j % 2, :] if head is None else identb[:, :]
                        last = nc.tensor.matmul(psum[:, buf + c0:buf + c0 + mask.shape[1]], rows_of, mask,
                                                start=False, stop=m == len(masks) - 1)
                    last.then_inc(scores_ready, 1)

                def turn(u):
                    pi, j = units[u]
                    p = st["passes"][pi]
                    a, b, nk = unit_keys(p, j)
                    pe.wait_ge(probs_ready, base + u + 1)
                    if u >= d["nt"]:
                        pe.wait_ge(copied, base + u - d["nt"] + 1)
                    t0 = (4 + (u % d["nt"])) * BANK
                    for j in range(b - a):
                        w = min(P, nk - j * P)
                        last = nc.tensor.transpose(psum[0:w, t0 + j * P:t0 + j * P + P],
                                                   probs[u % d["nb"]][:, j * P:j * P + w], ident[:, :])
                    last.then_inc(turned, 1)

                def weigh(chunk, quarter):
                    pi, j = units[4 * chunk]
                    p = st["passes"][pi]
                    pr = pairs[0]
                    if quarter == 0:
                        pe.wait_ge(copied, base + 4 * chunk + 4)
                        if p["first"] and j == 0 and pr >= 2:
                            pe.wait_ge(o_taken, pair0 + pr - 1)
                    c0 = j // 4 * CHUNK
                    parts = [(kt, g, max(q0, c0), min(q1, c0 + CHUNK)) for kt, q0, q1 in p["pv"]
                             if q0 < c0 + CHUNK and q1 > c0 for g in range(2)]
                    for i in range(len(parts) // 2 * quarter // 4 * 2, len(parts) // 2 * (quarter + 1) // 4 * 2):
                        kt, g, q0, q1 = parts[i]
                        last = nc.tensor.matmul(
                            psum[HD * g:HD * g + HD, (6 + pr % 2) * BANK + q0:(6 + pr % 2) * BANK + q1], p["v"](g, kt),
                            turned_b[0:p["krows"], chunk % 2, kt, g, q0 - c0:q1 - c0],
                            start=(i < 2 and c0 == 0 and p["first"]),
                            stop=(i >= len(parts) - 2 and p["last"]), skip_group_check=True)
                    if quarter == 3:
                        last.then_inc(pv_done, 1)
                        if p["last"] and j + 4 == p["units"]:
                            pairs[0] += 1

                U, lag = len(units), d["turn"]
                for u in range(U + lag + 4):
                    if u < U:
                        scores(u)
                    if u >= lag + 4:
                        weigh((u - lag - 4) // 4, (u - lag) % 4)
                    if lag <= u < U + lag:
                        turn(u - lag)
                n["unit"] += U
                n["pair"] += pairs[0]

            def dsa(st):
                for qt in range(1, ST):
                    nk = (qt + 1) * P
                    for h in range(4):
                        if n["idx"] >= 2:
                            pe.wait_ge(relu_ready, n["idx"] - 1)
                        lo = 64 * (h % 2)
                        nc.tensor.matmul(bank(6 + n["idx"] % 2, nk), QI[lo:lo + 64, h // 2, qt * P:qt * P + P],
                                         KI[lo:lo + 64, 0, 0:nk], start=True, stop=True).then_inc(idx_ready, 1)
                        n["idx"] += 1

            def compress(st):
                wk = st["wk"]
                F = wk[:, 0:4 * CMP_HALF * NCMP].rearrange("p (v l n) -> p v l n", v=2, l=CMP_HALF)
                hid = wk[:, 2048:2048 + 4 * NCMP].rearrange("p (v g n) -> p v g n", v=2, g=2)
                for v, src in enumerate((KC, VC)):
                    nc.tensor.matmul(bank(4 + v)[0:HD], ident[HD:P, HD:P], src[HD:P, 0, :], start=True, stop=True)
                    nc.tensor.matmul(bank(4 + v)[HD:P], ident[0:HD, 0:HD], src[0:HD, 0, :], start=True,
                                     stop=True).then_inc(misc_pe, 1)
                for v in range(2):
                    b1 = st["wblocks"][2 * v]
                    weights(b1)
                    pe.wait_ge(misc_dve, v + 1)
                    for l in range(CMP_HALF):
                        last = nc.tensor.matmul(bank(v, 2 * NCMP), slot(b1, CMP_HALF)[:, l, :], F[:, v, l, :],
                                                start=(l == 0), stop=(l == CMP_HALF - 1))
                    last.then_inc(misc_pe, 1)
                for v in range(2):
                    b2 = st["wblocks"][2 * v + 1]
                    weights(b2)
                    pe.wait_ge(misc_act, v + 1)
                    w2 = ring[:, b2 % RING, 0:HD]
                    for g in range(2):
                        if v == 0:
                            last = nc.tensor.matmul(psum[64 * g:64 * g + 64, 2 * BANK:2 * BANK + NCMP], w2, hid[:, v, g, :],
                                                    start=True, stop=True)
                        else:
                            last = nc.tensor.matmul(psum[0:NCMP, 3 * BANK + 64 * g:3 * BANK + 64 * g + 64],
                                                    hid[:, v, g, :], w2, start=(g == 0), stop=True, skip_group_check=True)
                    last.then_inc(misc_pe, 1)
                for half in range(2):
                    for g in range(2):
                        last = nc.tensor.matmul(bank(6)[HD * g:HD * g + HD, half * 12 * ST:(half + 1) * 12 * ST],
                                                ident[:, HD * half:HD * half + HD], GC[:, :, 12 * g:12 * g + 12],
                                                start=(half == 0), stop=True, skip_group_check=True)
                last.then_inc(misc_pe, 1)
                n["misc"] += 7

            def latnorm(st):
                sqb = st["wk"][:, 0:3 * S].rearrange("p (b s) -> p b s", b=3)
                for i in range(3):
                    pe.wait_ge(squares_ready, n["sq"] + i + 1)
                    last = nc.tensor.matmul(bank(0 if i < 2 else 1), mean_d[:, :], sqb[:, i, :], start=(i != 1),
                                            stop=(i != 0))
                last.then_inc(mean_ready, 1)
                n["sq"] += 3

            def rpb(st):
                for m in range(2):
                    for c in range(8):
                        if m * 8 + c >= 2:
                            pe.wait_ge(misc_act, 4 + m * 8 + c - 1)
                        nc.tensor.matmul(bank(c % 2)[0:120], st["rpb"][0:32, 120 * m:120 * m + 120],
                                         st["sel"][0:32, 512 * c:512 * c + 512], start=True, stop=True).then_inc(misc_pe, 1)
                        n["misc"] += 1

            def conv(st):
                for c in range(CONV_PE):
                    k = KD - CONV_PE + c
                    pe.wait_ge(glu_done, k + 1)
                    if CONV_BANK + c in bank_freed:
                        pe.wait_ge(*bank_freed[CONV_BANK + c])
                    for tap in range(TAPS):
                        pe.wait_ge(taps_ready, c * TAPS + tap + 1)
                        nc.tensor.matmul(bank(CONV_BANK + c), st["taps"][:, tap, :], st["U"][:, k, tap:tap + S],
                                         start=(tap == 0), stop=(tap == TAPS - 1)).then_inc(taps_used, 1)

            def layernorm(st):
                for k in range(KD):
                    last = nc.tensor.matmul(bank(0), mean_d[:, :], st["src"][:, k, :], start=(k == 0), stop=(k == KD - 1))
                last.then_inc(misc_pe, 1)
                n["misc"] += 1
                for k in range(KD):
                    pe.wait_ge(squares_ready, n["sq"] + k + 1)
                    last = nc.tensor.matmul(bank(1), mean_d[:, :], st["sq"][:, k, :], start=(k == 0), stop=(k == KD - 1))
                last.then_inc(mean_ready, 1)
                n["sq"] += KD

            work_of = dict(project=project, down=down, norm=norm_sum, headnorm=headnorm, attention=attention, dsa=dsa,
                           compress=compress, latnorm=latnorm, rpb=rpb, conv=conv, layernorm=layernorm)
            for s, st in enumerate(stages):
                if s == 0 or not (st["kind"] in ("norm", "down", "prep", "conv") or st.get("chases") or st.get("beside")):
                    gate(pe, "pe", s)
                elif tables_before[s] > tables_before[s - 1]:
                    pe.wait_ge(tables_in, tables_before[s])
                f = work_of.get(st["kind"])
                if f:
                    f(st)
                pe.sem_inc(stage_of["pe"], 1)


        @nc_block.scalar
        def _(act):
            steps = [0]
            n = dict(tile=0, sq=0, mean=0, unit=0, read=0, scaled=0, idx=0, misc_pe=0, misc_act=0, norm=0, pv=0, normed=0)

            def step(ins):
                ins.then_inc(act_steps, 1)
                steps[0] += 1

            def settle():
                if steps[0]:
                    act.wait_ge(act_steps, steps[0])

            def preload(function):
                step(nc.scalar.activation(unused[:, :], eps, function))

            def project(st):
                if st.get("after_tables"):
                    act.wait_ge(scratch_in, 16 * 16)
                if st.get("pads") is not None:
                    pads = st["pads"]
                for b, tiles, a in st["groups"]:
                    for t in tiles:
                        n["tile"] += 1
                        if t.taker != "act":
                            continue
                        act.wait_ge(tile_ready, n["tile"])
                        part, rows, cols = t.out
                        at = (n["tile"] - 1) % PROJ_BANKS * BANK
                        src = psum[part:part + rows, at:at + cols]
                        if t.op == "copy":
                            nc.scalar.activation(t.dst, src, ACT.Copy).then_inc(act_took, 1)
                        elif t.op == "scale":
                            nc.scalar.activation(t.dst, src, ACT.Copy, scale=t.arg).then_inc(act_took, 1)
                        elif t.op == "silu":
                            nc.scalar.activation(t.dst, src, ACT.Silu).then_inc(act_took, 1)
                        elif t.op == "sigmoid":
                            nc.scalar.activation(t.dst, src, ACT.Sigmoid).then_inc(act_took, 1)
                        elif t.op == "plus":
                            nc.scalar.activation(t.dst, src, ACT.Identity, bias=t.arg).then_inc(act_took, 1)
                        elif t.op == "sigmoidb":
                            nc.scalar.activation(t.dst, src, ACT.Sigmoid, bias=t.arg).then_inc(act_took, 1)
                        elif t.op == "relu2":
                            step(nc.scalar.activation(t.dst, src, ACT.Relu))
                            settle()
                            nc.scalar.activation(t.dst, t.dst, ACT.Square).then_inc(act_took, 1)
                        n["read"] += 1
                for dst, src in st.get("extra", []):
                    step(nc.scalar.activation(dst, src, ACT.Copy))
                if n["read"]:
                    act.wait_ge(act_took, n["read"])

            def down(st):
                n["tile"] += 14

            def norm(st):
                N = st["n"]
                into = st["dst"] if st["sq"] is None else st["sq"]
                if st["src"] is CX:
                    act.wait_ge(context_in, 16)
                for k in range(KD):
                    if st["sq"] is not None:
                        act.wait_ge(dve_took, st["x_done"][k])
                    nc.scalar.activation(into[:, k, 0:N], st["src"][:, k, 0:N], ACT.Square).then_inc(squares_ready, 1)
                n["norm"] += 1
                act.wait_ge(mean_ready, n["norm"])
                cols = N if st["sq"] is None else ST
                nc.scalar.activation(sd[:, 0:cols], bank(6, cols), ACT.Sqrt, bias=eps).then_inc(sd_ready, 1)
                n["normed"] += KD
                if st["shift"] is not None:
                    for k in range(KD):
                        act.wait_ge(scaled_ready, n["scaled"] + k + 1)
                        nc.scalar.activation(st["dst"][:, k, 0:N], st["dst"][:, k, 0:N], ACT.Identity,
                                             bias=st["shift"](k)).then_inc(norm_ready, 1)
                    act.wait_ge(norm_ready, n["normed"])
                    n["scaled"] += KD

            def headnorm(st):
                N, parts, rows = st["n"], st["parts"], st["rows"]
                normed = [t for t in st["tiles"] if t[1] is not None]
                sqb = st["wk"][:, 0:2 * S].rearrange("p (b s) -> p b s", b=2)
                for i, (data, g) in enumerate(normed):
                    if i >= 2:
                        act.wait_ge(square_read, n["sq"] + i - 1)
                    nc.scalar.activation(sqb[0:parts, i % 2, 0:N], data, ACT.Square).then_inc(squares_ready, 1)
                n["sq"] += len(normed)
                act.wait_ge(square_read, n["sq"])
                nc.scalar.activation(st["wk"][0:rows, 2 * S:2 * S + N], bank(0, N)[0:rows], ACT.Sqrt,
                                     bias=eps[0:rows]).then_inc(sd_ready, 1)

            def attention(st):
                units = units_of(st)
                probs, turned_b = attn_buffers(st)
                d = depths(st)
                base, pv0 = n["unit"], n["pv"]

                def copy_turned(u):
                    pi, j = units[u]
                    p = st["passes"][pi]
                    a, b, nk = unit_keys(p, j)
                    rows, chunk = min(P, p["krows"]), u // 4
                    act.wait_ge(turned, base + u + 1)
                    if chunk >= 2:
                        act.wait_ge(pv_done, pv0 + chunk - 1)
                    t0 = (4 + (u % d["nt"])) * BANK
                    g, q0, q1 = unit_rows(p, j)
                    q0, q1 = q0 % CHUNK, (q1 - 1) % CHUNK + 1
                    if p["split"]:
                        src = psum[0:rows, t0:t0 + (b - a) * P].rearrange("p (t g s) -> p t g s", g=2, s=HD)
                        dst = turned_b[0:rows, chunk % 2, a:b, :, q0:q1]
                    else:
                        src = psum[0:rows, t0:t0 + (b - a) * P].rearrange("p (t s) -> p t s", s=P)
                        dst = turned_b[0:rows, chunk % 2, a:b, g, q0:q1]
                    nc.scalar.activation(dst, src, ACT.Copy).then_inc(copied, 1)

                U, lag = len(units), d["turn"]
                for u in range(U + lag):
                    if u >= lag:
                        copy_turned(u - lag)
                    if u < U:
                        pi, j = units[u]
                        p = st["passes"][pi]
                        a, b, nk = unit_keys(p, j)
                        act.wait_ge(negmax_ready, base + u + 1)
                        if u >= d["nb"]:
                            act.wait_ge(turned, base + u - d["nb"] + 1)
                        c = (base + u) % 8
                        if p["sink"] is not None:
                            step(nc.scalar.activation(small[:, 32 + c:33 + c], p["sink"], ACT.Exp, bias=small[:, c:c + 1]))
                        s0 = (u % d["nb"]) * d["wide"]
                        nc.scalar.activation(probs[u % d["nb"]][:, 0:nk], psum[:, s0:s0 + nk], ACT.Exp,
                                             bias=small[:, c:c + 1], accum_out=small[:, 8 + c:9 + c]).then_inc(exp_done, 1)
                n["unit"] += U
                n["pv"] += U // 4
                act.wait_ge(copied, n["unit"])

            def dsa(st):
                wk = st["wk"]
                for qt in range(1, ST):
                    nk = (qt + 1) * P
                    for h in range(4):
                        act.wait_ge(idx_ready, n["idx"] + 1)
                        nc.scalar.activation(relu_buffer(wk, qt, h), bank(6 + n["idx"] % 2, nk),
                                             ACT.Relu).then_inc(relu_ready, 1)
                        n["idx"] += 1

            def compress(st):
                wk = st["wk"]
                hid = wk[:, 2048:2048 + 4 * NCMP].rearrange("p (v n) -> p v n", v=2)
                for v in range(2):
                    act.wait_ge(misc_pe, 3 + v)
                    nc.scalar.activation(hid[:, v, :], bank(v, 2 * NCMP), ACT.Silu).then_inc(misc_act, 1)
                act.wait_ge(misc_pe, 5)
                nc.scalar.activation(KCT[:, 0:NCMP], bank(2, NCMP), ACT.Copy).then_inc(misc_act, 1)
                act.wait_ge(misc_pe, 6)
                nc.scalar.activation(VCN[0:NCMP, :], bank(3, P)[0:NCMP], ACT.Copy).then_inc(misc_act, 1)
                act.wait_ge(misc_pe, 7)
                step(nc.scalar.activation(GH.rearrange("p e t n -> p (e t n)"), bank(6, 2 * 12 * ST), ACT.Copy))
                act.wait_ge(misc_act, 4)
                n["misc_pe"] += 7

            def latnorm(st):
                sqb = st["wk"][:, 0:3 * S].rearrange("p (b s) -> p b s", b=3)
                for i in range(3):
                    nc.scalar.activation(sqb[:, i, :], CQ[:, i, :] if i < 2 else CKV[:, 0, :],
                                         ACT.Square).then_inc(squares_ready, 1)
                n["norm"] += 1
                act.wait_ge(mean_ready, n["norm"])
                step(nc.scalar.activation(st["wk"][:, 3 * S:4 * S], bank(0), ACT.Sqrt, bias=eps, scale=float(D // 256)))
                nc.scalar.activation(st["wk"][:, 4 * S:5 * S], bank(1), ACT.Sqrt, bias=eps,
                                     scale=float(D // 128)).then_inc(sd_ready, 1)

            def rpb(st):
                for m in range(2):
                    for c in range(8):
                        act.wait_ge(misc_pe, st["pe0"] + m * 8 + c + 1)
                        nc.scalar.activation(st["tab"][0:120, m, 512 * c:512 * c + 512], bank(c % 2)[0:120],
                                             ACT.Copy).then_inc(misc_act, 1)
                    act.wait_ge(misc_act, 4 + 8 * (m + 1))
                    for h in range(8):
                        act.dma_start(rpb_table[8 * m + h].rearrange("c r j -> r c j"),
                                      st["tab"][15 * h:15 * h + 15, m, :].rearrange("p (c j) -> p c j", c=GRID)
                                      ).then_inc(scratch_in, 16)

            def conv(st):
                for c in range(CONV_PE):
                    k = KD - CONV_PE + c
                    for tap in range(TAPS):
                        if c >= 1:
                            act.wait_ge(taps_used, (c - 1) * TAPS + tap + 1)
                        nc.scalar.activation(st["taps"][:, tap, :], ident[:, :], ACT.Copy,
                                             scale=V("cv_w")[:, k * TAPS + tap:k * TAPS + tap + 1]).then_inc(taps_ready, 1)
                for c in range(CONV_PE):
                    k = KD - CONV_PE + c
                    act.wait_ge(taps_used, (c + 1) * TAPS)
                    step(nc.scalar.activation(st["CV"][:, k, :], bank(CONV_BANK + c), ACT.Identity, bias=V("cv_bd")[:, k:k + 1]))

            def layernorm(st):
                for k in range(KD):
                    act.wait_ge(centred, k + 1)
                    nc.scalar.activation(st["sq"][:, k, :], st["src"][:, k, :], ACT.Square).then_inc(squares_ready, 1)
                n["norm"] += 1
                act.wait_ge(mean_ready, n["norm"])
                nc.scalar.activation(sd[:, :], bank(1), ACT.Sqrt, bias=eps).then_inc(sd_ready, 1)
                for k in range(KD):
                    act.wait_ge(scaled_ready, n["scaled"] + k + 1)
                    nc.scalar.activation(st["dst"][:, k, :], st["dst"][:, k, :], ACT.Silu, bias=V("cv_lnb")[:, k:k + 1],
                                         scale=V("cv_lng")[:, k:k + 1]).then_inc(norm_ready, 1)
                n["scaled"] += KD
                n["normed"] += KD
                act.wait_ge(norm_ready, n["normed"])

            work_of = dict(project=project, down=down, norm=norm, headnorm=headnorm, attention=attention, dsa=dsa,
                           compress=compress, latnorm=latnorm, rpb=rpb, conv=conv, layernorm=layernorm)
            act.wait_ge(inputs_in, 16 * 6)
            for v, name in enumerate(("c", "c_ctx")):
                step(nc.scalar.activation(cond[:, :, v], V(name), ACT.Silu))
            step(nc.scalar.activation(identb[:, :], ident[:, :], ACT.Copy))
            for half in range(2):
                for g in range(2):
                    step(nc.scalar.activation(half_select[:, half, HD * g:HD * g + HD], ident[:, HD * half:HD * half + HD],
                                              ACT.Copy))
            step(nc.scalar.activation(diagm[:, :], arena[:, 0:P], ACT.Copy))
            step(nc.scalar.activation(prevm[:, :], arena[:, P:2 * P], ACT.Copy))
            settle()
            act.sem_inc(inputs_in, 32)
            for s, st in enumerate(stages):
                if s == 0 or not (st["kind"] in ("prep", "conv") or st.get("beside") or (st["kind"] == "norm" and st["sq"] is not None)):
                    gate(act, "act", s)
                if st["kind"] in ("norm", "headnorm", "latnorm", "layernorm"):
                    preload(ACT.Sqrt)
                if st["kind"] == "attention":
                    preload(ACT.Exp)
                for dst, src in st["loads"]:
                    act.dma_start(dst, src).then_inc(tables_in, 16)
                f = work_of.get(st["kind"])
                if f:
                    f(st)
                settle()
                act.sem_inc(stage_of["act"], 1)

        @nc_block.vector
        def _(dve):
            steps = [0]
            n = dict(tile=0, took=0, ada=0, unit=0, pair=0, spread=0, swap=0, cos=0, sd=0, idx=0, scaled=0, rope=0, yn=0, pv=0, diag=0)

            def step(ins):
                ins.then_inc(dve_steps, 1)
                steps[0] += 1

            def settle():
                dve.wait_ge(dve_steps, steps[0])

            def chain(ins):
                step(ins)
                settle()

            pending = []

            def ride(a):
                if pending:
                    layer, j = pending.pop()[1:]
                    vs = ada_vectors(layer, j)
                    dve.wait_ge(ada_ready, n["ada"] + 1)
                    bias = V(f"ada_b{layer}")[:, 4 * j:4 * j + 4].unsqueeze(2).to_broadcast([P, 4, vs])
                    nc.vector.tensor_tensor(mods[:, layer % 2, 4 * j:4 * j + 4, 0:vs],
                                            bank(7)[:, 0:8].rearrange("p (m v) -> p m v", v=2)[:, :, 0:vs], bias,
                                            ALU.add).then_inc(ada_taken, 1)
                    n["ada"] += 1
                if a:
                    b, layer, j = a
                    dve.wait_ge(weights_in[b % RING], landed[b])
                    vs = ada_vectors(layer, j)
                    w = slot(b, KD)
                    settle()
                    for k in range(KD):
                        for v in range(vs):
                            if k == 0:
                                ins = nc.vector.tensor_scalar(partial[:, v, :], w[:, k, :], cond[:, k, v:v + 1], None,
                                                              ALU.mult)
                            else:
                                dve.wait_ge(dve_steps, steps[0] - vs + 1)
                                ins = nc.vector.scalar_tensor_tensor(partial[:, v, :], w[:, k, :], cond[:, k, v:v + 1],
                                                                     partial[:, v, :], ALU.mult, ALU.add)
                            if k == KD - 1 and v == vs - 1:
                                ins.then_inc(ada_summed, 1)
                            else:
                                step(ins)
                    pending.append(a)

            def project(st):
                if st.get("pads") is not None:
                    U = st["pads"]
                    step(nc.vector.memset(U[:, :, 0:TAPS // 2], 0.0))
                    step(nc.vector.memset(U[:, :, TAPS // 2 + S:], 0.0))
                for b, tiles, a in st["groups"]:
                    for t in tiles:
                        n["tile"] += 1
                        if t.taker != "dve":
                            continue
                        dve.wait_ge(tile_ready, n["tile"])
                        part, rows, cols = t.out
                        at = (n["tile"] - 1) % PROJ_BANKS * BANK
                        src = psum[part:part + rows, at:at + cols]
                        if t.op == "copy":
                            nc.vector.tensor_copy(t.dst, src).then_inc(dve_took, 1)
                        elif t.op == "scale":
                            nc.vector.tensor_scalar(t.dst, src, t.arg, None, ALU.mult).then_inc(dve_took, 1)
                        elif t.op == "resid" and t.arg is None:
                            nc.vector.tensor_tensor(t.dst, src, t.dst, ALU.add).then_inc(dve_took, 1)
                        elif t.op == "resid":
                            nc.vector.scalar_tensor_tensor(t.dst, src, t.arg, t.dst, ALU.mult,
                                                           ALU.add).then_inc(dve_took, 1)
                        elif t.op == "residb":
                            chain(nc.vector.tensor_scalar(t.arg[2], src, t.arg[0], t.arg[1], ALU.add, ALU.mult))
                            nc.vector.tensor_tensor(t.dst, t.arg[2], t.dst, ALU.add).then_inc(dve_took, 1)
                            dve.wait_ge(dve_took, n["took"] + 1)
                        n["took"] += 1
                    ride(a)
                if n["took"]:
                    dve.wait_ge(dve_took, n["took"])
                if n["ada"]:
                    dve.wait_ge(ada_taken, n["ada"])

            def down(st):
                for half, kb, b, a in st["groups"]:
                    if kb < 3:
                        n["tile"] += 1
                    else:
                        for m in range(4):
                            n["tile"] += 1
                            n["took"] += 1
                            dve.wait_ge(tile_ready, n["tile"])
                            o = 4 * half + m
                            ins = nc.vector.scalar_tensor_tensor(X[:, o, :], bank(m), st["gate"](o), X[:, o, :], ALU.mult,
                                                                 ALU.add)
                            if st["hidc"] is not None and m % 2:
                                for c in (m - 1, m):
                                    step(ins)
                                    ins = nc.vector.scalar_tensor_tensor(
                                        CX[:, 4 * half + c, :], bank(4 + m // 2, C, C * (c % 2)), st["gatec"](4 * half + c),
                                        CX[:, 4 * half + c, :], ALU.mult, ALU.add)
                            ins.then_inc(dve_took, 1)
                    ride(a)
                dve.wait_ge(dve_took, n["took"])
                if n["ada"]:
                    dve.wait_ge(ada_taken, n["ada"])

            def norm(st):
                N = st["n"]
                dve.wait_ge(sd_ready, n["sd"] + 1)
                if st["src"] is CX:
                    dve.wait_ge(context_in, 16)
                if st["sq"] is None:
                    chain(nc.vector.reciprocal(rstd[:, 0:N], sd[:, 0:N]))
                    by = rstd[:, 0:N]
                else:
                    chain(nc.vector.reciprocal(sd[:, ST:2 * ST], sd[:, 0:ST]))
                    nc.vector.scalar_tensor_tensor(
                        rstd[:, :].rearrange("p (t q) -> p t q", t=ST), ident[:, :].unsqueeze(1).to_broadcast([P, ST, P]),
                        float(D), sd[:, ST:2 * ST].unsqueeze(2).to_broadcast([P, ST, P]), ALU.mult,
                        ALU.mult).then_inc(rstd_diagonal, 1)
                    n["diag"] += 1
                    dve.wait_ge(rstd_ready, n["diag"])
                    by = bank(6)
                for k in range(KD):
                    nc.vector.scalar_tensor_tensor(st["dst"][:, k, 0:N], st["src"][:, k, 0:N], st["gain"](k),
                                                   by, ALU.mult, ALU.mult
                                                   ).then_inc(norm_ready if st["shift"] is None else scaled_ready, 1)
                n["sd"] += 1
                if st["shift"] is None:
                    dve.wait_ge(norm_ready, st["norm0"] + KD)
                else:
                    n["scaled"] += KD
                    dve.wait_ge(scaled_ready, n["scaled"])

            def headnorm(st):
                N, parts, rows, wk = st["n"], st["parts"], st["rows"], st["wk"]
                ynb = wk[0:parts, 4 * S:6 * S].rearrange("p (b s) -> p b s", b=2)
                t1b = wk[0:parts, 6 * S:8 * S].rearrange("p (b s) -> p b s", b=2)
                t2b = wk[0:parts, 8 * S:10 * S].rearrange("p (b s) -> p b s", b=2)
                dve.wait_ge(sd_ready, n["sd"] + 1)
                nc.vector.reciprocal(wk[0:rows, 3 * S:3 * S + N], wk[0:rows, 2 * S:2 * S + N]).then_inc(sd_ready, 1)
                n["sd"] += 2
                T = len(st["tiles"])
                rope = st["swap"] is not None

                def scale(i):
                    data, g = st["tiles"][i]
                    if g is None:
                        return
                    dve.wait_ge(spread_ready, n["spread"] + 1)
                    if rope and i >= 2:
                        dve.wait_ge(rope_done, n["rope"] + i - 1)
                    out = ynb[:, i % 2, 0:N] if rope else data
                    nc.vector.scalar_tensor_tensor(out, data, g[0:parts], bank(1 + i % 2, N)[0:parts], ALU.mult,
                                                   ALU.mult).then_inc(yn_ready, 1)
                    n["spread"] += 1

                def rotate(i):
                    data, g = st["tiles"][i]
                    dve.wait_ge(swap_ready, n["swap"] + 1)
                    if i >= 2:
                        dve.wait_ge(rope_done, n["rope"] + i - 1)
                    step(nc.vector.tensor_tensor(t2b[:, i % 2, 0:N], bank(3 + i % 2, N)[0:parts], st["sin"][0:parts, 0:N],
                                                 ALU.mult))
                    settle()
                    dve.wait_ge(cos_ready, n["cos"] + 1)
                    nc.vector.tensor_tensor(data, t1b[:, i % 2, 0:N], t2b[:, i % 2, 0:N], ALU.add).then_inc(rope_done, 1)
                    n["swap"] += 1
                    n["cos"] += 1

                for i in range(T + 1):
                    if i < T:
                        scale(i)
                    if rope and i >= 1:
                        rotate(i - 1)
                n["yn"] = n["spread"]
                if rope:
                    n["rope"] += T
                    dve.wait_ge(rope_done, n["rope"])
                dve.wait_ge(yn_ready, n["yn"])

            def attention(st):
                units = units_of(st)
                probs, turned_b = attn_buffers(st)
                d = depths(st)
                base, pair0 = n["unit"], n["pair"]
                pairs = [0]

                def negmax(u):
                    pi, j = units[u]
                    p = st["passes"][pi]
                    a, b, nk = unit_keys(p, j)
                    c = (base + u) % 8
                    s0 = (u % d["nb"]) * d["wide"]
                    dve.wait_ge(scores_ready, base + u + 1)
                    if p["bias"] is not None:
                        if j == 0:
                            dve.wait_ge(bias_in[pi % 2], 32 * (pi // 2 + 1))
                        chain(nc.vector.tensor_tensor(psum[:, s0:s0 + S], psum[:, s0:s0 + S], p["bias"](j), ALU.add))
                        if j == p["units"] - 1:
                            dve.sem_inc(bias_used, 1)
                    if p["sink"] is None and not p["clamp"]:
                        nc.vector.tensor_reduce(small[:, c:c + 1], psum[:, s0:s0 + nk], AX, ALU.max,
                                                negate=True).then_inc(negmax_ready, 1)
                        return
                    chain(nc.vector.tensor_reduce(small[:, 40 + c:41 + c], psum[:, s0:s0 + nk], AX, ALU.max))
                    other = p["sink"] if p["sink"] is not None else -1e29
                    nc.vector.tensor_scalar(small[:, c:c + 1], small[:, 40 + c:41 + c], other, -1.0, ALU.max,
                                            ALU.mult).then_inc(negmax_ready, 1)

                def scale(u):
                    pi, j = units[u]
                    p = st["passes"][pi]
                    a, b, nk = unit_keys(p, j)
                    c = (base + u) % 8
                    dve.wait_ge(exp_done, base + u + 1)
                    total = small[:, 8 + c:9 + c]
                    if p["sink"] is not None:
                        chain(nc.vector.tensor_tensor(small[:, 16 + c:17 + c], total, small[:, 32 + c:33 + c], ALU.add))
                        total = small[:, 16 + c:17 + c]
                    elif p["clamp"]:
                        chain(nc.vector.tensor_scalar(small[:, 16 + c:17 + c], total, 1e-30, None, ALU.max))
                        total = small[:, 16 + c:17 + c]
                    chain(nc.vector.reciprocal(small[:, 24 + c:25 + c], total))
                    by = small[:, 24 + c:25 + c]
                    pb = probs[u % d["nb"]][:, 0:nk]
                    if p["gate"] is not None:
                        nc.vector.tensor_scalar(pb, pb, by, p["gate"](j), ALU.mult, ALU.mult).then_inc(probs_ready, 1)
                    else:
                        nc.vector.tensor_scalar(pb, pb, by, None, ALU.mult).then_inc(probs_ready, 1)

                def take(pi, chunks):
                    p = st["passes"][pi]
                    if not p["last"]:
                        return
                    dve.wait_ge(pv_done, pv0 + chunks)
                    N = p["n"]
                    src = bank(6 + pairs[0] % 2, N)
                    if p["z"] is not None:
                        nc.vector.tensor_tensor(p["dst"][:, 0:N], src, p["z"][:, 0:N], ALU.mult).then_inc(o_taken, 1)
                    else:
                        nc.vector.tensor_copy(p["dst"][:, 0:N], src).then_inc(o_taken, 1)
                    pairs[0] += 1

                pv0 = n["pv"]
                U, lag = len(units), d["turn"]
                for u in range(U + lag + 7):
                    if u < U:
                        negmax(u)
                    if d["scale"] <= u < U + d["scale"]:
                        scale(u - d["scale"])
                    if u >= lag + 7:
                        pi, j = units[u - lag - 7]
                        if j == st["passes"][pi]["units"] - 1:
                            take(pi, (u - lag - 7) // 4 + 1)
                n["pv"] = pv0 + U // 4
                n["unit"] += U
                n["pair"] += pairs[0]
                dve.wait_ge(o_taken, n["pair"])

            def dsa(st):
                wk = st["wk"]
                acc = [wk[:, 0:S], wk[:, S:2 * S]]
                best = small[:, 48:56]
                for qt in range(1, ST):
                    nk = (qt + 1) * P
                    for h in range(4):
                        dve.wait_ge(relu_ready, n["idx"] + 1)
                        w = WI[:, qt, h:h + 1]
                        if h == 0:
                            ins = nc.vector.tensor_scalar(acc[0][:, 0:nk], relu_buffer(wk, qt, h), w, None, ALU.mult)
                        else:
                            ins = nc.vector.scalar_tensor_tensor(acc[h % 2][:, 0:nk], relu_buffer(wk, qt, h), w,
                                                                 acc[1 - h % 2][:, 0:nk], ALU.mult, ALU.add)
                        ins.then_inc(idx_taken, 1)
                        n["idx"] += 1
                        dve.wait_ge(idx_taken, n["idx"])
                    chain(nc.vector.tensor_tensor(acc[1][:, qt * P:nk], acc[1][:, qt * P:nk], diagm[:, :], ALU.add))
                    for r in range(TOPK // 8):
                        chain(nc.vector.max(best, acc[1][:, 0:nk]))
                        chain(nc.vector.match_replace(acc[1][:, 0:nk], best, acc[1][:, 0:nk], -3e38))
                    chain(nc.vector.tensor_scalar(dsa_mask[:, qt - 1, 0:nk], acc[1][:, 0:nk], -2e38, NEG, ALU.is_ge,
                                                  ALU.mult))

            def compress(st):
                wk = st["wk"]
                F = wk[:, 0:4 * CMP_HALF * NCMP].rearrange("p (v l g n) -> p v l g n", v=2, l=CMP_HALF, g=2)
                step(nc.vector.tensor_copy(cmpmb[:, :, 0:NCMP], cmpm[:, :, :]))
                for v, (own, pe_) in enumerate(((KC, "pe_k"), (VC, "pe_v"))):
                    dve.wait_ge(misc_pe, v + 1)
                    for g in range(2):
                        for half in range(2):
                            lo = HD * half
                            src = own[lo:lo + HD, 0, :] if g == half else bank(4 + v)[lo:lo + HD]
                            win = src[:, CMP_HALF * half:CMP_HALF * half + CMP_HALF * NCMP].rearrange(
                                "p (n l) -> p l n", l=CMP_HALF)
                            add = V(pe_)[lo:lo + HD, CMP_HALF * half:CMP_HALF * half + CMP_HALF].unsqueeze(2).to_broadcast(
                                [HD, CMP_HALF, NCMP])
                            ins = nc.vector.tensor_tensor(F[lo:lo + HD, v, :, g, :], win, add, ALU.add)
                            if g and half:
                                ins.then_inc(misc_dve, 1)
                            else:
                                step(ins)
                dve.wait_ge(misc_dve, 2)

            def latnorm(st):
                wk = st["wk"]
                dve.wait_ge(sd_ready, n["sd"] + 1)
                chain(nc.vector.reciprocal(wk[:, 5 * S:7 * S], wk[:, 3 * S:5 * S]))
                for i in range(2):
                    step(nc.vector.scalar_tensor_tensor(CQ[:, i, :], CQ[:, i, :], V("qlat_g")[:, i:i + 1],
                                                        wk[:, 5 * S:6 * S], ALU.mult, ALU.mult))
                step(nc.vector.scalar_tensor_tensor(CKV[:, 0, :], CKV[:, 0, :], V("kvlat_g"), wk[:, 6 * S:7 * S],
                                                    ALU.mult, ALU.mult))
                n["sd"] += 1

            def prep(st):
                L = st["layer"]
                dve.wait_ge(ada_taken, n["ada"])
                for half, v in st["needs"]:
                        name = f"norm{half + 1}_{L}"
                        step(nc.vector.scalar_tensor_tensor(
                            sgain[:, half, v, :], mods[:, L % 2, (3 * half + 1) * KD:(3 * half + 2) * KD, v], 1.0, V(name),
                            ALU.add, ALU.mult))

            def conv(st):
                U, CV = st["U"], st["CV"]
                for tiles in ((0, 1), range(2, KD - CONV_PE)):
                    dve.wait_ge(glu_done, tiles[-1] + 1)
                    for tap in range(TAPS):
                        for k in tiles:
                            w = V("cv_w")[:, k * TAPS + tap:k * TAPS + tap + 1]
                            if tap == 0:
                                step(nc.vector.tensor_scalar(CV[:, k, :], U[:, k, 0:S], w, V("cv_bd")[:, k:k + 1],
                                                             ALU.mult, ALU.add))
                            else:
                                dve.wait_ge(dve_steps, steps[0] - len(tiles) + 1)
                                step(nc.vector.scalar_tensor_tensor(CV[:, k, :], U[:, k, tap:tap + S], w, CV[:, k, :],
                                                                    ALU.mult, ALU.add))

            def layernorm(st):
                dve.wait_ge(misc_pe, st["pe0"] + 1)
                for k in range(KD):
                    nc.vector.tensor_tensor(st["src"][:, k, :], st["src"][:, k, :], bank(0), ALU.subtract).then_inc(centred, 1)
                dve.wait_ge(centred, KD)
                dve.wait_ge(sd_ready, n["sd"] + 1)
                chain(nc.vector.reciprocal(rstd[:, :], sd[:, :]))
                for k in range(KD):
                    nc.vector.tensor_tensor(st["dst"][:, k, :], st["src"][:, k, :], rstd[:, :],
                                            ALU.mult).then_inc(scaled_ready, 1)
                n["sd"] += 1
                n["scaled"] += KD
                dve.wait_ge(scaled_ready, n["scaled"])

            work_of = dict(project=project, down=down, norm=norm, headnorm=headnorm, attention=attention, dsa=dsa,
                           compress=compress, latnorm=latnorm, prep=prep, conv=conv, layernorm=layernorm)
            step(nc.vector.memset(mean_d[:, :], 1.0 / D))
            step(nc.vector.memset(small[:, :], 0.0))
            step(nc.vector.memset(ones[:, :], 1.0))
            step(nc.vector.memset(eps, EPS))
            dve.wait_ge(inputs_in, 16 * 6)
            for name, by in (("qa_g", 0.125), ("qb_g", 0.125), ("qc_g", 0.125), ("at_q_g", 0.125),
                             ("qd_g", float(MLA_W) ** -0.5)):
                step(nc.vector.tensor_scalar(V(name), V(name), by, None, ALU.mult))
            settle()
            dve.sem_inc(inputs_in, 32)
            for s, st in enumerate(stages):
                if st["kind"] != "conv":
                    gate(dve, "dve", s)
                f = work_of.get(st["kind"])
                if f:
                    f(st)
                settle()
                dve.sem_inc(stage_of["dve"], 1)

        @nc_block.gpsimd
        def _(pool):
            n = dict(yn=0, rope=0, swap=0, unit=0, split=0)
            pool_count = 0

            def load_bias(t):
                for g in range(2):
                    pool.dma_start(bias_buf[HD * g:HD * g + HD, t % 2, 0:15 * GRID],
                                   rpb_table[2 * t + g].rearrange("c r j -> c (r j)")).then_inc(bias_in[t % 2], 16)

            for s, st in enumerate(stages):
                follows = st["kind"] in ("prep", "conv") or (st["kind"] == "norm" and st["sq"] is not None)
                if s == 0 or not follows:
                    gate(pool, "pool", s)
                if st["kind"] == "norm" and st["sq"] is not None:
                    N = st["n"]
                    for k in range(1, KD):
                        pool.wait_ge(squares_ready, st["sq0"] + k + 1)
                        if k > 1:
                            pool.wait_ge(pool_steps, pool_count)
                        ins = nc.gpsimd.tensor_tensor(st["sq"][:, 0, 0:N], st["sq"][:, 0, 0:N], st["sq"][:, k, 0:N],
                                                      ALU.add)
                        if k < KD - 1:
                            ins.then_inc(pool_steps, 1)
                            pool_count += 1
                        else:
                            ins.then_inc(sumsq_ready, 1)
                if st["kind"] == "conv":
                    for k in range(KD):
                        pool.wait_ge(act_took, st["u_done"][k])
                        u = st["U"][:, k, TAPS // 2:TAPS // 2 + S]
                        nc.gpsimd.tensor_tensor(u, u, st["sig"][:, k, :], ALU.mult).then_inc(glu_done, 1)
                    pool.wait_ge(glu_done, KD)
                if st["kind"] == "headnorm":
                    N, parts, wk = st["n"], st["parts"], st["wk"]
                    ynb = wk[0:parts, 4 * S:6 * S].rearrange("p (b s) -> p b s", b=2)
                    t1b = wk[0:parts, 6 * S:8 * S].rearrange("p (b s) -> p b s", b=2)
                    for i, (data, g) in enumerate(st["tiles"]):
                        if st["swap"] is None:
                            n["yn"] += 1
                            continue
                        if g is not None:
                            n["yn"] += 1
                            pool.wait_ge(yn_ready, n["yn"])
                            src = ynb[:, i % 2, 0:N]
                        else:
                            src = data
                        if i >= 2:
                            pool.wait_ge(rope_done, n["rope"] + i - 1)
                        nc.gpsimd.tensor_tensor(t1b[:, i % 2, 0:N], src, st["cos"][0:parts, 0:N],
                                                ALU.mult).then_inc(cos_ready, 1)
                        n["swap"] += 1
                    if st["swap"] is not None:
                        n["rope"] += len(st["tiles"])
                        pool.wait_ge(cos_ready, n["swap"])
                if st["kind"] == "attention" and st["passes"][0]["split"]:
                    has_bias = st["passes"][0]["bias"] is not None
                    units = units_of(st)
                    for g in range(2):
                        nc.gpsimd.memset(q_diagonal[HD * g:HD * g + HD, :, HD - HD * g:P - HD * g], 0.0).then_inc(pool_steps, 1)
                        pool_count += 1
                    for t in range(2 if has_bias else 0):
                        load_bias(t)
                    for u, (pi, j) in enumerate(units):
                        if has_bias and j == 4 and 1 <= pi < 7:
                            pool.wait_ge(bias_used, pi)
                            load_bias(pi + 1)
                        if u >= Q_BUFS:
                            pool.wait_ge(scores_ready, n["unit"] + u - Q_BUFS + 1)
                        q = st["passes"][pi]["q"](None, HD * j, HD * j + HD)
                        nc.gpsimd.tensor_copy(q_diagonal[0:HD, u % Q_BUFS, 0:HD], q[0:HD]).then_inc(pool_steps, 1)
                        nc.gpsimd.tensor_copy(q_diagonal[HD:P, u % Q_BUFS, HD:P], q[HD:P]).then_inc(q_ready, 1)
                        pool_count += 1
                        n["split"] += 1
                    pool.wait_ge(pool_steps, pool_count)
                    pool.wait_ge(q_ready, n["split"])
                if st["kind"] == "attention":
                    n["unit"] += len(units_of(st))
                pool.sem_inc(stage_of["pool"], 1)
            for k in range(KD):
                pool.wait_ge(norm_ready, n_normed - KD + k + 1)
                pool.dma_start(out_dram[k], H[:, k, :]).then_inc(out_done, 16)
            pool.wait_ge(out_done, 16 * KD)
            for name, sm in stage_of.items():
                pool.wait_ge(sm, len(stages))
            if n_tab:
                pool.wait_ge(tables_in, n_tab)


AB_SPLITS = (512, 128, 128, 256, 64, 4, 512, 512, 128, 128, 512)
CD_SPLITS = (512, 128, 128, 128, 128, 128, 128, 24, 512, 256, 128, 32, 512)


def pair_order(heads, width=HD):
    return np.concatenate([np.arange(h * width, (h + 1) * width) for h in heads])


def laid_out(i):
    grouped = [h for t in range(4) for h in (t, t + 4)]
    at_heads = [h for t in range(4) for h in (t, t + 4)] + [h for t in range(4) for h in (8 + t, 12 + t)]
    half, full = pair_order(grouped), pair_order(at_heads)
    qa, ka, va, qi, ki, wi, za, qb, kb, vb, zb = np.split(i["ab_w_in"][0], np.cumsum(AB_SPLITS)[:-1], axis=1)
    qc, kc, vc, ks, vs, kw, vw, gc, zc, cq, ckv, kr, zd = np.split(i["cd_w_in"][0], np.cumsum(CD_SPLITS)[:-1], axis=1)
    ukv = i["d_w_ukv"][0].reshape(128, 8, 2, 64)
    out = {
        "x": i["x"][0].T.reshape(KD, P, S), "ctx": i["ctx_2"][0].T.reshape(KD, P, C),
        "sinks": np.repeat(i["b_sinks"][0].reshape(2, 4), HD, 0),
        "ab_in": np.concatenate([qi, ki, ki, wi, qa[:, half], ka, qb[:, half], kb, za[:, half], zb[:, half], va, vb], 1),
        "ab_out": np.concatenate([i["ab_w_out"][0][:512][half], i["ab_w_out"][0][512:][half]]),
        "cd_in": np.concatenate([qc[:, half], kc, vc, ks, kw, cq, ckv, zc[:, half], zd, kr, gc, vs, vw], 1),
        "cd_out": np.concatenate([i["cd_w_out"][0][:512][half], i["cd_w_out"][0][512:]]),
        "cmp_w1": i["c_cmp_w1"][0], "cmp_w2": i["c_cmp_w2"][0], "uq": i["d_w_uq"][0],
        "ukv": np.concatenate([ukv[:, :, 0].reshape(128, 512), ukv[:, :, 1].reshape(128, 512)], 1),
        "ada_w": i["ada_w_2"], "mlp_w1": i["mlp_w1_2"], "mlp_w2": i["mlp_w2_2"],
        "at_qkv": np.concatenate([i["at_w_qkv_2"][0][:, :1024][:, full], i["at_w_qkv_2"][0][:, 1024:]], 1),
        "at_o": i["at_w_o_2"][0][full], "na_qkv": i["na_w_qkv_2"][0], "na_o": i["na_w_o_2"][0],
        "pw1": i["cv_w_pw1_2"][0], "pw2": i["cv_w_pw2_2"][0], "ft_w": i["ft_w_2"][0],
    }
    rpb = np.ones((32, 16 * 15), np.float32)
    rpb[:31] = i["na_rpb_2"][0].reshape(240, 31).T
    out["na_rpb"] = rpb

    def cols(a):
        return np.asarray(a).reshape(-1, P).T

    def twice(a):
        return np.concatenate([a, a])[:, None]

    def heads96(a, b):
        return np.concatenate([a, b, np.zeros(32, np.float32)])[:, None]

    pe = i["c_cmp_pe"][0]
    v = {
        "ab_norm": cols(i["ab_norm"][0]), "cd_norm": cols(i["cd_norm"][0]), "qa_g": twice(i["a_qk_norm"][0, 0]),
        "ka_g": twice(i["a_qk_norm"][0, 1]), "ki_g": twice(i["a_kidx_norm"][0]), "qb_g": twice(i["b_qk_norm"][0, 0]),
        "kb_g": twice(i["b_qk_norm"][0, 1]), "qc_g": twice(i["c_q_norm"][0]), "kc_g": twice(i["c_k_norm"][0, 0]),
        "ks_g": twice(i["c_k_norm"][0, 1]), "kw_g": twice(i["c_k_norm"][0, 2]),
        "pe_k": np.concatenate([pe[0].T, pe[0].T]), "pe_v": np.concatenate([pe[1].T, pe[1].T]),
        "qlat_g": cols(i["d_q_lat_norm"][0]), "kvlat_g": cols(i["d_kv_lat_norm"][0]),
        "qd_g": heads96(i["d_nope_norm"][0, 0], i["d_rope_norm"][0, 0]),
        "kd_g": heads96(i["d_nope_norm"][0, 1], i["d_rope_norm"][0, 1]),
        "c": cols(i["c_2"][0]), "c_ctx": cols(i["c_ctx_2"]), "final_g": cols(i["final_g_2"]),
        "at_q_g": twice(i["at_q_g_2"][0]), "at_k_g": twice(i["at_k_g_2"][0]), "cv_b1": cols(i["cv_b_pw1_2"][0]),
        "cv_w": i["cv_w_dw_2"][0].T.reshape(KD, P, TAPS).transpose(1, 0, 2).reshape(P, KD * TAPS),
        "cv_bd": cols(i["cv_b_dw_2"][0]), "cv_lng": cols(i["cv_ln_g_2"][0]), "cv_lnb": cols(i["cv_ln_b_2"][0]),
        "cv_b2": cols(i["cv_b_pw2_2"][0]), "ft_b": cols(i["ft_b_2"][0]),
    }
    for n in range(4):
        v[f"norm1_{n}"], v[f"norm2_{n}"] = cols(i["norm1_g_2"][n]), cols(i["norm2_g_2"][n])
        v[f"ada_b{n}"] = cols(i["ada_b_2"][n])
    out["vectors"] = np.concatenate([v[n] for n, _ in VECTORS], 1)
    for n, shape in IN_SHAPES.items():
        assert out[n].shape == shape, (n, out[n].shape)
    out.update(constants())
    return {n: np.ascontiguousarray(a) for n, a in out.items()}


def kernel(**inputs):
    import concourse.bacc as bacc
    from concourse.bass_utils import run_bass_kernel_spmd

    arrays = laid_out({n: np.asarray(a) for n, a in inputs.items()})
    nc = bacc.Bacc("TRN2", target_bir_lowering=False, num_devices=1)
    dram = {n: nc.dram_tensor(f"in_{n}", a.shape, mybir.dt.from_np(a.dtype), kind="ExternalInput").ap()
            for n, a in arrays.items()}
    out = nc.dram_tensor("out_x", (KD, P, S), F32, kind="ExternalOutput").ap()
    build_program(nc, dram, out)
    r = run_bass_kernel_spmd(nc, [{f"in_{n}": a for n, a in arrays.items()}], core_ids=[0])
    return np.ascontiguousarray(r.results[0]["out_x"].reshape(D, S).T)[None]
```
